# Optimizing a Trainium2 kernel written in Bass

```python
import math
import jax
import jax.numpy as jnp
from jax import lax
import numpy as np
import jax, jax.numpy as jnp

D_MODEL = 1024
BATCH = 1
SEQ = 512
DEPTH = 2

N_BRANCH = 4
BRANCH_WIDTH = 256
MLA_HEADS = 4
MLA_Q_LORA = 384
MLA_KV_LORA = 128
MLA_NOPE = 64
MLA_ROPE = 32
MLA_V = 64
FNET_GROUPS = 4
FNET_GROUP_DIM = 64
DIFF_HEADS = 4
DIFF_HEAD_DIM = 32
HGRN_HEADS = 4
HGRN_KEY_DIM = 64
HGRN_VAL_DIM = 64
HGRN_CHUNK = 64
D_FF = -(-8 * D_MODEL // (3 * 256)) * 256

ROPE_THETA = 10000.0
Q_BLOCK = 128
EPS = 1e-6

IN_WIDTHS = (
    MLA_Q_LORA,
    MLA_KV_LORA,
    MLA_ROPE,
    FNET_GROUPS * FNET_GROUP_DIM,
    2 * DIFF_HEADS * DIFF_HEAD_DIM,
    2 * DIFF_HEADS * DIFF_HEAD_DIM,
    DIFF_HEADS * 2 * DIFF_HEAD_DIM,
    HGRN_HEADS * HGRN_KEY_DIM,
    HGRN_HEADS * HGRN_VAL_DIM,
    HGRN_HEADS * HGRN_KEY_DIM,
    HGRN_HEADS * HGRN_KEY_DIM,
    HGRN_HEADS * HGRN_VAL_DIM,
    N_BRANCH * D_MODEL,
)
IN_TOTAL = sum(IN_WIDTHS)


def rmsnorm(x, g):
    xf = x.astype(jnp.float32)
    y = xf * lax.rsqrt(jnp.mean(xf * xf, axis=-1, keepdims=True) + EPS)
    return (y * g.astype(jnp.float32)).astype(x.dtype)

def split_cols(z, widths):
    offsets = [int(o) for o in np.cumsum(widths)[:-1]]
    return jnp.split(z, offsets, axis=-1)

def rope_tables(seq_len, dim):
    inv_freq = 1.0 / (ROPE_THETA ** (jnp.arange(0, dim, 2, dtype=jnp.float32) / dim))
    ang = jnp.arange(seq_len, dtype=jnp.float32)[:, None] * inv_freq[None, :]
    return jnp.cos(ang), jnp.sin(ang)

def apply_rope(t, cos, sin):
    tf = t.astype(jnp.float32)
    t1, t2 = jnp.split(tf, 2, axis=-1)
    c = cos[None, :, None, :]
    s = sin[None, :, None, :]
    return jnp.concatenate([t1 * c - t2 * s, t1 * s + t2 * c], axis=-1).astype(t.dtype)

def to_query_blocks(t):
    b, s, h, d = t.shape
    return t.reshape(b, s // Q_BLOCK, Q_BLOCK, h, d).transpose(1, 0, 2, 3, 4)

def from_query_blocks(t):
    nb, b, qb, h, d = t.shape
    return t.transpose(1, 0, 2, 3, 4).reshape(b, nb * qb, h, d)

def block_softmax_attention(q, k, v, scale):
    def one_block(qb):
        s = jnp.einsum('bqhd,bkhd->bhqk', qb, k).astype(jnp.float32) * scale
        p = jax.nn.softmax(s, axis=-1)
        return jnp.einsum('bhqk,bkhd->bqhd', p.astype(v.dtype), v)
    return from_query_blocks(lax.map(one_block, to_query_blocks(q)))

def block_diff_attention(q1, q2, k1, k2, v, lam, scale):
    def one_block(qs):
        qb1, qb2 = qs
        s1 = jnp.einsum('bqhd,bkhd->bhqk', qb1, k1).astype(jnp.float32) * scale
        s2 = jnp.einsum('bqhd,bkhd->bhqk', qb2, k2).astype(jnp.float32) * scale
        p = jax.nn.softmax(s1, axis=-1) - lam * jax.nn.softmax(s2, axis=-1)
        return jnp.einsum('bhqk,bkhd->bqhd', p.astype(v.dtype), v)
    return from_query_blocks(lax.map(one_block, (to_query_blocks(q1), to_query_blocks(q2))))

def mla_mixer(c_q, c_kv, k_rope, g_qa, w_uq, g_kva, w_ukv, g_qn, g_kn, cos, sin):
    b, s, _ = c_q.shape
    qk_dim = MLA_NOPE + MLA_ROPE
    q = (rmsnorm(c_q, g_qa) @ w_uq).reshape(b, s, MLA_HEADS, qk_dim)
    kv = (rmsnorm(c_kv, g_kva) @ w_ukv).reshape(b, s, MLA_HEADS, MLA_NOPE + MLA_V)
    k_nope, v = jnp.split(kv, [MLA_NOPE], axis=-1)
    k_pe = jnp.broadcast_to(k_rope[:, :, None, :], (b, s, MLA_HEADS, MLA_ROPE))
    k = jnp.concatenate([k_nope, k_pe], axis=-1)
    q = rmsnorm(q, g_qn)
    k = rmsnorm(k, g_kn)
    q = jnp.concatenate([q[..., :MLA_NOPE], apply_rope(q[..., MLA_NOPE:], cos, sin)], axis=-1)
    k = jnp.concatenate([k[..., :MLA_NOPE], apply_rope(k[..., MLA_NOPE:], cos, sin)], axis=-1)
    o = block_softmax_attention(q, k, v, qk_dim ** -0.5)
    return o.reshape(b, s, MLA_HEADS * MLA_V)

def fnet_mixer(u):
    b, s, _ = u.shape
    uf = u.astype(jnp.float32).reshape(b, s, FNET_GROUPS, FNET_GROUP_DIM)
    y = jnp.fft.fft2(uf, axes=(1, 3), norm='ortho').real
    return y.reshape(b, s, FNET_GROUPS * FNET_GROUP_DIM).astype(u.dtype)

def diff_mixer(q_in, k_in, v_in, g_qn, g_kn, lq1, lk1, lq2, lk2, g_sub, layer_idx, cos, sin):
    b, s, _ = q_in.shape
    d = DIFF_HEAD_DIM
    q = apply_rope(rmsnorm(q_in.reshape(b, s, 2 * DIFF_HEADS, d), g_qn), cos, sin)
    k = apply_rope(rmsnorm(k_in.reshape(b, s, 2 * DIFF_HEADS, d), g_kn), cos, sin)
    q = q.reshape(b, s, DIFF_HEADS, 2, d)
    k = k.reshape(b, s, DIFF_HEADS, 2, d)
    v = v_in.reshape(b, s, DIFF_HEADS, 2 * d)
    lambda_init = 0.8 - 0.6 * math.exp(-0.3 * layer_idx)
    lam = (jnp.exp(jnp.sum(lq1.astype(jnp.float32) * lk1.astype(jnp.float32)))
           - jnp.exp(jnp.sum(lq2.astype(jnp.float32) * lk2.astype(jnp.float32)))
           + lambda_init)
    o = block_diff_attention(q[:, :, :, 0], q[:, :, :, 1], k[:, :, :, 0], k[:, :, :, 1], v, lam, d ** -0.5)
    o = rmsnorm(o, g_sub) * (1.0 - lambda_init)
    return o.reshape(b, s, DIFF_HEADS * 2 * d)

def hgrn2_chunk_scan(q, k, v, log_f):
    b, s, h, dk = q.shape
    dv = v.shape[-1]
    c = HGRN_CHUNK
    n_chunks = s // c

    def chunks(t):
        return t.reshape(b, n_chunks, c, h, t.shape[-1]).transpose(1, 0, 3, 2, 4)

    lower_tri = jnp.tril(jnp.ones((c, c), dtype=bool))[:, :, None]

    def step(state, inp):
        qc, kc, vc, lc = inp
        cum = jnp.cumsum(lc, axis=2)
        inter = jnp.einsum('bhtk,bhkv->bhtv', qc * jnp.exp(cum), state)
        rel = cum[:, :, :, None, :] - cum[:, :, None, :, :]
        decay = jnp.exp(jnp.where(lower_tri, rel, -jnp.inf))
        scores = jnp.einsum('bhtk,bhtsk,bhsk->bhts', qc, decay, kc)
        intra = jnp.einsum('bhts,bhsv->bhtv', scores, vc)
        last = cum[:, :, -1:, :]
        new_state = (jnp.exp(last[:, :, 0, :])[..., None] * state
                     + jnp.einsum('bhsk,bhsv->bhkv', kc * jnp.exp(last - cum), vc))
        return new_state, inter + intra

    init = jnp.zeros((b, h, dk, dv), jnp.float32)
    _, o = lax.scan(step, init, (chunks(q), chunks(k), chunks(v), chunks(log_f)))
    return o.transpose(1, 0, 3, 2, 4).reshape(b, s, h, dv)

def hgrn2_mixer(q_in, i_in, f_fwd_in, f_bwd_in, g_in, lb_fwd, lb_bwd, g_on):
    b, s, _ = q_in.shape
    h, dk, dv = HGRN_HEADS, HGRN_KEY_DIM, HGRN_VAL_DIM
    q = q_in.astype(jnp.float32).reshape(b, s, h, dk)
    v = i_in.astype(jnp.float32).reshape(b, s, h, dv)

    def forget(z, lb):
        lbh = lb.reshape(h, dk)
        f = lbh + (1.0 - lbh) * jax.nn.sigmoid(z.astype(jnp.float32).reshape(b, s, h, dk))
        return 1.0 - f, jnp.log(f)

    k_f, lf_f = forget(f_fwd_in, lb_fwd)
    k_b, lf_b = forget(f_bwd_in, lb_bwd)
    o_fwd = hgrn2_chunk_scan(q, k_f, v, lf_f)
    o_bwd = jnp.flip(hgrn2_chunk_scan(jnp.flip(q, 1), jnp.flip(k_b, 1), jnp.flip(v, 1), jnp.flip(lf_b, 1)), 1)
    o = rmsnorm(o_fwd + o_bwd, g_on) * jax.nn.sigmoid(g_in.astype(jnp.float32).reshape(b, s, h, dv))
    return o.reshape(b, s, h * dv).astype(q_in.dtype)

def first_inputs(seed: int = 0) -> dict:
    key = jax.random.key(seed)
    ks = jax.random.split(key, 24)
    L = DEPTH
    qk_m = MLA_NOPE + MLA_ROPE

    def nrm(k, shape, scale):
        return jax.random.normal(k, shape, jnp.float32) * scale

    def gain(k, shape):
        return 1.0 + 0.02 * jax.random.normal(k, shape, jnp.float32)

    return {
        'x': nrm(ks[0], (BATCH, SEQ, D_MODEL), 1.0),
        'ln_mix': gain(ks[1], (L, D_MODEL)),
        'w_in': nrm(ks[2], (L, D_MODEL, IN_TOTAL), D_MODEL ** -0.5),
        'mla_g_qa': gain(ks[3], (L, MLA_Q_LORA)),
        'mla_w_uq': nrm(ks[4], (L, MLA_Q_LORA, MLA_HEADS * qk_m), MLA_Q_LORA ** -0.5),
        'mla_g_kva': gain(ks[5], (L, MLA_KV_LORA)),
        'mla_w_ukv': nrm(ks[6], (L, MLA_KV_LORA, MLA_HEADS * (MLA_NOPE + MLA_V)), MLA_KV_LORA ** -0.5),
        'mla_g_qn': gain(ks[7], (L, qk_m)),
        'mla_g_kn': gain(ks[8], (L, qk_m)),
        'diff_g_qn': gain(ks[9], (L, DIFF_HEAD_DIM)),
        'diff_g_kn': gain(ks[10], (L, DIFF_HEAD_DIM)),
        'diff_lq1': nrm(ks[11], (L, DIFF_HEAD_DIM), 0.1),
        'diff_lk1': nrm(ks[12], (L, DIFF_HEAD_DIM), 0.1),
        'diff_lq2': nrm(ks[13], (L, DIFF_HEAD_DIM), 0.1),
        'diff_lk2': nrm(ks[14], (L, DIFF_HEAD_DIM), 0.1),
        'diff_g_sub': gain(ks[15], (L, 2 * DIFF_HEAD_DIM)),
        'hgrn_lb_logits': nrm(ks[16], (2, L, HGRN_HEADS * HGRN_KEY_DIM), 0.5),
        'hgrn_g_on': gain(ks[17], (L, HGRN_VAL_DIM)),
        'w_branch': nrm(ks[18], (L, N_BRANCH, BRANCH_WIDTH, D_MODEL), BRANCH_WIDTH ** -0.5),
        'w_out': nrm(ks[19], (L, D_MODEL, D_MODEL), D_MODEL ** -0.5),
        'ln_ffn': gain(ks[20], (L, D_MODEL)),
        'w_gate_up': nrm(ks[21], (L, D_MODEL, 2 * D_FF), D_MODEL ** -0.5),
        'w_down': nrm(ks[22], (L, D_FF, D_MODEL), D_FF ** -0.5),
    }

def first_block(x, ln_mix, w_in, mla_g_qa, mla_w_uq, mla_g_kva, mla_w_ukv, mla_g_qn, mla_g_kn,
              diff_g_qn, diff_g_kn, diff_lq1, diff_lk1, diff_lq2, diff_lk2, diff_g_sub,
              hgrn_lb_logits, hgrn_g_on, w_branch, w_out, ln_ffn, w_gate_up, w_down):
    seq_len = x.shape[1]
    cos_m, sin_m = rope_tables(seq_len, MLA_ROPE)
    cos_d, sin_d = rope_tables(seq_len, DIFF_HEAD_DIM)
    lb_p = jax.nn.softmax(hgrn_lb_logits.astype(jnp.float32), axis=1)
    lower_bounds = jnp.cumsum(lb_p, axis=1) - lb_p[:, :1]

    for l in range(DEPTH):
        h = rmsnorm(x, ln_mix[l])
        z = h @ w_in[l]
        (c_q, c_kv, k_rope, fnet_in, dq, dk, dv,
         hq, hi, hf_fwd, hf_bwd, hg, gate_logits) = split_cols(z, IN_WIDTHS)

        o_mla = mla_mixer(c_q, c_kv, k_rope, mla_g_qa[l], mla_w_uq[l], mla_g_kva[l], mla_w_ukv[l],
                          mla_g_qn[l], mla_g_kn[l], cos_m, sin_m)
        o_fnet = fnet_mixer(fnet_in)
        o_diff = diff_mixer(dq, dk, dv, diff_g_qn[l], diff_g_kn[l], diff_lq1[l], diff_lk1[l],
                            diff_lq2[l], diff_lk2[l], diff_g_sub[l], l, cos_d, sin_d)
        o_hgrn = hgrn2_mixer(hq, hi, hf_fwd, hf_bwd, hg, lower_bounds[0, l], lower_bounds[1, l],
                             hgrn_g_on[l])

        merged = jnp.zeros_like(x)
        for n, o_branch in enumerate((o_mla, o_fnet, o_diff, o_hgrn)):
            gate = jax.nn.sigmoid(gate_logits[..., n * D_MODEL:(n + 1) * D_MODEL].astype(jnp.float32))
            merged = merged + gate.astype(x.dtype) * (o_branch @ w_branch[l, n])
        x = x + merged @ w_out[l]

        h2 = rmsnorm(x, ln_ffn[l])
        g_part, u_part = jnp.split(h2 @ w_gate_up[l], 2, axis=-1)
        x = x + (jax.nn.silu(g_part) * u_part) @ w_down[l]
    return x


DEPTH_2 = 1

GRID_W = 64
CTX_LEN = 256
MIX_W = D_MODEL
NA_HEADS = 8
NA_HEAD_DIM = 64
NA_W = NA_HEADS * NA_HEAD_DIM
NA_KH = 8
NA_KW = 16
SGU_GROUPS = 8
SGU_W = MIX_W - NA_W
SGU_GROUP_DIM = SGU_W // SGU_GROUPS
SGU_CHUNK = 128
IN_COLS = 3 * NA_W + 2 * SGU_W
N_GROUPS = 4
EXPERTS_PER_GROUP = 4
N_EXPERTS = N_GROUPS * EXPERTS_PER_GROUP
TOP_K = 2
D_EXPERT = D_MODEL // 2
N_MOD = 6


def _rms(x):
    x32 = x.astype(jnp.float32)
    return (x32 * lax.rsqrt(jnp.mean(x32 * x32, -1, keepdims=True) + EPS)).astype(x.dtype)

def _layernorm(x, g):
    x32 = x.astype(jnp.float32)
    mu = jnp.mean(x32, -1, keepdims=True)
    var = jnp.mean(jnp.square(x32 - mu), -1, keepdims=True)
    return ((x32 - mu) * lax.rsqrt(var + EPS)).astype(x.dtype) * g

def _adaln(cond, w, b):
    return jnp.split(jax.nn.silu(cond) @ w + b, N_MOD, axis=-1)

def _modulate(x, shift, scale):
    return _rms(x) * (1 + scale) + shift

def _heads(t):
    return t.reshape(t.shape[:-1] + (NA_HEADS, NA_HEAD_DIM))

def _project(h, w_in, q_gain, k_gain):
    p = h @ w_in
    q = _rms(_heads(p[..., :NA_W])) * q_gain
    k = _rms(_heads(p[..., NA_W:2 * NA_W])) * k_gain
    v = _heads(p[..., 2 * NA_W:3 * NA_W])
    u = p[..., 3 * NA_W:3 * NA_W + SGU_W]
    vs = p[..., 3 * NA_W + SGU_W:]
    return q, k, v, u, vs

def _project_kv(h, w_in, k_gain):
    p = h @ w_in[:, NA_W:3 * NA_W]
    return _rms(_heads(p[..., :NA_W])) * k_gain, _heads(p[..., NA_W:])

def _neighborhood_attention(q, k, v, k_ctx, v_ctx, rpb):
    bsz, seq, heads, dh = q.shape
    rows = seq // GRID_W
    kh = min(NA_KH, rows)
    kw = NA_KW
    scale = dh ** -0.5
    q_rows = jnp.moveaxis(q.reshape(bsz, rows, GRID_W, heads, dh), 1, 0)
    k_grid = k.reshape(bsz, rows, GRID_W, heads, dh)
    v_grid = v.reshape(bsz, rows, GRID_W, heads, dh)
    col = jnp.arange(GRID_W)
    col_start = jnp.clip(col - kw // 2, 0, GRID_W - kw)
    col_idx = col_start[:, None] + jnp.arange(kw)[None, :]
    rpb_cols = rpb[:, :, col_idx - col[:, None] + (NA_KW - 1)].astype(jnp.float32)

    def row_block(args):
        q_r, r = args
        r_start = jnp.clip(r - kh // 2, 0, rows - kh)
        k_win = lax.dynamic_slice_in_dim(k_grid, r_start, kh, axis=1)[:, :, col_idx]
        v_win = lax.dynamic_slice_in_dim(v_grid, r_start, kh, axis=1)[:, :, col_idx]
        bias = rpb_cols[:, r_start + jnp.arange(kh) - r + (NA_KH - 1)]
        s_win = jnp.einsum('bqhd,bkqwhd->bhqkw', q_r, k_win).astype(jnp.float32) * scale
        s_win = s_win + jnp.transpose(bias, (0, 2, 1, 3))[None]
        s_ctx = jnp.einsum('bqhd,bchd->bhqc', q_r, k_ctx).astype(jnp.float32) * scale
        s = jnp.concatenate([s_win.reshape(bsz, heads, GRID_W, kh * kw), s_ctx], axis=-1)
        p = jax.nn.softmax(s, axis=-1).astype(v.dtype)
        p_win = p[..., :kh * kw].reshape(bsz, heads, GRID_W, kh, kw)
        p_ctx = p[..., kh * kw:]
        return (jnp.einsum('bhqkw,bkqwhd->bqhd', p_win, v_win)
                + jnp.einsum('bhqc,bchd->bqhd', p_ctx, v_ctx))

    out = lax.map(row_block, (q_rows, jnp.arange(rows)))
    return jnp.moveaxis(out, 0, 1).reshape(bsz, seq, heads * dh)

def _context_attention(q, k, v):
    bsz, clen, heads, dh = q.shape
    s = jnp.einsum('bqhd,bkhd->bhqk', q, k).astype(jnp.float32) * dh ** -0.5
    p = jax.nn.softmax(s, axis=-1).astype(v.dtype)
    return jnp.einsum('bhqk,bkhd->bqhd', p, v).reshape(bsz, clen, heads * dh)

def _sgu(u, v, ln_g, w_s, b_s):
    bsz, length, _ = u.shape
    u = jax.nn.gelu(u)
    v = _layernorm(jax.nn.gelu(v), ln_g)
    v = v.reshape(bsz, length // SGU_CHUNK, SGU_CHUNK, SGU_GROUPS, SGU_GROUP_DIM)
    mixed = jnp.einsum('hpq,bnqhd->bnphd', w_s, v) + b_s.T[:, :, None]
    return u * mixed.reshape(bsz, length, SGU_W)

def _merge(o_na, o_sgu, out_gain, w_out):
    y = jnp.concatenate([_rms(o_na), _rms(o_sgu)], axis=-1) * out_gain
    return y @ w_out

def _hier_moe(h, rg_w, rg_b, re_w, re_b, w1, w3, w2):
    shp = h.shape
    t = h.reshape(-1, D_MODEL)
    p_g = jax.nn.softmax((t @ rg_w).astype(jnp.float32) + rg_b, axis=-1)
    p_top, g_idx = lax.top_k(p_g, 1)
    e_all = jnp.einsum('nd,gde->nge', t, re_w).astype(jnp.float32) + re_b
    e_logits = jnp.take_along_axis(e_all, g_idx[:, :, None], axis=1)[:, 0]
    e_top, e_idx = lax.top_k(jax.nn.softmax(e_logits, axis=-1), TOP_K)
    w = e_top / jnp.sum(e_top, -1, keepdims=True) * p_top
    within = jnp.sum(jax.nn.one_hot(e_idx, EXPERTS_PER_GROUP, dtype=jnp.float32) * w[..., None], axis=1)
    gate = (jax.nn.one_hot(g_idx[:, 0], N_GROUPS, dtype=jnp.float32)[:, :, None]
            * within[:, None, :]).reshape(-1, N_EXPERTS).astype(t.dtype)
    out = jnp.zeros_like(t)
    for e in range(N_EXPERTS):
        hid = jax.nn.silu(t @ w1[e]) * (t @ w3[e])
        out = out + gate[:, e:e + 1] * (hid @ w2[e])
    return out.reshape(shp)

def second_inputs(seed: int = 0) -> dict:
    key = jax.random.key(seed)
    ks = jax.random.split(key, 22)

    def nrm(k, shape, s):
        return jax.random.normal(k, shape, jnp.float32) * s

    return {
        'x': nrm(ks[0], (BATCH, SEQ, D_MODEL), 1.0),
        'c': nrm(ks[1], (BATCH, D_MODEL), 1.0),
        'ctx': nrm(ks[2], (BATCH, CTX_LEN, D_MODEL), 1.0),
        'c_ctx': nrm(ks[3], (D_MODEL,), 1.0),
        'w_ada': nrm(ks[4], (DEPTH_2, D_MODEL, N_MOD * D_MODEL), 0.5 * D_MODEL ** -0.5),
        'b_ada': nrm(ks[5], (DEPTH_2, N_MOD * D_MODEL), 0.02),
        'w_in': nrm(ks[6], (DEPTH_2, D_MODEL, IN_COLS), D_MODEL ** -0.5),
        'q_gain': 1.0 + nrm(ks[7], (DEPTH_2, NA_HEAD_DIM), 0.02),
        'k_gain': 1.0 + nrm(ks[8], (DEPTH_2, NA_HEAD_DIM), 0.02),
        'rpb': nrm(ks[9], (DEPTH_2, NA_HEADS, 2 * NA_KH - 1, 2 * NA_KW - 1), 0.1),
        'sgu_ln': 1.0 + nrm(ks[10], (DEPTH_2, SGU_W), 0.02),
        'sgu_w': nrm(ks[11], (DEPTH_2, SGU_GROUPS, SGU_CHUNK, SGU_CHUNK), SGU_CHUNK ** -0.5),
        'sgu_b': 1.0 + nrm(ks[12], (DEPTH_2, SGU_GROUPS, SGU_CHUNK), 0.02),
        'out_gain': 1.0 + nrm(ks[13], (DEPTH_2, MIX_W), 0.02),
        'w_out': nrm(ks[14], (DEPTH_2, MIX_W, D_MODEL), MIX_W ** -0.5),
        'rg_w': nrm(ks[15], (DEPTH_2, D_MODEL, N_GROUPS), D_MODEL ** -0.5),
        'rg_b': nrm(ks[16], (DEPTH_2, N_GROUPS), 0.01),
        're_w': nrm(ks[17], (DEPTH_2, N_GROUPS, D_MODEL, EXPERTS_PER_GROUP), D_MODEL ** -0.5),
        're_b': nrm(ks[18], (DEPTH_2, N_GROUPS, EXPERTS_PER_GROUP), 0.01),
        'w1': nrm(ks[19], (DEPTH_2, N_EXPERTS, D_MODEL, D_EXPERT), D_MODEL ** -0.5),
        'w3': nrm(ks[20], (DEPTH_2, N_EXPERTS, D_MODEL, D_EXPERT), D_MODEL ** -0.5),
        'w2': nrm(ks[21], (DEPTH_2, N_EXPERTS, D_EXPERT, D_MODEL), D_EXPERT ** -0.5),
    }

def second_block(x, c, ctx, c_ctx, w_ada, b_ada, w_in, q_gain, k_gain, rpb, sgu_ln, sgu_w, sgu_b,
              out_gain, w_out, rg_w, rg_b, re_w, re_b, w1, w3, w2):
    for i in range(DEPTH_2):
        last = i == DEPTH_2 - 1
        sh_a, sc_a, g_a, sh_f, sc_f, g_f = _adaln(c, w_ada[i], b_ada[i])
        csh_a, csc_a, cg_a, csh_f, csc_f, cg_f = _adaln(c_ctx, w_ada[i], b_ada[i])

        h = _modulate(x, sh_a[:, None], sc_a[:, None])
        hc = _modulate(ctx, csh_a, csc_a)
        q, k, v, u, vs = _project(h, w_in[i], q_gain[i], k_gain[i])
        if last:
            kc, vc = _project_kv(hc, w_in[i], k_gain[i])
        else:
            qc, kc, vc, uc, vsc = _project(hc, w_in[i], q_gain[i], k_gain[i])
        o_na = _neighborhood_attention(q, k, v, kc, vc, rpb[i])
        o_sg = _sgu(u, vs, sgu_ln[i], sgu_w[i], sgu_b[i])
        x = x + g_a[:, None] * _merge(o_na, o_sg, out_gain[i], w_out[i])

        hf = _modulate(x, sh_f[:, None], sc_f[:, None])
        x = x + g_f[:, None] * _hier_moe(hf, rg_w[i], rg_b[i], re_w[i], re_b[i], w1[i], w3[i], w2[i])

        if not last:
            oc_na = _context_attention(qc, kc, vc)
            oc_sg = _sgu(uc, vsc, sgu_ln[i], sgu_w[i], sgu_b[i])
            ctx = ctx + cg_a * _merge(oc_na, oc_sg, out_gain[i], w_out[i])
            hcf = _modulate(ctx, csh_f, csc_f)
            ctx = ctx + cg_f * _hier_moe(hcf, rg_w[i], rg_b[i], re_w[i], re_b[i], w1[i], w3[i], w2[i])
    return x


def setup_inputs(seed=0):
    out = dict(first_inputs(seed))
    for name, value in second_inputs(seed + 1).items():
        if name != "x":
            out[name + "_2"] = value
    return out


def reference(
    x, ln_mix, w_in, mla_g_qa, mla_w_uq, mla_g_kva, mla_w_ukv, mla_g_qn, mla_g_kn, diff_g_qn,
    diff_g_kn, diff_lq1, diff_lk1, diff_lq2, diff_lk2, diff_g_sub, hgrn_lb_logits, hgrn_g_on,
    w_branch, w_out, ln_ffn, w_gate_up, w_down, c_2, ctx_2, c_ctx_2, w_ada_2, b_ada_2, w_in_2,
    q_gain_2, k_gain_2, rpb_2, sgu_ln_2, sgu_w_2, sgu_b_2, out_gain_2, w_out_2, rg_w_2, rg_b_2,
    re_w_2, re_b_2, w1_2, w3_2, w2_2,
):
    x = first_block(
        x, ln_mix, w_in, mla_g_qa, mla_w_uq, mla_g_kva, mla_w_ukv, mla_g_qn, mla_g_kn,
        diff_g_qn, diff_g_kn, diff_lq1, diff_lk1, diff_lq2, diff_lk2, diff_g_sub,
        hgrn_lb_logits, hgrn_g_on, w_branch, w_out, ln_ffn, w_gate_up, w_down,
    )
    return second_block(
        x, c_2, ctx_2, c_ctx_2, w_ada_2, b_ada_2, w_in_2, q_gain_2, k_gain_2, rpb_2, sgu_ln_2,
        sgu_w_2, sgu_b_2, out_gain_2, w_out_2, rg_w_2, rg_b_2, re_w_2, re_b_2, w1_2, w3_2, w2_2,
    )


_drawn_inputs = setup_inputs


def setup_inputs(seed=0):
    import zlib

    import numpy as np

    out = dict(_drawn_inputs(seed))
    spreads = {}
    factors = {'mla_g_qa': 8.0,
     'mla_g_kva': 8.0,
     'mla_g_qn': 8.0,
     'mla_g_kn': 8.0,
     'diff_g_qn': 4.811,
     'diff_g_kn': 4.499,
     'diff_lk2': 3.526,
     'diff_g_sub': 4.365,
     'hgrn_g_on': 6.742,
     'ln_ffn': 2.9,
     'b_ada_2': 2.921,
     'q_gain_2': 22.679,
     'k_gain_2': 21.474,
     'rpb_2': 46.065,
     'sgu_ln_2': 64.0,
     'sgu_b_2': 64.0,
     'out_gain_2': 64.0,
     'rg_b_2': 64.0,
     're_b_2': 64.0,
     'rg_w_2': 7.302,
     're_w_2': 8.0,
     'w1_2': 6.73,
     'w3_2': 6.268,
     'w2_2': 6.248}
    for name, (base, spread) in spreads.items():
        noise = np.random.default_rng([zlib.crc32(name.encode()), seed]).standard_normal(out[name].shape)
        drawn = base * np.exp(spread * noise) if base else spread * noise
        out[name] = jnp.asarray(drawn.astype(out[name].dtype))
    for name, factor in factors.items():
        out[name] = (out[name] * factor).astype(out[name].dtype)
    return out
```

```python
from contextlib import ExitStack

import concourse.bass as bass
from concourse import mybir

ALU = mybir.AluOpType
ACT = mybir.ActivationFunctionType
AX = mybir.AxisListType
F32 = mybir.dt.float32
F32R = mybir.dt.float32r

P = 128
T = 512
TT = T // P
D = 1024
KD = D // P
EPS = 1e-6
CW = 256
CHUNK = KD * CW
RING = 2
BW = 256
NB = 4
DFF = 2816
FF_STEPS = DFF // CW
NE, DE = 16, 512
MOE_STEPS = NE * DE // CW
CTX = 256
CT = CTX // P
NEG = -1.0e30

C_FU, C_DQ, C_DK, C_DV, C_HQ, C_HV, C_HF, C_HB, C_HG, C_GATE = (
    544, 800, 1056, 1312, 1568, 1824, 2080, 2336, 2592, 2848)
C_KR = 448
KRW = 96
Z_CQ, Z_CKV, Z_FU, Z_DQ, Z_DK, Z_HQ, Z_HF, Z_HB, Z_HG = 0, 3, 4, 6, 8, 10, 12, 14, 16
Z_KR, Z_DV, Z_HV = 18, 19, 21
ZT = 23

G_MIX, G_QA, G_KVA, G_MQ, G_MK, G_DQ, G_DK, G_SUB, G_ON, G_FFN, G_N = 0, 8, 11, 12, 13, 14, 15, 16, 17, 18, 26

LEVELS = (64, 32, 16, 8, 4, 2, 1)


class Phase:

    def __init__(self, nc, name):
        self.nc, self.name, self.stack, self.sems = nc, name, ExitStack(), []

    def __enter__(self):
        return self

    def sem(self, name):
        s = self.stack.enter_context(self.nc.semaphore(f"{self.name}_{name}"))
        self.sems.append(s)
        return s

    def sb(self, name, shape, dt=F32):
        return self.stack.enter_context(self.nc.sbuf_tensor(f"{self.name}_{name}", shape, dt))

    def psum(self):
        return self.stack.enter_context(self.nc.psum_tensor(f"{self.name}_ps", [P, 8, 512], F32))

    def __exit__(self, *error):
        if error[0] is None:
            self.nc.all_engine_barrier()
            for s in self.sems:
                self.nc.sync.sem_clear(s)
            self.nc.all_engine_barrier()
        self.stack.close()


def linker(eng, sem):
    count = [0]

    def link(instruction):
        count[0] += 1
        instruction.then_inc(sem, 1)
        eng.wait_ge(sem, count[0])

    return link


def cols(tensor, n, k=KD):
    return tensor[:, 0:k * n].rearrange("p (k n) -> p k n", k=k)


class Ring:

    def __init__(self, ph, wide):
        self.raw = ph.sb("raw", [P, RING, CHUNK])
        self.hi = ph.sb("whi", [P, RING, CHUNK], F32R)
        self.lo = ph.sb("wlo", [P, RING, CHUNK], F32R)
        self.raw_ready = [ph.sem(f"raw_ready{i}") for i in range(RING)]
        self.hi_done, self.lo_done = ph.sem("hi_done"), ph.sem("lo_done")
        if wide:
            self.wraw = ph.sb("wide_raw", [P, CHUNK])
            self.whi = ph.sb("wide_hi", [P, CHUNK], F32R)
            self.wlo = ph.sb("wide_lo", [P, CHUNK], F32R)
            self.wide_ready, self.wide_hi, self.wide_lo = (
                ph.sem("wide_ready"), ph.sem("wide_hi_done"), ph.sem("wide_lo_done"))

    def open(self, sp):
        sp.sem_inc(self.lo_done, RING)

    def load(self, sp, c, slot, src, n=CW, k=KD):
        sp.wait_ge(self.lo_done, c + 1)
        sp.dma_start(cols(self.raw[:, slot], n, k), src).then_inc(self.raw_ready[slot], 16)

    def cut_hi(self, act, slot, arrived, n=CHUNK):
        act.wait_ge(self.raw_ready[slot], arrived)
        act.activation(self.hi[:, slot, 0:n], self.raw[:, slot, 0:n], ACT.Copy).then_inc(self.hi_done, 1)

    def cut_lo(self, eng, c, slot, n=CHUNK):
        eng.wait_ge(self.hi_done, c + 1)
        eng.tensor_tensor(self.lo[:, slot, 0:n], self.raw[:, slot, 0:n],
                          self.hi[:, slot, 0:n].bitcast(F32), ALU.subtract).then_inc(self.lo_done, 1)

    def wait_cut(self, pe, c):
        pe.wait_ge(self.lo_done, RING + c + 1)

    def load_wide(self, sp, w, src):
        sp.wait_ge(self.wide_lo, w)
        sp.dma_start(cols(self.wraw, D, 2), src).then_inc(self.wide_ready, 16)

    def cut_wide_hi(self, act, w):
        act.wait_ge(self.wide_ready, 16 * w + 16)
        act.activation(self.whi[:], self.wraw[:], ACT.Copy).then_inc(self.wide_hi, 1)

    def cut_wide_lo(self, eng, w):
        eng.wait_ge(self.wide_hi, w + 1)
        eng.tensor_tensor(self.wlo[:], self.wraw[:], self.whi[:].bitcast(F32), ALU.subtract)\
           .then_inc(self.wide_lo, 1)


def product3(pe, out, whi, wlo, xhi, xlo, ks, start=True, stop=True):
    parts = ((whi, xhi), (whi, xlo), (wlo, xhi))
    mm = None
    for n, (w, x) in enumerate(parts):
        for i, k in enumerate(ks):
            mm = pe.matmul(out, w(k), x(k), start=start and n == 0 and i == 0,
                           stop=stop and n == 2 and i == len(ks) - 1)
    return mm


class Norm:

    def __init__(self, ph, name, src, sq, total, root, h, hi, lo, bank, ones, eps, width):
        self.src, self.sq, self.total, self.root, self.h, self.hi = src, sq, total, root, h, hi
        self.lo, self.bank, self.ones, self.eps, self.width = lo, bank, ones, eps, width
        (self.squares, self.totals, self.spread, self.roots, self.inverse, self.scaled,
         self.h_done, self.hi_cut, self.lo_cut) = (
            ph.sem(f"{name}_{s}") for s in ("squares", "totals", "spread", "roots", "inverse", "scaled", "h_done", "hi_cut", "lo_cut"))

    def act_squares(self, act):
        for k in range(KD):
            act.activation(self.sq[:, k], self.src[:, k], ACT.Square).then_inc(self.squares, 1)

    def dve_total(self, dve):
        dve.wait_ge(self.squares, KD)
        dve.tensor_reduce(self.total, self.sq.rearrange("p k t -> p t k"), AX.X, ALU.add)\
           .then_inc(self.totals, 1)

    def pe_spread(self, pe):
        pe.wait_ge(self.totals, 1)
        pe.matmul(self.bank, self.ones, self.total, start=True, stop=True).then_inc(self.spread, 1)

    def act_root(self, act):
        act.wait_ge(self.spread, 1)
        act.activation(self.root, self.bank, ACT.Sqrt, bias=self.eps, scale=1.0 / D).then_inc(self.roots, 1)

    def dve_apply(self, dve, gain, shift=None):
        dve.wait_ge(self.roots, 1)
        dve.reciprocal(self.root, self.root).then_inc(self.inverse, 1)
        dve.wait_ge(self.inverse, 1)
        for k in range(KD):
            ins = dve.scalar_tensor_tensor(self.h[:, k], self.src[:, k], gain(k), self.root,
                                           ALU.mult, ALU.mult)
            if shift is None:
                ins.then_inc(self.h_done, 1)
            else:
                ins.then_inc(self.scaled, 1)
        if shift is not None:
            for k in range(KD):
                dve.wait_ge(self.scaled, k + 1)
                dve.tensor_scalar(self.h[:, k], self.h[:, k], shift(k), None, ALU.add).then_inc(self.h_done, 1)
        for k in range(KD):
            dve.wait_ge(self.hi_cut, k + 1)
            dve.tensor_tensor(self.lo[:, k], self.h[:, k], self.hi[:, k].bitcast(F32), ALU.subtract)\
               .then_inc(self.lo_cut, 1)

    def act_hi(self, act):
        for k in range(KD):
            act.wait_ge(self.h_done, k + 1)
            act.activation(self.hi[:, k], self.h[:, k], ACT.Copy).then_inc(self.hi_cut, 1)


def load_constants(nc, m, a):
    with Phase(nc, "consts") as ph:
        loaded, x_loaded, made, step, astep = (ph.sem(s) for s in ("loaded", "x_loaded", "made", "step", "astep"))
        logits = ph.sb("logits", [P, 2, 2, 2])
        e, r = ph.sb("e", [P, 2, 2, 2]), ph.sb("r", [P, 4, 2, 2])
        with nc.Block() as block:
            @block.sync
            def _(sp):
                sp.dma_start(logits[:], a["lb_logits"]).then_inc(loaded, 16)
                sp.dma_start(m.gains[:], a["gains"]).then_inc(loaded, 16)
                sp.dma_start(m.lam[:], a["lam"].rearrange("l f d -> (l f d)").rearrange("(o n) -> o n", o=1)
                             .broadcast_to([P, 2 * 4 * 32])).then_inc(loaded, 16)
                sp.dma_start(m.mats[:], a["mats"]).then_inc(loaded, 16)
                sp.dma_start(m.rope[:], a["rope"]).then_inc(loaded, 16)
                sp.dma_start(m.small[:], a["small"]).then_inc(loaded, 16)
                sp.dma_start(m.vec2[:], a["vec2"]).then_inc(loaded, 16)
                sp.dma_start(m.x[:], a["xT"].rearrange("(k p) t -> p k t", p=P)).then_inc(x_loaded, 16)
                sp.wait_ge(loaded, 112)
                sp.wait_ge(x_loaded, 16)

            @block.vector
            def _(dve):
                link = linker(dve, step)
                dve.wait_ge(loaded, 112)
                link(dve.tensor_tensor(r[:, 0], logits[:, :, 0], logits[:, :, 1], ALU.max))
                link(dve.tensor_tensor(e[:, :, 0], logits[:, :, 0], r[:, 0], ALU.subtract))
                link(dve.tensor_tensor(e[:, :, 1], logits[:, :, 1], r[:, 0], ALU.subtract))
                dve.tensor_copy(r[:, 3], r[:, 0]).then_inc(made, 1)
                dve.wait_ge(astep, 1)
                link(dve.tensor_tensor(r[:, 1], e[:, :, 0], e[:, :, 1], ALU.add))
                link(dve.reciprocal(r[:, 2], r[:, 1]))
                link(dve.tensor_tensor(e[:, :, 0], e[:, :, 0], r[:, 2], ALU.mult))
                link(dve.tensor_tensor(e[:, :, 1], e[:, :, 1], r[:, 2], ALU.mult))
                link(dve.tensor_tensor(m.lb[:, 0], e[:, :, 0], e[:, :, 0], ALU.subtract))
                link(dve.tensor_tensor(r[:, 3], e[:, :, 0], e[:, :, 1], ALU.add))
                link(dve.tensor_tensor(m.lb[:, 1], r[:, 3], e[:, :, 0], ALU.subtract))

            @block.scalar
            def _(act):
                act.wait_ge(made, 1)
                act.activation(e[:], e[:], ACT.Exp).then_inc(astep, 1)
                act.wait_ge(astep, 1)


def project(nc, m, a, l):
    plan = [(0, CW, "feature", (0, 1)), (CW, CW, "feature", (2, 3)), (C_KR, KRW, "rope", (Z_KR,))]
    for col, z in ((C_FU, Z_FU), (C_DQ, Z_DQ), (C_DK, Z_DK), (C_HQ, Z_HQ), (C_HF, Z_HF), (C_HB, Z_HB), (C_HG, Z_HG)):
        plan.append((col, CW, "feature", (z, z + 1)))
    plan += [(C_DV, CW, "token", (Z_DV,)), (C_HV, CW, "token", (Z_HV,))]
    tiles = []
    for c, (_, _, kind, _) in enumerate(plan):
        tiles += [(c, i) for i in range({"feature": 2, "rope": 1, "token": TT}[kind])]
    with Phase(nc, "proj") as ph:
        ring = Ring(ph, False)
        ps = ph.psum()
        tile_done, evicted, layer = (ph.sem(s) for s in ("tile_done", "evicted", "layer_gains"))
        z = m.z
        norm = Norm(ph, "n", m.x, z[:, 8:16], z[:, 16], z[:, 17], z[:, 0:8], m.hi, m.lo, ps[:, 7],
                    m.ones, m.eps, T)
        w = a["w_in"][l].rearrange("(k p) n -> p k n", p=P)
        with nc.Block() as block:
            @block.sync
            def _(sp):
                ring.open(sp)
                for c, (col, n, _, _) in enumerate(plan):
                    ring.load(sp, c, c % RING, w[:, :, col:col + n], n)

            @block.gpsimd
            def _(pool):
                for c, (_, n, _, _) in enumerate(plan):
                    ring.cut_lo(pool, c, c % RING, KD * n)

            @block.vector
            def _(dve):
                dve.tensor_copy(m.g[:], m.gains[:, bass.ds(l, 1), :].rearrange("p o g -> p (o g)")).then_inc(layer, 1)
                dve.tensor_copy(m.lbl[:], m.lb[:, bass.ds(l, 1)].rearrange("p o d t -> p (o d t)")).then_inc(layer, 1)
                dve.tensor_copy(m.lamv[:], m.lam[:, bass.ds(l * 128, 128)]).then_inc(layer, 1)
                dve.tensor_copy(m.laminit[:], m.small[:, bass.ds(l * 2, 2)]).then_inc(layer, 1)
                norm.dve_total(dve)
                dve.wait_ge(layer, 4)
                norm.dve_apply(dve, lambda k: m.g[:, G_MIX + k:G_MIX + k + 1])

            @block.scalar
            def _(act):
                def cut(c):
                    if c < len(plan):
                        if c >= RING:
                            act.wait_ge(tile_done, max(i for i, t in enumerate(tiles) if t[0] == c - RING) + 1)
                        ring.cut_hi(act, c % RING, 16 * (c // RING + 1), KD * plan[c][1])

                norm.act_squares(act)
                cut(0)
                cut(1)
                norm.act_root(act)
                norm.act_hi(act)
                for i, (c, part) in enumerate(tiles):
                    if part == 0 and c:
                        cut(c + 1)
                    kind, dst = plan[c][2:]
                    bank = ps[:, i % 6]
                    act.wait_ge(tile_done, i + 1)
                    if kind == "feature":
                        ins = act.activation(z[:, dst[part]], bank, ACT.Copy)
                    elif kind == "rope":
                        ins = act.activation(z[0:KRW, dst[0]], bank[0:KRW], ACT.Copy)
                    else:
                        half = z[:, dst[0] + part // 2, (part % 2) * BW:(part % 2 + 1) * BW]
                        ins = act.activation(half, bank[:, 0:BW], ACT.Copy)
                    ins.then_inc(evicted, 1)
                act.wait_ge(evicted, len(tiles))

            @block.tensor
            def _(pe):
                norm.pe_spread(pe)
                pe.wait_ge(norm.lo_cut, KD)
                for i, (c, part) in enumerate(tiles):
                    _, n, kind, _ = plan[c]
                    hi, lo = cols(ring.hi[:, c % RING], n), cols(ring.lo[:, c % RING], n)
                    if part == 0:
                        ring.wait_cut(pe, c)
                    if i >= 6:
                        pe.wait_ge(evicted, i - 5)
                    bank = ps[:, i % 6]
                    if kind == "feature":
                        at = slice(part * P, (part + 1) * P)
                        mm = product3(pe, bank, lambda k: hi[:, k, at], lambda k: lo[:, k, at],
                                      lambda k: m.hi[:, k], lambda k: m.lo[:, k], range(KD))
                    elif kind == "rope":
                        mm = product3(pe, bank[0:KRW], lambda k: hi[:, k], lambda k: lo[:, k],
                                      lambda k: m.hi[:, k], lambda k: m.lo[:, k], range(KD))
                    else:
                        at = slice(part * P, (part + 1) * P)
                        mm = product3(pe, bank[:, 0:BW], lambda k: m.hi[:, k, at], lambda k: m.lo[:, k, at],
                                      lambda k: hi[:, k], lambda k: lo[:, k], range(KD))
                    mm.then_inc(tile_done, 1)


class GroupNorm:

    def __init__(self, ph, name, units, parts, size, ones, eps, ps, sq, rt, rope=None, width=T):
        self.units, self.parts, self.size, self.ones, self.eps, self.ps = units, parts, size, ones, eps, ps
        self.sq, self.rt, self.rope, self.width = sq, rt, rope, width
        self.step = ph.sb(f"{name}_newton", [P, T])
        (self.squares, self.spread, self.roots, self.inverse, self.refined, self.normed,
         self.rotated, self.with_cos, self.with_sin, self.done) = (
            ph.sem(f"{name}_{s}") for s in ("squares", "spread", "roots", "inverse", "refined", "normed", "rotated", "with_cos", "with_sin", "done"))

    def act(self, act):
        n, w = self.parts, self.width
        for i, (src, _, _) in enumerate(self.units):
            act.activation(self.sq[0:n, i, 0:w], src, ACT.Square).then_inc(self.squares, 1)
        for i in range(len(self.units)):
            act.wait_ge(self.spread, i + 1)
            act.activation(self.rt[0:n, i, 0:w], self.ps[0:n, i % 4, 0:w], ACT.Sqrt, bias=self.eps[0:n],
                           scale=1.0 / self.size).then_inc(self.roots, 1)

    def pe(self, pe):
        n, w = self.parts, self.width
        for i in range(len(self.units)):
            pe.wait_ge(self.squares, i + 1)
            if i >= 4:
                pe.wait_ge(self.normed, i - 3)
            pe.matmul(self.ps[0:n, i % 4, 0:w], self.ones, self.sq[0:n, i, 0:w], start=True, stop=True)\
              .then_inc(self.spread, 1)
        if self.rope:
            for i in range(len(self.units)):
                pe.wait_ge(self.normed, i + 1)
                if i >= 4:
                    pe.wait_ge(self.with_sin, i - 3)
                pe.matmul(self.ps[0:n, 4 + i % 4, 0:w], self.rope[2], self.sq[0:n, i, 0:w],
                          start=True, stop=True).then_inc(self.rotated, 1)

    def dve(self, dve):
        n, w = self.parts, self.width
        link = linker(dve, self.refined)
        for i, (src, gain, dst) in enumerate(self.units):
            dve.wait_ge(self.roots, i + 1)
            dve.reciprocal(self.rt[0:n, i, 0:w], self.rt[0:n, i, 0:w]).then_inc(self.inverse, 1)
            dve.wait_ge(self.inverse, i + 1)
            r, total, step = self.rt[0:n, i, 0:w], self.ps[0:n, i % 4, 0:w], self.step[0:n, 0:w]
            link(dve.tensor_tensor(step, r, r, ALU.mult))
            link(dve.scalar_tensor_tensor(step, total, 1.0 / self.size, step, ALU.mult, ALU.mult))
            link(dve.tensor_scalar(step, step, -0.5, 1.5, ALU.mult, ALU.add))
            link(dve.tensor_tensor(r, r, step, ALU.mult))
            to = self.sq[0:n, i, 0:w] if self.rope else dst
            dve.scalar_tensor_tensor(to, src, gain, self.rt[0:n, i, 0:w], ALU.mult, ALU.mult)\
               .then_inc(self.normed, 1)
        if not self.rope:
            return
        for i, (_, _, dst) in enumerate(self.units):
            dve.wait_ge(self.normed, i + 1)
            dve.tensor_tensor(dst, self.sq[0:n, i, 0:w], self.rope[0], ALU.mult).then_inc(self.with_cos, 1)
            dve.wait_ge(self.rotated, i + 1)
            dve.tensor_tensor(self.rt[0:n, i, 0:w], self.ps[0:n, 4 + i % 4, 0:w], self.rope[1], ALU.mult)\
               .then_inc(self.with_sin, 1)
            dve.wait_ge(self.with_cos, i + 1)
            dve.wait_ge(self.with_sin, i + 1)
            dve.tensor_tensor(dst, dst, self.rt[0:n, i, 0:w], ALU.add).then_inc(self.done, 1)


class Attention:

    def __init__(self, ph, kind, heads, ps, ident, scores, values, out, neglam=None, bias=None):
        self.kind, self.heads, self.ps, self.ident = kind, heads, ps, ident
        self.scores, self.values, self.out, self.neglam, self.bias = scores, values, out, neglam, bias
        self.nk = 6 if kind == "bias" else 4
        self.maps = 2 if kind == "diff" else 1
        self.t_slots = 1 if kind == "bias" else 2
        self.prob = ph.sb("prob", [P, 2, self.maps, self.nk * P])
        self.probT = ph.sb("probT", [P, 2, self.nk, T])
        self.stat = ph.sb("stat", [P, 2, 8])
        (self.scored, self.biased, self.ctx_copied, self.negmax, self.exps, self.inverse,
         self.scaled, self.prob_done, self.turned, self.turned_out, self.head_done, self.head_out) = (
            ph.sem(f"att_{s}") for s in ("scored", "biased", "ctx_copied", "negmax", "exps", "inverse", "scaled", "prob_done", "turned", "turned_out",
                  "head_done", "head_out"))
        self.units = heads * TT

    def pe(self, pe):
        units = self.units
        for step in range(units + 3):
            u = step
            if u < units:
                if u >= 2:
                    pe.wait_ge(self.exps, self.maps * (u - 1))
                self.scores(pe, u // TT, u % TT, self.ps[:, 2 * (u % 2):2 * (u % 2) + 2]).then_inc(self.scored, 1)
            u = step - 2
            if 0 <= u < units:
                pe.wait_ge(self.prob_done, u + 1)
                if u >= self.t_slots:
                    pe.wait_ge(self.turned_out, u - self.t_slots + 1)
                for kt in range(self.nk):
                    mm = pe.transpose(self.turned_at(u, kt), self.prob[:, u % 2, 0, kt * P:(kt + 1) * P], self.ident)
                mm.then_inc(self.turned, 1)
            u = step - 3
            if u >= 0 and u % TT == TT - 1:
                h = u // TT
                pe.wait_ge(self.turned_out, u + 1)
                if h >= 2:
                    pe.wait_ge(self.head_out, h - 1)
                for kt in range(self.nk):
                    mm = pe.matmul(self.head_at(h), self.values(h, kt), self.probT[:, h % 2, kt],
                                   start=(kt == 0), stop=(kt == self.nk - 1))
                mm.then_inc(self.head_done, 1)

    def turned_at(self, u, kt):
        slot = (u % 2) if self.t_slots == 2 else 0
        return self.ps[:, 4 + slot + kt // 4, (kt % 4) * P:(kt % 4 + 1) * P]

    def head_at(self, h):
        return self.ps[64 * (h % 2):64 * (h % 2) + 64, 6 + h % 2]

    def dve(self, dve):
        units, maps = self.units, self.maps
        for step in range(units + 1):
            u = step
            if u < units:
                st = self.stat[:, u % 2]
                dve.wait_ge(self.scored, u + 1)
                if u >= 2:
                    dve.wait_ge(self.prob_done, u - 1)
                if self.kind == "bias":
                    self.bias(dve, u)
                    if u >= 2:
                        dve.wait_ge(self.turned, u - 1)
                    dve.tensor_tensor(self.prob[:, u % 2, 0, 0:T], self.ps[:, 2 * (u % 2)],
                                      self.bias_at(u), ALU.add).then_inc(self.biased, 1)
                    dve.wait_ge(self.biased, u + 1)
                    dve.wait_ge(self.ctx_copied, u + 1)
                    dve.tensor_reduce(st[:, 0:1], self.prob[:, u % 2, 0, :], AX.X, ALU.max, negate=True)\
                       .then_inc(self.negmax, 1)
                else:
                    for i in range(maps):
                        dve.tensor_reduce(st[:, i:i + 1], self.ps[:, 2 * (u % 2) + i], AX.X, ALU.max,
                                          negate=True).then_inc(self.negmax, 1)
            u = step - 1
            if u >= 0:
                st = self.stat[:, u % 2]
                dve.wait_ge(self.exps, maps * (u + 1))
                dve.reciprocal(st[:, 4:4 + maps], st[:, 2:2 + maps]).then_inc(self.inverse, 1)
                dve.wait_ge(self.inverse, u + 1)
                p0 = self.prob[:, u % 2, 0]
                if maps == 1:
                    dve.tensor_scalar(p0, p0, st[:, 4:5], None, ALU.mult).then_inc(self.prob_done, 1)
                else:
                    dve.tensor_scalar(p0, p0, st[:, 4:5], None, ALU.mult).then_inc(self.scaled, 1)
                    dve.tensor_scalar(st[:, 6:7], st[:, 5:6], self.neglam, None, ALU.mult).then_inc(self.scaled, 1)
                    dve.wait_ge(self.scaled, 2 * (u + 1))
                    dve.scalar_tensor_tensor(p0, self.prob[:, u % 2, 1], st[:, 6:7], p0, ALU.mult, ALU.add)\
                       .then_inc(self.prob_done, 1)

    def act(self, act):
        units, maps = self.units, self.maps
        for step in range(units + 4):
            u = step
            if u < units:
                st = self.stat[:, u % 2]
                if self.kind == "bias":
                    act.wait_ge(self.scored, u + 1)
                if u >= 2:
                    act.wait_ge(self.turned, u - 1)
                if self.kind == "bias":
                    act.activation(self.prob[:, u % 2, 0, T:T + CTX], self.ps[:, 2 * (u % 2) + 1, 0:CTX], ACT.Copy)\
                       .then_inc(self.ctx_copied, 1)
                for i in range(maps):
                    act.wait_ge(self.negmax, maps * u + i + 1)
                    src = self.prob[:, u % 2, 0] if self.kind == "bias" else self.ps[:, 2 * (u % 2) + i]
                    act.activation(self.prob[:, u % 2, i], src, ACT.Exp, bias=st[:, i:i + 1],
                                   accum_out=st[:, 2 + i:3 + i]).then_inc(self.exps, 1)
            u = step - 2
            if 0 <= u < units:
                h, qt = u // TT, u % TT
                act.wait_ge(self.turned, u + 1)
                if h >= 2:
                    act.wait_ge(self.head_done, h - 1)
                n = min(4, self.nk)
                slot = 4 + ((u % 2) if self.t_slots == 2 else 0)
                ins = act.activation(self.probT[:, h % 2, 0:n, qt * P:(qt + 1) * P],
                                     self.ps[:, slot].rearrange("p (k t) -> p k t", k=4), ACT.Copy)
                if self.nk > 4:
                    ins = act.activation(self.probT[:, h % 2, 4:self.nk, qt * P:(qt + 1) * P],
                                         self.ps[:, 5, 0:(self.nk - 4) * P].rearrange("p (k t) -> p k t", k=self.nk - 4),
                                         ACT.Copy)
                ins.then_inc(self.turned_out, 1)
            u = step - 3
            if u >= 0 and u % TT == TT - 1:
                h = u // TT
                act.wait_ge(self.head_done, h + 1)
                act.activation(self.out(h), self.head_at(h), ACT.Copy).then_inc(self.head_out, 1)
        act.wait_ge(self.head_out, self.heads)


def mla_prepare(nc, m, a, l, mem):
    with Phase(nc, "mlap") as ph:
        ps = ph.psum()
        wuq, wukv = ph.sb("wuq", [P, 3, 384]), ph.sb("wukv", [P, 512])
        sq, rt = ph.sb("sq", [P, 8, T]), ph.sb("rt", [P, 8, T])
        raw = mem.raw
        loaded, step, astep, squares, spread, roots, latent, up, out, prep = (
            ph.sem(s) for s in ("loaded", "step", "astep", "squares", "spread", "roots", "latent", "up", "out", "prep"))
        z = m.z
        units = [(raw[0:96, i], mem.gq if i < 4 else m.g[0:96, G_MK:G_MK + 1], mem.qk[0:96, i]) for i in range(8)]
        gn = GroupNorm(ph, "gn", units, 96, 96, m.ones[0:96, 0:96], m.eps, ps, sq, rt,
                       (m.rope[0:96, 0], m.rope[0:96, 1], m.rot96))
        with nc.Block() as block:
            @block.sync
            def _(sp):
                sp.dma_start(wuq[:], a["w_uq"][l].rearrange("(k p) n -> p k n", p=P)).then_inc(loaded, 16)
                sp.dma_start(wukv[:], a["w_ukv"][l]).then_inc(loaded, 16)
                sp.wait_ge(loaded, 32)

            @block.scalar
            def _(act):
                for k in range(4):
                    act.activation(sq[:, k], z[:, k], ACT.Square).then_inc(squares, 1)
                for i, n in ((0, 384), (1, 128)):
                    act.wait_ge(spread, i + 1)
                    act.activation(rt[:, i], ps[:, i], ACT.Sqrt, bias=m.eps, scale=1.0 / n).then_inc(roots, 1)
                for i in range(8):
                    act.wait_ge(up, i + 1)
                    n = 96 if i < 4 else 64
                    act.activation(raw[0:n, i], ps[0:n, i % 4], ACT.Copy).then_inc(out, 1)
                    if i >= 4:
                        act.activation(raw[64:96, i], z[64:96, Z_KR], ACT.Copy).then_inc(astep, 1)
                for t in range(TT):
                    act.wait_ge(up, 9 + t)
                    act.activation(mem.v[:, t], ps[:, 4 + t, 0:BW], ACT.Copy).then_inc(out, 1)
                act.wait_ge(astep, 4)
                act.wait_ge(out, 12)
                gn.act(act)

            @block.vector
            def _(dve):
                link = linker(dve, step)
                dve.tensor_scalar(mem.gq, m.g[0:96, G_MQ:G_MQ + 1], float(96 ** -0.5), None, ALU.mult).then_inc(prep, 1)
                for i in range(2):
                    dve.wait_ge(roots, i + 1)
                    link(dve.reciprocal(rt[:, i], rt[:, i]))
                for k in range(4):
                    dve.scalar_tensor_tensor(z[:, k], z[:, k], m.g[:, G_QA + k:G_QA + k + 1], rt[:, k // 3],
                                             ALU.mult, ALU.mult).then_inc(latent, 1)
                dve.wait_ge(prep, 1)
                dve.wait_ge(latent, 4)
                dve.wait_ge(out, 12)
                gn.dve(dve)
                dve.wait_ge(gn.done, 8)

            @block.tensor
            def _(pe):
                pe.wait_ge(squares, 4)
                for k in range(3):
                    mm = pe.matmul(ps[:, 0], m.ones, sq[:, k], start=(k == 0), stop=(k == 2))
                mm.then_inc(spread, 1)
                pe.matmul(ps[:, 1], m.ones, sq[:, 3], start=True, stop=True).then_inc(spread, 1)
                pe.wait_ge(latent, 4)
                pe.wait_ge(loaded, 32)
                for h in range(4):
                    for k in range(3):
                        mm = pe.matmul(ps[0:96, h], wuq[:, k, 96 * h:96 * h + 96], z[:, k], start=(k == 0), stop=(k == 2))
                    mm.then_inc(up, 1)
                for h in range(4):
                    pe.wait_ge(out, h + 1)
                    pe.matmul(ps[0:64, h], wukv[:, 128 * h:128 * h + 64], z[:, Z_CKV], start=True, stop=True)\
                      .then_inc(up, 1)
                v_cols = wukv[:].rearrange("p (h n) -> p h n", h=4)[:, :, 64:128]
                for t in range(TT):
                    pe.matmul(ps[:, 4 + t, 0:BW], z[:, Z_CKV, t * P:(t + 1) * P], v_cols, start=True, stop=True)\
                      .then_inc(up, 1)
                pe.wait_ge(out, 12)
                gn.pe(pe)


def mla_attend(nc, m, mem):
    with Phase(nc, "mlaa") as ph:
        ps = ph.psum()

        def scores(pe, h, qt, banks):
            return pe.matmul(banks[:, 0], mem.qk[0:96, h, qt * P:(qt + 1) * P], mem.qk[0:96, 4 + h],
                             start=True, stop=True)

        att = Attention(ph, "plain", 4, ps, m.ident, scores,
                        lambda h, kt: mem.v[:, kt, 64 * h:64 * h + 64],
                        lambda h: m.o[64 * (h % 2):64 * (h % 2) + 64, h // 2])
        with nc.Block() as block:
            @block.scalar
            def _(act):
                att.act(act)

            @block.vector
            def _(dve):
                att.dve(dve)

            @block.tensor
            def _(pe):
                att.pe(pe)


def diff_prepare(nc, m, mem):
    with Phase(nc, "difp") as ph:
        ps = ph.psum()
        sq, rt = ph.sb("sq", [P, 4, T]), ph.sb("rt", [P, 4, T])
        lamp = ph.sb("lamp", [P, 64])
        step, astep, prep = ph.sem("step"), ph.sem("astep"), ph.sem("prep")
        z = m.z
        units = [(z[:, Z_DQ + i], mem.gq if i < 2 else m.g[:, G_DK:G_DK + 1], mem.qk[:, i]) for i in range(4)]
        gn = GroupNorm(ph, "gn", units, P, 32, m.ones32, m.eps, ps, sq, rt, (m.rope[:, 2], m.rope[:, 3], m.rot32))
        lam = m.lamv[:].rearrange("p (a b d) -> p a b d", a=2, b=2)
        with nc.Block() as block:
            @block.scalar
            def _(act):
                act.wait_ge(prep, 1)
                act.activation(mem.lam2[:], mem.lam2[:], ACT.Exp).then_inc(astep, 1)
                gn.act(act)

            @block.vector
            def _(dve):
                link = linker(dve, step)
                link(dve.tensor_tensor(lamp[:].rearrange("p (a d) -> p a d", a=2), lam[:, :, 0], lam[:, :, 1], ALU.mult))
                dve.tensor_reduce(mem.lam2[:], lamp[:].rearrange("p (a d) -> p a d", a=2), AX.X, ALU.add).then_inc(prep, 1)
                dve.wait_ge(astep, 1)
                link(dve.tensor_tensor(mem.lamt[:, 0:1], mem.lam2[:, 1:2], mem.lam2[:, 0:1], ALU.subtract))
                link(dve.tensor_tensor(mem.lamt[:, 1:2], mem.lamt[:, 0:1], m.laminit[:, 0:1], ALU.subtract))
                link(dve.tensor_scalar(mem.gq, m.g[:, G_DQ:G_DQ + 1], float(32 ** -0.5), None, ALU.mult))
                link(dve.tensor_tensor(mem.gsub, m.g[:, G_SUB:G_SUB + 1], m.laminit[:, 1:2], ALU.mult))
                gn.dve(dve)
                dve.wait_ge(gn.done, 4)

            @block.tensor
            def _(pe):
                gn.pe(pe)


def diff_attend(nc, m, mem):
    with Phase(nc, "difa") as ph:
        ps = ph.psum()
        values = m.z[:, Z_DV:Z_DV + 2].rearrange("p a (b n) -> p (a b) n", b=2)

        def scores(pe, h, qt, banks):
            for i in range(2):
                s = 2 * h + i
                at = slice(32 * (s % 4), 32 * (s % 4) + 32)
                mm = pe.matmul(banks[:, i], mem.qk[at, s // 4, qt * P:(qt + 1) * P], mem.qk[at, 2 + s // 4],
                               start=True, stop=True, tile_position=(32 * (s % 4), 0))
            return mm

        att = Attention(ph, "diff", 4, ps, m.ident, scores,
                        lambda h, kt: values[:, kt, 64 * h:64 * h + 64],
                        lambda h: mem.od[64 * (h % 2):64 * (h % 2) + 64, h // 2], neglam=mem.lamt[:, 1:2])
        with nc.Block() as block:
            @block.scalar
            def _(act):
                att.act(act)

            @block.vector
            def _(dve):
                att.dve(dve)

            @block.tensor
            def _(pe):
                att.pe(pe)


def head_norm(nc, m, name, src, gain, dst, gate=None):
    with Phase(nc, name) as ph:
        ps = ph.psum()
        sq, rt = ph.sb("sq", [P, 2, T]), ph.sb("rt", [P, 2, T])
        gated = ph.sem("gated")
        gn = GroupNorm(ph, "gn", [(src[:, j], gain, dst[:, j]) for j in range(2)], P, 64, m.ones64, m.eps, ps, sq, rt)
        with nc.Block() as block:
            @block.scalar
            def _(act):
                gn.act(act)

            @block.vector
            def _(dve):
                gn.dve(dve)
                dve.wait_ge(gn.normed, 2)
                if gate is not None:
                    dve.tensor_tensor(dst, dst, gate, ALU.mult).then_inc(gated, 1)
                    dve.wait_ge(gated, 1)

            @block.tensor
            def _(pe):
                gn.pe(pe)


def fnet(nc, m, a):
    with Phase(nc, "fnet") as ph:
        ps = ph.psum()
        dft = ph.sb("dft", [P, 2, TT, T])
        dft64 = ph.sb("dft64", [P, 2 * P])
        mixed = ph.sb("mixed", [P, 2, TT, 2 * P])
        loaded, inner, inner_out, outer, outer_out = (
            ph.sem(s) for s in ("loaded", "inner", "inner_out", "outer", "outer_out"))
        with nc.Block() as block:
            @block.sync
            def _(sp):
                sp.dma_start(dft64[:], a["dft64"]).then_inc(loaded, 16)
                sp.dma_start(dft[:], a["dft"]).then_inc(loaded, 16)
                sp.wait_ge(loaded, 32)

            @block.tensor
            def _(pe):
                pe.wait_ge(loaded, 32)
                for i in range(2 * TT):
                    j, t = divmod(i, TT)
                    if i >= 4:
                        pe.wait_ge(inner_out, i - 3)
                    pe.matmul(ps[:, i % 4, 0:2 * P], m.z[:, Z_FU + j, t * P:(t + 1) * P], dft64[:],
                              start=True, stop=True).then_inc(inner, 1)
                pe.wait_ge(inner_out, 2 * TT)
                for j in range(2):
                    for t in range(TT):
                        for part in range(2):
                            mm = pe.matmul(ps[:, 4 + j], mixed[:, j, t, part * P:(part + 1) * P], dft[:, part, t],
                                           start=(t == 0 and part == 0), stop=(t == TT - 1 and part == 1))
                    mm.then_inc(outer, 1)

            @block.scalar
            def _(act):
                for i in range(2 * TT):
                    j, t = divmod(i, TT)
                    act.wait_ge(inner, i + 1)
                    act.activation(mixed[:, j, t], ps[:, i % 4, 0:2 * P], ACT.Copy).then_inc(inner_out, 1)
                for j in range(2):
                    act.wait_ge(outer, j + 1)
                    act.activation(m.o[:, 2 + j], ps[:, 4 + j], ACT.Copy).then_inc(outer_out, 1)
                act.wait_ge(outer_out, 2)


def hgrn(nc, m, a, od):
    with Phase(nc, "hgrn") as ph:
        ps = ph.psum()
        big = lambda name, n=1: ph.sb(name, [P, n, 2 * T] if n > 1 else [P, 2 * T])
        cum, key, work = big("cum", 2), big("key", 2), big("work", 2)
        qs, ks = big("qs", 2), big("ks", 2)
        masks = ph.sb("masks", [P, len(LEVELS) + 1, P])
        reset = ph.sb("reset", [P, T])
        masked = ph.sb("masked", [P, 2, T])
        kturned = ph.sb("kturned", [P, 2, TT, 2 * P])
        state = ph.sb("state", [P, 2, 3, 2, P])
        decay = ph.sb("decay", [P, 2, 2, TT])
        omlb = ph.sb("omlb", [P, 4])
        names = ("loaded", "prep", "sig", "forget", "logs", "scans", "link_v", "link_a", "diffs", "exps", "operands", "scored",
                 "masked_s", "valued", "carry_in", "carry_turned", "carry_out", "grown", "states", "out_copied")
        s = {n: ph.sem(n) for n in names}
        z = m.z
        hq = z[:, Z_HQ:Z_HQ + 2].rearrange("p a t -> p (a t)")
        gates = z[:, Z_HF:Z_HF + 4]
        values = z[:, Z_HV:Z_HV + 2].rearrange("p a (b n) -> p (a b) n", b=2)
        nl = len(LEVELS) + 1

        def halves(x, b):
            v = x.rearrange("p (n c) -> p n c", c=2 * b)
            return v[:, :, 0:b], v[:, :, b:2 * b]

        def blocks(x):
            return x.rearrange("p (n c) -> p n c", c=P)

        with nc.Block() as block:
            @block.sync
            def _(sp):
                sp.dma_start(masks[:], a["masks"]).then_inc(s["loaded"], 16)
                sp.dma_start(reset[:], a["reset"]).then_inc(s["loaded"], 16)
                sp.wait_ge(s["loaded"], 32)

            @block.gpsimd
            def _(pool):
                pool.memset(state[:], 0.0).then_inc(s["states"], 1)

            @block.scalar
            def _(act):
                act.activation(gates, gates, ACT.Sigmoid).then_inc(s["sig"], 1)
                act.activation(z[:, Z_HG:Z_HG + 2], z[:, Z_HG:Z_HG + 2], ACT.Sigmoid).then_inc(s["sig"], 1)
                act.wait_ge(s["forget"], 4)
                act.activation(work[:].rearrange("p d t -> p (d t)"), gates.rearrange("p a t -> p (a t)"), ACT.Ln)\
                   .then_inc(s["logs"], 1)
                act.wait_ge(s["diffs"], 1)
                act.activation(work[:], work[:], ACT.Exp).then_inc(s["exps"], 1)
                act.activation(decay[:, 0], cum[:, 0].rearrange("p (j n c) -> p j n c", j=2, c=P)[:, :, :, P - 1],
                               ACT.Exp).then_inc(s["exps"], 1)
                act.activation(decay[:, 1], cum[:, 1].rearrange("p (j n c) -> p j n c", j=2, c=P)[:, :, :, 0],
                               ACT.Exp).then_inc(s["exps"], 1)
                act.activation(qs[:], cum[:], ACT.Exp).then_inc(s["exps"], 1)
                for i in range(4):
                    d, j = divmod(i, 2)
                    act.wait_ge(s["carry_turned"], i + 1)
                    act.activation(kturned[:, d].rearrange("p t (j n) -> p t j n", j=2)[:, :, j],
                                   ps[:, i].rearrange("p (t n) -> p t n", t=TT), ACT.Copy).then_inc(s["carry_out"], 1)
                for n, b in enumerate(LEVELS):
                    fl, fu = halves(work[:, 0], b)
                    bl, bu = halves(work[:, 1], b)
                    ql, qu = halves(qs[:, n % 2], b)
                    kl, ku = halves(ks[:, n % 2], b)
                    act.wait_ge(s["diffs"], 2 + 2 * n + 1)
                    if n >= 1:
                        act.wait_ge(s["scored"], TT * (n - 1))
                    act.activation(qu, fu, ACT.Exp).then_inc(s["exps"], 1)
                    act.activation(kl, fl, ACT.Exp, scale=-1.0).then_inc(s["exps"], 1)
                    act.activation(ql, bl, ACT.Exp).then_inc(s["exps"], 1)
                    act.activation(ku, bu, ACT.Exp, scale=-1.0).then_inc(s["exps"], 1)
                for j in range(2):
                    act.wait_ge(s["valued"], nl * TT + 1)
                    act.activation(od[:, j], ps[:, 6 + j], ACT.Copy).then_inc(s["out_copied"], 1)
                act.wait_ge(s["out_copied"], 2)

            @block.vector
            def _(dve):
                link = linker(dve, s["link_v"])
                link(dve.tensor_scalar(omlb[:], m.lbl[:], -1.0, 1.0, ALU.mult, ALU.add))
                dve.wait_ge(s["sig"], 1)
                for i in range(4):
                    dve.tensor_scalar(gates[:, i], gates[:, i], omlb[:, i:i + 1], m.lbl[:, i:i + 1], ALU.mult, ALU.add)\
                       .then_inc(s["forget"], 1)
                dve.wait_ge(s["forget"], 4)
                link(dve.tensor_scalar(key[:].rearrange("p d t -> p (d t)"), gates.rearrange("p a t -> p (a t)"),
                                       -1.0, 1.0, ALU.mult, ALU.add))
                dve.wait_ge(s["logs"], 1)
                dve.wait_ge(s["loaded"], 32)
                for j in range(2):
                    at = slice(j * T, (j + 1) * T)
                    dve.tensor_tensor_scan(cum[:, 0, at], reset[:], work[:, 0, at], 0.0, ALU.mult, ALU.add)\
                       .then_inc(s["scans"], 1)
                    dve.tensor_tensor_scan(cum[:, 1, at][:, ::-1], reset[:], work[:, 1, at][:, ::-1], 0.0,
                                           ALU.mult, ALU.add).then_inc(s["scans"], 1)
                dve.wait_ge(s["scans"], 4)
                last_f = blocks(cum[:, 0])[:, :, P - 1:P].broadcast_to([P, 2 * TT, P])
                last_b = blocks(cum[:, 1])[:, :, 0:1].broadcast_to([P, 2 * TT, P])
                link(dve.tensor_tensor(blocks(work[:, 0]), last_f, blocks(cum[:, 0]), ALU.subtract))
                dve.tensor_tensor(blocks(work[:, 1]), last_b, blocks(cum[:, 1]), ALU.subtract).then_inc(s["diffs"], 1)
                dve.wait_ge(s["exps"], 4)
                dve.tensor_tensor(work[:], work[:], key[:], ALU.mult).then_inc(s["carry_in"], 1)
                hq2 = hq.rearrange("p (o t) -> p o t", o=1).broadcast_to([P, 2, 2 * T])
                dve.tensor_tensor(qs[:], qs[:], hq2, ALU.mult).then_inc(s["carry_in"], 1)
                dve.wait_ge(s["states"], 1)
                done = 1
                for d in range(2):
                    for i in range(3):
                        c = i if d == 0 else TT - 1 - i
                        for j in range(2):
                            g = (d * 3 + i) * 2 + j
                            dve.wait_ge(s["grown"], 4 * (g // 4) + 4)
                            for half in range(2):
                                r = slice(64 * half, 64 * half + 64)
                                new = state[r, d, i, j, r]
                                src = ps[r, 4 + g // 4 if g < 8 else 0, (g % 4) * P + 64 * half:(g % 4) * P + 64 * half + 64]
                                if i == 0:
                                    ins = dve.tensor_copy(new, src)
                                else:
                                    dve.wait_ge(s["states"], done - 3)
                                    ins = dve.scalar_tensor_tensor(new, state[r, d, i - 1, j, r], decay[r, d, j, c:c + 1],
                                                                   src, ALU.mult, ALU.add)
                                ins.then_inc(s["states"], 1)
                                done += 1
                def mask_out(n):
                    for t in range(TT):
                        i = n * TT + t
                        dve.wait_ge(s["scored"], i + 1)
                        if i >= 2:
                            dve.wait_ge(s["valued"], i)
                        b = 2 * (i % 3)
                        for odd in range(2):
                            ins = dve.tensor_tensor(
                                masked[:, i % 2, odd * 2 * P:(odd + 1) * 2 * P].rearrange("p (h t) -> p h t", h=2),
                                ps[:, b + odd, 0:2 * P].rearrange("p (h t) -> p h t", h=2),
                                masks[:, n:n + 1].broadcast_to([P, 2, P]), ALU.mult)
                        ins.then_inc(s["masked_s"], 1)

                dve.wait_ge(s["carry_out"], 4)
                dve.wait_ge(s["valued"], 1)
                for n, b in enumerate(LEVELS):
                    if n >= 1:
                        dve.wait_ge(s["exps"], 4 + 4 * n)
                    for d in range(2):
                        v = cum[:, d].rearrange("p (n c) -> p n c", c=2 * b)
                        ref = v[:, :, b - 1:b] if d == 0 else v[:, :, b:b + 1]
                        dve.tensor_tensor(work[:, d].rearrange("p (n c) -> p n c", c=2 * b), v,
                                          ref.broadcast_to([P, T // b, 2 * b]), ALU.subtract).then_inc(s["diffs"], 1)
                    if n >= 1:
                        mask_out(n - 1)
                    dve.wait_ge(s["exps"], 4 + 4 * (n + 1))
                    dve.tensor_tensor(qs[:, n % 2], qs[:, n % 2], hq, ALU.mult).then_inc(s["operands"], 1)
                    kl, ku = halves(ks[:, n % 2], b)
                    dve.tensor_tensor(kl, kl, halves(key[:, 0], b)[0], ALU.mult).then_inc(s["operands"], 1)
                    dve.tensor_tensor(ku, ku, halves(key[:, 1], b)[1], ALU.mult).then_inc(s["operands"], 1)
                n = nl - 1
                mask_out(n - 1)
                dve.tensor_copy(qs[:, n % 2], hq).then_inc(s["operands"], 1)
                dve.tensor_tensor(ks[:, n % 2], key[:, 0], key[:, 1], ALU.add).then_inc(s["operands"], 1)
                mask_out(n)

            @block.tensor
            def _(pe):
                pe.wait_ge(s["carry_in"], 2)
                for i in range(4):
                    d, j = divmod(i, 2)
                    for t in range(TT):
                        mm = pe.transpose(ps[:, i, t * P:(t + 1) * P], work[:, d, j * T + t * P:j * T + (t + 1) * P], m.ident)
                    mm.then_inc(s["carry_turned"], 1)
                for g in range(12):
                    di, j = divmod(g, 2)
                    d, i = divmod(di, 3)
                    c = i if d == 0 else TT - 1 - i
                    pe.wait_ge(s["carry_out"], 4)
                    pe.matmul(ps[:, 4 + g // 4 if g < 8 else 0, (g % 4) * P:(g % 4 + 1) * P],
                              kturned[:, d, c, j * P:(j + 1) * P], values[:, c, j * P:(j + 1) * P],
                              start=True, stop=True).then_inc(s["grown"], 1)
                pe.wait_ge(s["states"], 25)
                for j in range(2):
                    for d in range(2):
                        for i in range(3):
                            c = i + 1 if d == 0 else TT - 2 - i
                            mm = pe.matmul(ps[:, 6 + j, c * P:(c + 1) * P], state[:, d, i, j],
                                           qs[:, d, j * T + c * P:j * T + (c + 1) * P],
                                           start=(d == 0 and i == 0), stop=False, skip_group_check=True)
                mm.then_inc(s["valued"], 1)
                total = nl * TT
                for i in range(total + 1):
                    if i < total:
                        n, t = divmod(i, TT)
                        if t == 0:
                            pe.wait_ge(s["operands"], 3 * (n + 1) if n < nl - 1 else 3 * n + 2)
                        if i >= 3:
                            pe.wait_ge(s["masked_s"], i - 2)
                        for h in range(4):
                            r = slice(64 * (h % 2), 64 * (h % 2) + 64)
                            at = slice((h // 2) * T + t * P, (h // 2) * T + (t + 1) * P)
                            mm = pe.matmul(ps[:, 2 * (i % 3) + h % 2, (h // 2) * P:(h // 2 + 1) * P], ks[r, n % 2, at], qs[r, n % 2, at],
                                           start=True, stop=True)
                        mm.then_inc(s["scored"], 1)
                    i -= 1
                    if i >= 0:
                        n, t = divmod(i, TT)
                        pe.wait_ge(s["masked_s"], i + 1)
                        for h in range(4):
                            mm = pe.matmul(ps[64 * (h % 2):64 * (h % 2) + 64, 6 + h // 2, t * P:(t + 1) * P],
                                           values[:, t, 64 * h:64 * h + 64], masked[:, i % 2, (2 * (h % 2) + h // 2) * P:(2 * (h % 2) + h // 2 + 1) * P],
                                           start=False, stop=(i == total - 1), skip_group_check=True)
                        mm.then_inc(s["valued"], 1)


class Experts:

    def __init__(self, ph, m, ring, ps, steps, c0, w0, hidden, subs=1, gate_tile=None, factor=None):
        self.m, self.ring, self.ps, self.steps, self.c0, self.w0 = m, ring, ps, steps, c0, w0
        self.subs, self.gate_tile, self.factor = subs, gate_tile, factor
        self.hid_hi, self.hid_lo = hidden
        self.silu, self.hid = m.z[:, 18:20], m.z[:, 20:22]
        (self.up_done, self.silu_done, self.product_done, self.weighted, self.hid_hi_done,
         self.hid_lo_done, self.down_done, self.down_added) = (
            ph.sem(f"x_{s}") for s in ("up_done", "silu_done", "product_done", "weighted", "hid_hi_done", "hid_lo_done", "down_done", "down_added"))

    def open(self, sp):
        sp.sem_inc(self.product_done, 2)
        sp.sem_inc(self.down_added, 4)

    def each(self, eng):
        with eng.Fori(0, self.steps // self.subs) as turn:
            for sub in range(self.subs):
                yield turn * self.subs + sub, turn, sub

    def sp(self, sp, gate_src, up_src, down_src):
        for j, turn, sub in self.each(sp):
            self.ring.load(sp, 2 * j + self.c0, self.c0 % 2, gate_src(turn, sub))
            self.ring.load(sp, 2 * j + (self.c0 + 1), (self.c0 + 1) % 2, up_src(turn, sub))
            self.ring.load_wide(sp, j + self.w0, down_src(turn, sub))

    def pool(self, pool):
        for j, _, _ in self.each(pool):
            self.ring.cut_lo(pool, 2 * j + self.c0, self.c0 % 2)
            self.ring.cut_lo(pool, 2 * j + (self.c0 + 1), (self.c0 + 1) % 2)
            self.ring.cut_wide_lo(pool, j + self.w0)

    def act(self, act):
        ring, c0 = self.ring, self.c0
        for j, _, _ in self.each(act):
            act.wait_ge(self.up_done, 2 * j)
            ring.cut_hi(act, c0 % 2, 16 * j + 16 * (c0 // 2 + 1))
            ring.cut_hi(act, (c0 + 1) % 2, 16 * j + 16 * ((c0 + 1) // 2 + 1))
            act.wait_ge(self.down_done, 8 * j)
            ring.cut_wide_hi(act, j + self.w0)
            for i in range(2):
                act.wait_ge(self.up_done, 2 * j + (i + 1))
                act.activation(self.silu[:, i], self.ps[:, 2 * i], ACT.Silu).then_inc(self.silu_done, 1)
            for i in range(2):
                act.wait_ge(self.weighted if self.gate_tile else self.product_done,
                            2 * j + (i + 1 if self.gate_tile else i + 3))
                act.activation(self.hid_hi[:, i], self.hid[:, i], ACT.Copy).then_inc(self.hid_hi_done, 1)

    def dve(self, dve):
        m = self.m
        for j, turn, _ in self.each(dve):
            for i in range(2):
                dve.wait_ge(self.silu_done, 2 * j + (i + 1))
                dve.tensor_tensor(self.hid[:, i], self.silu[:, i], self.ps[:, 2 * i + 1], ALU.mult)\
                   .then_inc(self.product_done, 1)
                if self.gate_tile:
                    dve.wait_ge(self.product_done, 2 * j + (i + 3))
                    dve.tensor_tensor(self.hid[:, i], self.hid[:, i], self.gate_tile(turn), ALU.mult)\
                       .then_inc(self.weighted, 1)
            for i in range(2):
                dve.wait_ge(self.hid_hi_done, 2 * j + (i + 1))
                dve.tensor_tensor(self.hid_lo[:, i], self.hid[:, i], self.hid_hi[:, i].bitcast(F32), ALU.subtract)\
                   .then_inc(self.hid_lo_done, 1)
            for c in range(KD):
                dve.wait_ge(self.down_done, 8 * j + (c + 1))
                bank = self.ps[:, 4 + c % 4]
                if self.factor:
                    ins = dve.scalar_tensor_tensor(m.x[:, c], bank, self.factor(c), m.x[:, c], ALU.mult, ALU.add)
                else:
                    ins = dve.tensor_tensor(m.x[:, c], m.x[:, c], bank, ALU.add)
                ins.then_inc(self.down_added, 1)
        dve.wait_ge(self.down_added, 4 + 8 * self.steps)

    def pe(self, pe):
        m, ring, ps = self.m, self.ring, self.ps
        slots = [(cols(ring.hi[:, (self.c0 + i) % 2], CW), cols(ring.lo[:, (self.c0 + i) % 2], CW)) for i in range(2)]
        whi, wlo = cols(ring.whi, D, 2), cols(ring.wlo, D, 2)
        for j, _, _ in self.each(pe):
            ring.wait_cut(pe, 2 * j + (self.c0 + 1))
            for i in range(2):
                pe.wait_ge(self.product_done, 2 * j + (i + 1))
                at = slice(i * P, (i + 1) * P)
                for g, (hi, lo) in enumerate(slots):
                    mm = product3(pe, ps[:, 2 * i + g], lambda k: hi[:, k, at], lambda k: lo[:, k, at],
                                  lambda k: m.hi[:, k], lambda k: m.lo[:, k], range(KD))
                mm.then_inc(self.up_done, 1)
            pe.wait_ge(ring.wide_lo, j + (self.w0 + 1))
            pe.wait_ge(self.hid_lo_done, 2 * j + 1)

            def down(c, ks, start, stop):
                at = slice(c * P, (c + 1) * P)
                return product3(pe, ps[:, 4 + c % 4], lambda k: whi[:, k, at], lambda k: wlo[:, k, at],
                                lambda k: self.hid_hi[:, k], lambda k: self.hid_lo[:, k], ks, start, stop)

            for c in range(4):
                pe.wait_ge(self.down_added, 8 * j + (c + 1))
                down(c, (0,), True, False)
            pe.wait_ge(self.hid_lo_done, 2 * j + 2)
            for c in range(4):
                down(c, (1,), False, True).then_inc(self.down_done, 1)
            for c in range(4, 8):
                pe.wait_ge(self.down_added, 8 * j + (c + 1))
                down(c, (0, 1), True, True).then_inc(self.down_done, 1)


def merge_and_ffn(nc, m, a, l):
    with Phase(nc, "ffn") as ph:
        ring = Ring(ph, True)
        ps = ph.psum()
        z = m.z
        ohi, olo = ph.sb("ohi", [P, 2, T], F32R), ph.sb("olo", [P, 2, T], F32R)
        merged, sig, tmp = z[:, 0:8], z[:, 18:22], z[:, 22]
        names = ("o_hi", "o_lo", "gate_done", "sig_done", "gated", "merged_s", "m_hi", "m_lo", "out_done", "out_added", "zeroed")
        s = {n: ph.sem(n) for n in names}
        norm = Norm(ph, "n", m.x, z[:, 8:16], z[:, 16], z[:, 17], z[:, 0:8], m.hi, m.lo, ps[:, 7], m.ones, m.eps, T)
        c_out, c_ffn = 4 * NB, 4 * NB + 4
        ex = Experts(ph, m, ring, ps, FF_STEPS, c_ffn, NB, (ohi, olo))
        w_in = a["w_in"][l].rearrange("(k p) n -> p k n", p=P)
        w_br = a["w_branch"][l].rearrange("n (k p) d -> n p k d", p=P)
        w_out = a["w_out"][l].rearrange("(k p) n -> p k n", p=P)
        w_gu = a["w_gate_up"][l].rearrange("(k p) n -> p k n", p=P)
        w_dn = a["w_down"][l].rearrange("(j k p) n -> j p k n", p=P, k=2)
        with nc.Block() as block:
            @block.sync
            def _(sp):
                ring.open(sp)
                ex.open(sp)
                sp.sem_inc(s["merged_s"], 4)
                with sp.Fori(0, NB) as n:
                    ring.load_wide(sp, n, w_br[n])
                    for i in range(4):
                        ring.load(sp, 4 * n + i, i % 2, w_in[:, :, bass.ds(n * D + (C_GATE + i * CW), CW)])
                for i in range(4):
                    ring.load(sp, c_out + i, i % 2, w_out[:, :, i * CW:(i + 1) * CW])
                ex.sp(sp, lambda j, _: w_gu[:, :, bass.ds(j * CW, CW)],
                      lambda j, _: w_gu[:, :, bass.ds(j * CW + DFF, CW)], lambda j, _: w_dn[j])

            @block.gpsimd
            def _(pool):
                with pool.Fori(0, NB) as n:
                    ring.cut_wide_lo(pool, n)
                    for i in range(4):
                        ring.cut_lo(pool, 4 * n + i, i % 2)
                for i in range(4):
                    ring.cut_lo(pool, c_out + i, i % 2)
                ex.pool(pool)

            @block.scalar
            def _(act):
                ring.cut_hi(act, 0, 16)
                with act.Fori(0, NB) as n:
                    act.wait_ge(s["gate_done"], 8 * n)
                    for j in range(2):
                        act.activation(ohi[:, j], m.o[:, bass.ds(2 * n + j, 1)].rearrange("p o t -> p (o t)"), ACT.Copy)\
                           .then_inc(s["o_hi"], 1)
                    ring.cut_wide_hi(act, n)
                    for i in range(4):
                        act.wait_ge(s["gate_done"], 8 * n + 2 * i)
                        ring.cut_hi(act, (i + 1) % 2, 32 * n + 16 * ((i + 1) // 2 + 1))
                        for p in range(2):
                            t = 2 * i + p
                            act.wait_ge(s["gate_done"], 8 * n + (t + 1))
                            act.wait_ge(s["merged_s"], 8 * n + (t + 1))
                            act.activation(sig[:, t % 4], ps[:, t % 4], ACT.Sigmoid).then_inc(s["sig_done"], 1)
                act.wait_ge(s["gate_done"], 8 * NB)
                for k in range(KD):
                    act.wait_ge(s["merged_s"], 4 + 8 * (NB - 1) + k + 1)
                    act.activation(m.hi[:, k], merged[:, k], ACT.Copy).then_inc(s["m_hi"], 1)
                for i in range(3):
                    act.wait_ge(s["out_done"], 2 * i)
                    ring.cut_hi(act, (i + 1) % 2, 16 * ((c_out + i + 1) // 2 + 1))
                act.wait_ge(s["out_added"], KD)
                norm.act_squares(act)
                norm.act_root(act)
                act.wait_ge(s["out_done"], KD)
                norm.act_hi(act)
                ex.act(act)

            @block.vector
            def _(dve):
                dve.memset(merged, 0.0).then_inc(s["zeroed"], 1)
                dve.wait_ge(s["zeroed"], 1)
                with dve.Fori(0, NB) as n:
                    for j in range(2):
                        dve.wait_ge(s["o_hi"], 2 * n + (j + 1))
                        dve.tensor_tensor(olo[:, j], m.o[:, bass.ds(2 * n + j, 1)].rearrange("p o t -> p (o t)"),
                                          ohi[:, j].bitcast(F32), ALU.subtract).then_inc(s["o_lo"], 1)
                    for t in range(KD):
                        dve.wait_ge(s["sig_done"], 8 * n + (t + 1))
                        dve.wait_ge(s["merged_s"], 8 * n + (t + 4))
                        dve.tensor_tensor(tmp, sig[:, t % 4], ps[:, 4 + t % 4], ALU.mult).then_inc(s["gated"], 1)
                        dve.wait_ge(s["gated"], 8 * n + (t + 1))
                        dve.tensor_tensor(merged[:, t], merged[:, t], tmp, ALU.add).then_inc(s["merged_s"], 1)
                for k in range(KD):
                    dve.wait_ge(s["m_hi"], k + 1)
                    dve.tensor_tensor(m.lo[:, k], merged[:, k], m.hi[:, k].bitcast(F32), ALU.subtract).then_inc(s["m_lo"], 1)
                for t in range(KD):
                    dve.wait_ge(s["out_done"], t + 1)
                    dve.tensor_tensor(m.x[:, t], m.x[:, t], ps[:, t % 4], ALU.add).then_inc(s["out_added"], 1)
                norm.dve_total(dve)
                norm.dve_apply(dve, lambda k: m.g[:, G_FFN + k:G_FFN + k + 1])
                ex.dve(dve)

            @block.tensor
            def _(pe):
                whi, wlo = cols(ring.whi, D, 2), cols(ring.wlo, D, 2)
                with pe.Fori(0, NB) as n:
                    pe.wait_ge(s["o_lo"], 2 * n + 2)
                    pe.wait_ge(ring.wide_lo, n + 1)
                    for i in range(4):
                        ring.wait_cut(pe, 4 * n + i)
                        hi, lo = cols(ring.hi[:, i % 2], CW), cols(ring.lo[:, i % 2], CW)
                        for p in range(2):
                            t = 2 * i + p
                            pe.wait_ge(s["merged_s"], 8 * n + (t + 1))
                            ct, cp = slice(t * P, (t + 1) * P), slice(p * P, (p + 1) * P)
                            product3(pe, ps[:, 4 + t % 4], lambda k: whi[:, k, ct], lambda k: wlo[:, k, ct],
                                     lambda k: ohi[:, k], lambda k: olo[:, k], range(2))
                            product3(pe, ps[:, t % 4], lambda k: hi[:, k, cp], lambda k: lo[:, k, cp],
                                     lambda k: m.hi[:, k], lambda k: m.lo[:, k], range(KD)).then_inc(s["gate_done"], 1)
                pe.wait_ge(s["m_lo"], KD)
                for t in range(KD):
                    i = t // 2
                    if t % 2 == 0:
                        ring.wait_cut(pe, c_out + i)
                    hi, lo = cols(ring.hi[:, i % 2], CW), cols(ring.lo[:, i % 2], CW)
                    cp = slice((t % 2) * P, (t % 2 + 1) * P)
                    if t >= 4:
                        pe.wait_ge(s["out_added"], t - 3)
                    product3(pe, ps[:, t % 4], lambda k: hi[:, k, cp], lambda k: lo[:, k, cp],
                             lambda k: m.hi[:, k], lambda k: m.lo[:, k], range(KD)).then_inc(s["out_done"], 1)
                norm.pe_spread(pe)
                pe.wait_ge(norm.lo_cut, KD)
                ex.pe(pe)


M_SHA, M_SCA, M_GA, M_SHF, M_SCF, M_GF = 0, 8, 16, 24, 32, 40
MODS = 48


def modulation(nc, m, a):
    slots, turns = 4, 6
    with Phase(nc, "ada") as ph:
        ps = ph.psum()
        raw = ph.sb("raw", [P, slots, CHUNK])
        cond = ph.sb("cond", [P, KD, 2])
        bias = ph.sb("bias", [P, MODS])
        small, silu, chunk_used, done, scaled = (ph.sem(s) for s in ("small", "silu", "chunk_used", "done", "scaled"))
        ready = [ph.sem(f"ready{i}") for i in range(slots)]
        w = a["w_ada"].rearrange("(k p) n -> p k n", p=P)
        with nc.Block() as block:
            @block.sync
            def _(sp):
                sp.dma_start(cond[:], a["cond"]).then_inc(small, 16)
                sp.dma_start(bias[:], a["b_ada"]).then_inc(small, 16)
                sp.sem_inc(chunk_used, slots)
                with sp.Fori(0, turns) as j:
                    for i in range(slots):
                        sp.wait_ge(chunk_used, slots * j + (i + 1))
                        sp.dma_start(cols(raw[:, i], CW), w[:, :, bass.ds(j * (slots * CW) + i * CW, CW)])\
                          .then_inc(ready[i], 16)

            @block.scalar
            def _(act):
                act.wait_ge(small, 32)
                act.activation(cond[:], cond[:], ACT.Silu).then_inc(silu, 1)

            @block.tensor
            def _(pe):
                pe.wait_ge(silu, 1)
                with pe.Fori(0, turns) as j:
                    for i in range(slots):
                        pe.wait_ge(ready[i], 16 * j + 16)
                        chunk = cols(raw[:, i], CW)
                        for p in range(2):
                            for k in range(KD):
                                mm = pe.matmul(ps[:, 0, bass.ds(j * (4 * slots) + (4 * i + 2 * p), 2)],
                                               chunk[:, k, p * P:(p + 1) * P], cond[:, k],
                                               start=(k == 0), stop=(k == KD - 1))
                        mm.then_inc(chunk_used, 1)

            @block.vector
            def _(dve):
                dve.wait_ge(chunk_used, slots * (turns + 1))
                dve.tensor_tensor(m.mod[:], ps[:, 0, 0:2 * MODS].rearrange("p (n o) -> p n o", o=2),
                                  bias[:].rearrange("p (n o) -> p n o", o=1).broadcast_to([P, MODS, 2]), ALU.add)\
                   .then_inc(done, 1)
                dve.wait_ge(done, 1)
                for t in (M_SCA, M_SCF):
                    dve.tensor_scalar(m.mod[:, t:t + KD], m.mod[:, t:t + KD], 1.0, None, ALU.add).then_inc(scaled, 1)
                dve.wait_ge(scaled, 2)


NA_W = 512
N_Q, N_K, N_U, N_VS, N_V, N_KC = 0, 4, 8, 12, 16, 20


def project2(nc, m, a):
    plan = []
    for base, kind in ((0, "q"), (NA_W, "k"), (3 * NA_W, "u"), (2 * NA_W, "v"), (4 * NA_W, "vs")):
        plan += [(base + half * CW, kind, half) for half in range(2)]
    tiles = []
    for c, (_, kind, _) in enumerate(plan):
        n = {"q": 2, "u": 2, "k": 4, "vs": TT, "v": TT + CT}[kind]
        tiles += [(c, i) for i in range(n)]
    with Phase(nc, "proj2") as ph:
        ring = Ring(ph, False)
        ps = ph.psum()
        ctx = ph.sb("ctx", [P, KD, CTX])
        chi, clo = ph.sb("ctx_hi", [P, KD, CTX], F32R), ph.sb("ctx_lo", [P, KD, CTX], F32R)
        ctx_loaded, tile_done, evicted = (ph.sem(s) for s in ("ctx_loaded", "tile_done", "evicted"))
        z = m.z
        norm = Norm(ph, "n", m.x, z[:, 8:16], z[:, 16], z[:, 17], z[:, 0:8], m.hi, m.lo, ps[:, 7],
                    m.ones, m.eps, T)
        half_tiles = lambda x: x.rearrange("p a (b t) -> p (a b) t", b=2)
        cnorm = Norm(ph, "c", ctx, half_tiles(m.o[:, 4:8]), z[:, 18, 0:CTX], z[:, 19, 0:CTX],
                     half_tiles(m.o[:, 0:4]), chi, clo, ps[:, 6, 0:CTX], m.ones, m.eps, CTX)
        w = a["w_in2"].rearrange("(k p) n -> p k n", p=P)
        with nc.Block() as block:
            @block.sync
            def _(sp):
                ring.open(sp)
                sp.dma_start(ctx[:], a["ctxT"].rearrange("(k p) t -> p k t", p=P)).then_inc(ctx_loaded, 16)
                for c, (col, _, _) in enumerate(plan):
                    ring.load(sp, c, c % RING, w[:, :, col:col + CW])

            @block.gpsimd
            def _(pool):
                for c in range(len(plan)):
                    ring.cut_lo(pool, c, c % RING)

            @block.vector
            def _(dve):
                norm.dve_total(dve)
                norm.dve_apply(dve, lambda k: m.mod[:, M_SCA + k, 0:1], lambda k: m.mod[:, M_SHA + k, 0:1])
                cnorm.dve_total(dve)
                cnorm.dve_apply(dve, lambda k: m.mod[:, M_SCA + k, 1:2], lambda k: m.mod[:, M_SHA + k, 1:2])

            @block.scalar
            def _(act):
                def cut(c):
                    if c < len(plan):
                        if c >= RING:
                            act.wait_ge(tile_done, max(i for i, t in enumerate(tiles) if t[0] == c - RING) + 1)
                        ring.cut_hi(act, c % RING, 16 * (c // RING + 1))

                norm.act_squares(act)
                act.wait_ge(ctx_loaded, 16)
                cnorm.act_squares(act)
                cut(0)
                cut(1)
                norm.act_root(act)
                norm.act_hi(act)
                cnorm.act_root(act)
                cnorm.act_hi(act)
                for i, (c, part) in enumerate(tiles):
                    if part == 0 and c:
                        cut(c + 1)
                    _, kind, half = plan[c]
                    bank = ps[:, i % 6]
                    act.wait_ge(tile_done, i + 1)
                    if kind == "k" and part >= 2:
                        t = 2 * half + part - 2
                        ins = act.activation(z[:, N_KC + t // 2, (t % 2) * CTX:(t % 2 + 1) * CTX], bank[:, 0:CTX], ACT.Copy)
                    elif kind in "qku":
                        first = {"q": N_Q, "k": N_K, "u": N_U}[kind]
                        ins = act.activation(z[:, first + 2 * half + part], bank,
                                             ACT.Gelu_apprx_tanh if kind == "u" else ACT.Copy)
                    else:
                        at = slice(half * CW, (half + 1) * CW)
                        if kind == "vs":
                            ins = act.activation(z[:, N_VS + part, at], bank[:, 0:CW], ACT.Gelu_apprx_tanh)
                        elif part < TT:
                            ins = act.activation(z[:, N_V + part, at], bank[:, 0:CW], ACT.Copy)
                        else:
                            ins = act.activation(m.o[:, part - TT, at], bank[:, 0:CW], ACT.Copy)
                    ins.then_inc(evicted, 1)
                act.wait_ge(evicted, len(tiles))

            @block.tensor
            def _(pe):
                norm.pe_spread(pe)
                cnorm.pe_spread(pe)
                pe.wait_ge(norm.lo_cut, KD)
                for i, (c, part) in enumerate(tiles):
                    _, kind, _ = plan[c]
                    hi, lo = cols(ring.hi[:, c % RING], CW), cols(ring.lo[:, c % RING], CW)
                    if part == 0:
                        ring.wait_cut(pe, c)
                    if i >= 6:
                        pe.wait_ge(evicted, i - 5)
                    bank = ps[:, i % 6]
                    if kind in "qku":
                        of_ctx = part >= 2
                        if of_ctx:
                            pe.wait_ge(cnorm.lo_cut, KD)
                        at = slice((part % 2) * P, (part % 2 + 1) * P)
                        xh, xl = (chi, clo) if of_ctx else (m.hi, m.lo)
                        mm = product3(pe, bank[:, 0:CTX] if of_ctx else bank, lambda k: hi[:, k, at], lambda k: lo[:, k, at],
                                      lambda k: xh[:, k], lambda k: xl[:, k], range(KD))
                    else:
                        xh, xl, t = (m.hi, m.lo, part) if part < TT else (chi, clo, part - TT)
                        at = slice(t * P, (t + 1) * P)
                        mm = product3(pe, bank[:, 0:CW], lambda k: xh[:, k, at], lambda k: xl[:, k, at],
                                      lambda k: hi[:, k], lambda k: lo[:, k], range(KD))
                    mm.then_inc(tile_done, 1)


def na_prepare(nc, m, a):
    with Phase(nc, "nap") as ph:
        ps = ph.psum()
        sq, rt = ph.sb("sq", [P, 12, T]), ph.sb("rt", [P, 12, T])
        prep = ph.sem("prep")
        z, kc = m.z, m.z[:, N_KC:N_KC + 2].rearrange("p a (b t) -> p (a b) t", b=2)
        qg, kg = m.vec2[:, 0:1], m.vec2[:, 1:2]
        gn = GroupNorm(ph, "gn", [(z[:, i], qg if i < 4 else kg, z[:, i]) for i in range(8)], P, 64, m.ones64,
                       m.eps, ps, sq, rt)
        cn = GroupNorm(ph, "cn", [(kc[:, i], kg, kc[:, i]) for i in range(4)], P, 64, m.ones64, m.eps,
                       ps[:, 4:8], sq[:, 8:12], rt[:, 8:12], width=CTX)
        with nc.Block() as block:
            @block.scalar
            def _(act):
                gn.act(act)
                cn.act(act)

            @block.vector
            def _(dve):
                dve.tensor_scalar(qg, qg, 0.125, None, ALU.mult).then_inc(prep, 1)
                dve.wait_ge(prep, 1)
                gn.dve(dve)
                cn.dve(dve)
                dve.wait_ge(cn.normed, 4)

            @block.tensor
            def _(pe):
                gn.pe(pe)
                cn.pe(pe)


def na_attend(nc, m, a):
    OFFSETS = 14
    heads = 8
    with Phase(nc, "naa") as ph:
        ps = ph.psum()
        bias = ph.sb("rpb", [P, 2, OFFSETS * 64])
        mask = ph.sb("mask", [P, 64])
        mask_loaded, masked = ph.sem("mask_loaded"), ph.sem("masked")
        bias_loaded = [ph.sem(f"bias_loaded{i}") for i in range(2)]
        z, kc = m.z, m.z[:, N_KC:N_KC + 2].rearrange("p a (b t) -> p (a b) t", b=2)

        def scores(pe, h, qt, banks):
            r, j = slice(64 * (h % 2), 64 * (h % 2) + 64), h // 2
            q = z[r, N_Q + j, qt * P:(qt + 1) * P]
            pe.matmul(banks[:, 0], q, z[r, N_K + j], start=True, stop=True)
            return pe.matmul(banks[:, 1, 0:CTX], q, kc[r, j], start=True, stop=True)

        def values(h, kt):
            v = z[:, N_V + kt] if kt < 4 else m.o[:, kt - 4]
            return v[:, 64 * h:64 * h + 64]

        def add_mask(dve, u):
            h = u // TT
            if u % TT == 0:
                dve.wait_ge(mask_loaded, 16)
                dve.wait_ge(bias_loaded[h % 2], 32 * (h // 2 + 1))
                b = bias[:, h % 2].rearrange("p (r c) -> p r c", c=64)
                dve.tensor_tensor(b, b, mask[:].rearrange("p (o c) -> p o c", o=1).broadcast_to([P, OFFSETS, 64]),
                                  ALU.add).then_inc(masked, 1)
                dve.wait_ge(masked, h + 1)

        att = Attention(ph, "bias", heads, ps, m.ident, scores, values,
                        lambda h: m.o[64 * (h % 2):64 * (h % 2) + 64, 4 + h // 2], bias=add_mask)
        att.bias_at = lambda u: bias[:, (u // TT) % 2, (6 - 2 * (u % TT)) * 64:(14 - 2 * (u % TT)) * 64]
        with nc.Block() as block:
            @block.sync
            def _(sp):
                sp.dma_start(mask[:], a["window"]).then_inc(mask_loaded, 16)
                for h in range(heads):
                    if h >= 2:
                        sp.wait_ge(att.biased, TT * (h - 1))
                    for parity in range(2):
                        sp.dma_start(bias[64 * parity:64 * parity + 64, h % 2].rearrange("p (r c) -> p r c", c=64),
                                     a["rpb"][h, :, 1 - parity:15 - parity]).then_inc(bias_loaded[h % 2], 16)

            @block.scalar
            def _(act):
                att.act(act)

            @block.vector
            def _(dve):
                att.dve(dve)

            @block.tensor
            def _(pe):
                att.pe(pe)


def spatial_gate(nc, m, a):
    with Phase(nc, "sgu") as ph:
        ps = ph.psum()
        ws, bs, lng = ph.sb("ws", [P, 8, P]), ph.sb("bs", [P, 4, P]), ph.sb("lng", [P, T])
        stats, mv, std = ph.sb("stats", [P, TT, 6]), ph.sb("mv", [P, TT, 2]), ph.sb("std", [P, TT])
        mixed = ph.sb("mixed", [P, 4, T])
        loaded, st, ag, root, inv, centered, normed, mix, biased, gated = (ph.sem(s) for s in (
            "loaded", "stats_done", "aggr", "root", "inverse", "centered", "normed", "mixed_s", "biased", "gated"))
        v = m.z[:, N_VS:N_VS + TT]
        with nc.Block() as block:
            @block.sync
            def _(sp):
                sp.dma_start(ws[:], a["sgu_w"]).then_inc(loaded, 16)
                sp.dma_start(bs[:], a["sgu_b"]).then_inc(loaded, 16)
                sp.dma_start(lng[:], a["sgu_ln"].broadcast_to([P, T])).then_inc(loaded, 16)
                sp.wait_ge(loaded, 48)

            @block.vector
            def _(dve):
                for t in range(TT):
                    dve.bn_stats(stats[:, t], v[:, t]).then_inc(st, 1)
                for t in range(TT):
                    dve.wait_ge(st, t + 1)
                    dve.bn_aggr(mv[:, t], stats[:, t]).then_inc(ag, 1)
                dve.wait_ge(root, 1)
                dve.reciprocal(std[:], std[:]).then_inc(inv, 1)
                dve.wait_ge(inv, 1)
                dve.wait_ge(loaded, 48)
                for t in range(TT):
                    dve.tensor_scalar(v[:, t], v[:, t], mv[:, t, 0:1], std[:, t:t + 1], ALU.subtract, ALU.mult)\
                       .then_inc(centered, 1)
                for t in range(TT):
                    dve.wait_ge(centered, t + 1)
                    dve.tensor_tensor(v[:, t], v[:, t], lng[:], ALU.mult).then_inc(normed, 1)
                for j in range(4):
                    dve.wait_ge(mix, j + 1)
                    dve.tensor_tensor(mixed[:, j].rearrange("p (n q) -> p n q", n=TT), ps[:, j].rearrange("p (n q) -> p n q", n=TT),
                                      bs[:, j:j + 1].broadcast_to([P, TT, P]), ALU.add).then_inc(biased, 1)
                for j in range(4):
                    dve.wait_ge(biased, j + 1)
                    dve.tensor_tensor(m.o[:, j], mixed[:, j], m.z[:, N_U + j], ALU.mult).then_inc(gated, 1)
                dve.wait_ge(gated, 4)

            @block.scalar
            def _(act):
                act.wait_ge(ag, TT)
                act.activation(std[:], mv[:, :, 1], ACT.Sqrt, bias=m.eps).then_inc(root, 1)

            @block.tensor
            def _(pe):
                pe.wait_ge(normed, TT)
                for j in range(4):
                    for h in (2 * j, 2 * j + 1):
                        r = slice(64 * (h % 2), 64 * (h % 2) + 64)
                        for t in range(TT):
                            mm = pe.matmul(ps[r, j, t * P:(t + 1) * P], v[:, t, 64 * h:64 * h + 64], ws[:, h],
                                           start=True, stop=True)
                    mm.then_inc(mix, 1)


def merge2(nc, m, a):
    with Phase(nc, "out2") as ph:
        ring = Ring(ph, False)
        ps = ph.psum()
        names = ("squares", "totals", "spread", "roots", "inverse", "y_done", "y_hi", "y_lo", "out_done", "out_added")
        s = {n: ph.sem(n) for n in names}
        z = m.z
        norm = Norm(ph, "n", m.x, z[:, 8:16], z[:, 16], z[:, 17], z[:, 0:8], m.hi, m.lo, ps[:, 7], m.ones, m.eps, T)
        w = a["w_out2"].rearrange("(k p) n -> p k n", p=P)
        of = lambda k: m.o[:, (k + 4) % 8]
        with nc.Block() as block:
            @block.sync
            def _(sp):
                ring.open(sp)
                for i in range(4):
                    ring.load(sp, i, i % 2, w[:, :, i * CW:(i + 1) * CW])

            @block.gpsimd
            def _(pool):
                for i in range(4):
                    ring.cut_lo(pool, i, i % 2)

            @block.scalar
            def _(act):
                for k in range(KD):
                    act.activation(z[:, 8 + k], of(k), ACT.Square).then_inc(s["squares"], 1)
                ring.cut_hi(act, 0, 16)
                ring.cut_hi(act, 1, 16)
                for g in range(2):
                    act.wait_ge(s["spread"], g + 1)
                    act.activation(z[:, 18 + g], ps[:, 5 + g], ACT.Sqrt, bias=m.eps, scale=1.0 / NA_W).then_inc(s["roots"], 1)
                for k in range(KD):
                    act.wait_ge(s["y_done"], k + 1)
                    act.activation(m.hi[:, k], z[:, k], ACT.Copy).then_inc(s["y_hi"], 1)
                for i in range(2, 4):
                    act.wait_ge(s["out_done"], 2 * (i - 1))
                    ring.cut_hi(act, i % 2, 32)
                act.wait_ge(s["out_added"], KD)
                norm.act_squares(act)
                norm.act_root(act)
                norm.act_hi(act)

            @block.vector
            def _(dve):
                for g in range(2):
                    dve.wait_ge(s["squares"], 4 * g + 4)
                    dve.tensor_reduce(z[:, 20 + g], z[:, 8 + 4 * g:12 + 4 * g].rearrange("p k t -> p t k"), AX.X, ALU.add)\
                       .then_inc(s["totals"], 1)
                for g in range(2):
                    dve.wait_ge(s["roots"], g + 1)
                    dve.reciprocal(z[:, 18 + g], z[:, 18 + g]).then_inc(s["inverse"], 1)
                    dve.wait_ge(s["inverse"], g + 1)
                    for k in range(4 * g, 4 * g + 4):
                        dve.scalar_tensor_tensor(z[:, k], of(k), m.vec2[:, 2 + k:3 + k], z[:, 18 + g], ALU.mult, ALU.mult)\
                           .then_inc(s["y_done"], 1)
                for k in range(KD):
                    dve.wait_ge(s["y_hi"], k + 1)
                    dve.tensor_tensor(m.lo[:, k], z[:, k], m.hi[:, k].bitcast(F32), ALU.subtract).then_inc(s["y_lo"], 1)
                for t in range(KD):
                    dve.wait_ge(s["out_done"], t + 1)
                    dve.scalar_tensor_tensor(m.x[:, t], ps[:, t % 4], m.mod[:, M_GA + t, 0:1], m.x[:, t], ALU.mult, ALU.add)\
                       .then_inc(s["out_added"], 1)
                norm.dve_total(dve)
                norm.dve_apply(dve, lambda k: m.mod[:, M_SCF + k, 0:1], lambda k: m.mod[:, M_SHF + k, 0:1])
                dve.wait_ge(norm.lo_cut, KD)

            @block.tensor
            def _(pe):
                for g in range(2):
                    pe.wait_ge(s["totals"], g + 1)
                    pe.matmul(ps[:, 5 + g], m.ones, z[:, 20 + g], start=True, stop=True).then_inc(s["spread"], 1)
                pe.wait_ge(s["y_lo"], KD)
                for t in range(KD):
                    i = t // 2
                    if t % 2 == 0:
                        ring.wait_cut(pe, i)
                    hi, lo = cols(ring.hi[:, i % 2], CW), cols(ring.lo[:, i % 2], CW)
                    cp = slice((t % 2) * P, (t % 2 + 1) * P)
                    if t >= 4:
                        pe.wait_ge(s["out_added"], t - 3)
                    product3(pe, ps[:, t % 4], lambda k: hi[:, k, cp], lambda k: lo[:, k, cp],
                             lambda k: m.hi[:, k], lambda k: m.lo[:, k], range(KD)).then_inc(s["out_done"], 1)
                norm.pe_spread(pe)


def route(nc, m, a):
    NG, NX = 4, 4
    with Phase(nc, "route") as ph:
        ps = ph.psum()
        wr, rb = ph.sb("wr", [P, KD, 20]), ph.sb("rb", [P, 20])
        lg = ph.sb("logits", [P, TT, 20])
        four = {n: ph.sb(n, [P, TT, 4]) for n in ("ge", "geq", "ghot", "le", "le2", "eq1", "eq2", "hot1", "hot2", "within")}
        one = {n: ph.sb(n, [P, TT, 1]) for n in ("gm", "gs", "ptop", "m1", "m2", "d", "den", "w1", "w2", "rem")}
        by = ph.sb("by", [P, TT, NG, NX])
        gate = ph.sb("gate", [P, TT, NE])
        gate_t = ph.sb("gate_t", [NE, T])
        loaded, logit, step, to_exp, exp_done, gates, turned, turned_out, spread, spread_out = (ph.sem(s) for s in (
            "loaded", "logit", "step", "to_exp", "exp_done", "gates", "turned", "turned_out", "spread", "spread_out"))
        with nc.Block() as block:
            @block.sync
            def _(sp):
                sp.dma_start(wr[:], a["w_route"].rearrange("(k p) n -> p k n", p=P)).then_inc(loaded, 16)
                sp.dma_start(rb[:], a["b_route"].broadcast_to([P, 20])).then_inc(loaded, 16)
                sp.wait_ge(loaded, 32)

            @block.tensor
            def _(pe):
                pe.wait_ge(loaded, 32)
                for t in range(TT):
                    for k in range(KD):
                        mm = pe.matmul(ps[:, 0, t * 32:t * 32 + 20], m.z[:, k, t * P:(t + 1) * P], wr[:, k],
                                       start=(k == 0), stop=(k == KD - 1))
                mm.then_inc(logit, 1)
                pe.wait_ge(gates, 1)
                for t in range(TT):
                    mm = pe.transpose(ps[0:NE, 1, t * P:(t + 1) * P], gate[:, t], m.ident)
                mm.then_inc(turned, 1)
                pe.wait_ge(turned_out, 1)
                for e in range(NE):
                    if e >= 4:
                        pe.wait_ge(spread_out, e - 3)
                    pe.matmul(ps[:, 2 + e % 4], m.ident[0:NE, e:e + 1].broadcast_to([NE, P]), gate_t[:],
                              start=True, stop=True).then_inc(spread, 1)

            @block.scalar
            def _(act):
                act.wait_ge(to_exp, 1)
                act.activation(four["ge"][:], four["ge"][:], ACT.Exp).then_inc(exp_done, 1)
                act.wait_ge(to_exp, 2)
                act.activation(one["d"][:], one["d"][:], ACT.Exp).then_inc(exp_done, 1)
                act.wait_ge(turned, 1)
                act.activation(gate_t[:], ps[0:NE, 1], ACT.Copy).then_inc(turned_out, 1)
                for e in range(NE):
                    act.wait_ge(spread, e + 1)
                    act.activation(m.z[:, e], ps[:, 2 + e % 4], ACT.Copy).then_inc(spread_out, 1)
                act.wait_ge(spread_out, NE)

            @block.vector
            def _(dve):
                link = linker(dve, step)

                def wide(x):
                    return x[:].broadcast_to([P, TT, 4])

                def first_hot(dst, eq):
                    rem = one["rem"]
                    link(dve.tensor_copy(dst[:, :, 0:1], eq[:, :, 0:1]))
                    link(dve.tensor_scalar(rem[:], eq[:, :, 0:1], -1.0, 1.0, ALU.mult, ALU.add))
                    for i in range(1, 4):
                        link(dve.tensor_tensor(dst[:, :, i:i + 1], eq[:, :, i:i + 1], rem[:], ALU.mult))
                        if i < 3:
                            link(dve.tensor_tensor(rem[:], rem[:], dst[:, :, i:i + 1], ALU.subtract))

                dve.wait_ge(logit, 1)
                dve.wait_ge(loaded, 32)
                link(dve.tensor_tensor(lg[:], ps[:, 0, 0:TT * 32].rearrange("p (t n) -> p t n", n=32)[:, :, 0:20],
                                       rb[:].rearrange("p (o n) -> p o n", o=1).broadcast_to([P, TT, 20]), ALU.add))
                link(dve.tensor_reduce(one["gm"][:], lg[:, :, 0:4], AX.X, ALU.max))
                dve.tensor_tensor(four["ge"][:], lg[:, :, 0:4], wide(one["gm"]), ALU.subtract).then_inc(to_exp, 1)
                link(dve.tensor_tensor(four["geq"][:], lg[:, :, 0:4], wide(one["gm"]), ALU.is_equal))
                first_hot(four["ghot"], four["geq"])
                dve.wait_ge(exp_done, 1)
                link(dve.tensor_reduce(one["gs"][:], four["ge"][:], AX.X, ALU.add))
                link(dve.reciprocal(one["ptop"][:], one["gs"][:]))
                hot_g = four["ghot"][:].rearrange("p t (g o) -> p t g o", o=1).broadcast_to([P, TT, NG, NX])
                for t in range(TT):
                    ins = dve.tensor_tensor(by[:, t], lg[:, t, 4:20].rearrange("p (g x) -> p g x", g=NG), hot_g[:, t], ALU.mult)
                link(ins)
                for t in range(TT):
                    ins = dve.tensor_reduce(four["le"][:, t], by[:, t].rearrange("p g x -> p x g"), AX.X, ALU.add)
                link(ins)
                link(dve.tensor_reduce(one["m1"][:], four["le"][:], AX.X, ALU.max))
                link(dve.tensor_tensor(four["eq1"][:], four["le"][:], wide(one["m1"]), ALU.is_equal))
                first_hot(four["hot1"], four["eq1"])
                link(dve.scalar_tensor_tensor(four["le2"][:], four["hot1"][:], NEG, four["le"][:], ALU.mult, ALU.add))
                link(dve.tensor_reduce(one["m2"][:], four["le2"][:], AX.X, ALU.max))
                link(dve.tensor_tensor(four["eq2"][:], four["le2"][:], wide(one["m2"]), ALU.is_equal))
                dve.tensor_tensor(one["d"][:], one["m2"][:], one["m1"][:], ALU.subtract).then_inc(to_exp, 1)
                first_hot(four["hot2"], four["eq2"])
                dve.wait_ge(exp_done, 2)
                link(dve.tensor_scalar(one["den"][:], one["d"][:], 1.0, None, ALU.add))
                link(dve.reciprocal(one["w1"][:], one["den"][:]))
                link(dve.tensor_tensor(one["w1"][:], one["w1"][:], one["ptop"][:], ALU.mult))
                link(dve.tensor_tensor(one["w2"][:], one["w1"][:], one["d"][:], ALU.mult))
                link(dve.tensor_tensor(four["hot1"][:], four["hot1"][:], wide(one["w1"]), ALU.mult))
                link(dve.tensor_tensor(four["hot2"][:], four["hot2"][:], wide(one["w2"]), ALU.mult))
                link(dve.tensor_tensor(four["within"][:], four["hot1"][:], four["hot2"][:], ALU.add))
                within = four["within"][:].rearrange("p t (o x) -> p t o x", o=1).broadcast_to([P, TT, NG, NX])
                for t in range(TT):
                    ins = dve.tensor_tensor(gate[:, t].rearrange("p (g x) -> p g x", g=NG), within[:, t], hot_g[:, t], ALU.mult)
                ins.then_inc(gates, 1)


def experts(nc, m, a):
    with Phase(nc, "moe") as ph:
        ring = Ring(ph, True)
        ps = ph.psum()
        hidden = ph.sb("hid_hi", [P, 2, T], F32R), ph.sb("hid_lo", [P, 2, T], F32R)
        ex = Experts(ph, m, ring, ps, MOE_STEPS, 0, 0, hidden, subs=DE // CW,
                     gate_tile=lambda e: m.z[:, bass.ds(e, 1)].rearrange("p o t -> p (o t)"),
                     factor=lambda c: m.mod[:, M_GF + c, 0:1])
        w1 = a["w1"].rearrange("e (k p) n -> e p k n", p=P)
        w3 = a["w3"].rearrange("e (k p) n -> e p k n", p=P)
        w2 = a["w2"].rearrange("e (s k p) n -> e s p k n", p=P, k=2)
        with nc.Block() as block:
            @block.sync
            def _(sp):
                ring.open(sp)
                ex.open(sp)
                ex.sp(sp, lambda e, s: w1[e, :, :, s * CW:(s + 1) * CW], lambda e, s: w3[e, :, :, s * CW:(s + 1) * CW],
                      lambda e, s: w2[e, s])

            @block.gpsimd
            def _(pool):
                ex.pool(pool)

            @block.scalar
            def _(act):
                ex.act(act)

            @block.vector
            def _(dve):
                ex.dve(dve)

            @block.tensor
            def _(pe):
                ex.pe(pe)


def store(nc, m, out):
    with Phase(nc, "store") as ph:
        stored = ph.sem("stored")
        with nc.Block() as block:
            @block.sync
            def _(sp):
                sp.dma_start(out.rearrange("(k p) t -> p k t", p=P), m.x[:]).then_inc(stored, 16)
                sp.wait_ge(stored, 16)


def second_block(nc, m, a):
    modulation(nc, m, a)
    project2(nc, m, a)
    na_prepare(nc, m, a)
    na_attend(nc, m, a)
    spatial_gate(nc, m, a)
    merge2(nc, m, a)
    route(nc, m, a)
    experts(nc, m, a)


class Memory:

    def __init__(self, nc, stack):
        def sb(name, shape, dt=F32):
            return stack.enter_context(nc.sbuf_tensor(name, shape, dt))

        self.x = sb("x", [P, KD, T])
        self.hi, self.lo = sb("h_hi", [P, KD, T], F32R), sb("h_lo", [P, KD, T], F32R)
        self.o = sb("o", [P, 2 * NB, T])
        self.z = sb("z", [P, ZT, T])
        self.mats = sb("mats", [P, 5 * P + KRW])
        self.rope = sb("rope", [P, 4, T])
        self.small = sb("small", [P, 6])
        self.gains, self.g = sb("gains", [P, 2, G_N]), sb("g", [P, G_N])
        self.lam, self.lamv = sb("lam", [P, 256]), sb("lamv", [P, 128])
        self.lb, self.lbl, self.laminit = sb("lb", [P, 2, 2, 2]), sb("lbl", [P, 4]), sb("laminit", [P, 2])
        self.ones, self.ident, self.ones32, self.ones64, self.rot32 = (
            self.mats[:, i * P:(i + 1) * P] for i in range(5))
        self.rot96 = self.mats[0:KRW, 5 * P:5 * P + KRW]
        self.eps = self.small[:, 4:5]
        self.mod = sb("mod", [P, MODS, 2])
        self.vec2 = sb("vec2", [P, 10])


class MixerMemory:
    def __init__(self, nc, stack, name, mla):
        def sb(n, shape):
            return stack.enter_context(nc.sbuf_tensor(f"{name}_{n}", shape, F32))

        self.gqt = sb("gq", [P, 2])
        self.gq = self.gqt[0:96, 0:1] if mla else self.gqt[:, 0:1]
        self.gsub = self.gqt[:, 1:2]
        if mla:
            self.raw, self.qk, self.v = sb("raw", [96, 8, T]), sb("qk", [96, 8, T]), sb("v", [P, TT, BW])
        else:
            self.qk = sb("qk", [P, 4, T])
            self.lam2, self.lamt = sb("lam2", [P, 2]), sb("lamt", [P, 2])
        self.od = sb("od", [P, 2, T])


def first_block(nc, m, a, layers=2):
    with nc.Fori(0, layers) as l:
        project(nc, m, a, l)
        with ExitStack() as stack:
            mem = MixerMemory(nc, stack, "mla", True)
            mla_prepare(nc, m, a, l, mem)
            mla_attend(nc, m, mem)
        with ExitStack() as stack:
            mem = MixerMemory(nc, stack, "diff", False)
            diff_prepare(nc, m, mem)
            diff_attend(nc, m, mem)
            head_norm(nc, m, "difn", mem.od, mem.gsub, m.o[:, 4:6])
            fnet(nc, m, a)
        with ExitStack() as stack:
            od = stack.enter_context(nc.sbuf_tensor("hgrn_od", [P, 2, T], F32))
            hgrn(nc, m, a, od)
            head_norm(nc, m, "hgrnn", od, m.g[:, G_ON:G_ON + 1], m.o[:, 6:8], m.z[:, Z_HG:Z_HG + 2])
        merge_and_ffn(nc, m, a, l)

def feature_columns(np, v):
    v = np.asarray(v)
    return np.moveaxis(v.reshape(v.shape[:-1] + (v.shape[-1] // 128, 128)), -1, 0)


def repeated(np, v):
    v = np.asarray(v)
    return np.moveaxis(np.stack([np.resize(r, 128) for r in v]), -1, 0)[:, :, None]


def constants(np):
    eye = np.eye(128)
    blocks = lambda n: np.kron(np.eye(128 // n), np.ones((n, n)))

    def rotation(size, starts, half):
        r = np.zeros((size, size))
        for s in starts:
            for i in range(half):
                r[s + half + i, s + i] = -1.0
                r[s + i, s + half + i] = 1.0
        return r

    rot96 = np.zeros((128, 96))
    rot96[:96] = rotation(96, [64], 16)
    mats = np.concatenate([np.ones((128, 128)), eye, blocks(32), blocks(64), rotation(128, [0, 32, 64, 96], 16), rot96], 1)
    inv = (1.0 / (np.float32(10000.0) ** (np.arange(0, 32, 2, dtype=np.float32) / np.float32(32)))).astype(np.float32)
    ang = (np.arange(512, dtype=np.float32)[None, :] * inv[:, None]).astype(np.float32)
    cos, sin = np.cos(ang.astype(np.float64)), np.sin(ang.astype(np.float64))
    rope = np.zeros((128, 4, 512))
    rope[:64, 0] = 1.0
    rope[64:96, 0], rope[64:96, 1] = np.tile(cos, (2, 1)), np.tile(sin, (2, 1))
    rope[:, 2], rope[:, 3] = np.tile(cos, (8, 1)), np.tile(sin, (8, 1))
    small = np.zeros((128, 6))
    for l in range(2):
        init = 0.8 - 0.6 * np.exp(-0.3 * l)
        small[:, 2 * l], small[:, 2 * l + 1] = init, 1.0 - init
    small[:, 4] = 1e-6
    t = np.arange(512)
    phase = 2 * np.pi * (np.outer(t, t) % 512) / 512
    dft = np.stack([np.cos(phase), np.sin(phase)]) / np.sqrt(512)
    dft = dft.reshape(2, 4, 128, 512).transpose(2, 0, 1, 3)
    c = np.arange(64)
    p64 = 2 * np.pi * (np.outer(c, c) % 64) / 64
    dft64 = np.concatenate([np.kron(np.eye(2), np.cos(p64)), np.kron(np.eye(2), -np.sin(p64))], 1) / 8
    s, q = np.arange(128)[:, None], np.arange(128)[None, :]
    masks = [((s // (2 * b) == q // (2 * b)) & (s // b != q // b)) for b in (64, 32, 16, 8, 4, 2, 1)] + [s == q]
    masks = np.stack(masks, 1)
    reset = np.tile((np.arange(512) % 128 != 0)[None], (128, 1))
    c, kc = np.arange(128)[:, None] % 64, np.arange(64)[None, :]
    start = np.clip(c - 8, 0, 48)
    window = np.where((kc >= start) & (kc < start + 16), 0.0, -1.0e30)
    return {k: np.ascontiguousarray(v, dtype=np.float32) for k, v in dict(
        window=window, mats=mats, rope=rope, small=small, dft=dft, dft64=dft64, masks=masks, reset=reset).items()}


def lay_out_first(np, i):
    fc = lambda n: feature_columns(np, i[n])
    rep = lambda n: repeated(np, i[n])
    gains = np.concatenate([fc("ln_mix"), fc("mla_g_qa"), fc("mla_g_kva"), rep("mla_g_qn"), rep("mla_g_kn"),
                            rep("diff_g_qn"), rep("diff_g_kn"), rep("diff_g_sub"), rep("hgrn_g_on"), fc("ln_ffn")], -1)
    lb = np.asarray(i["hgrn_lb_logits"]).reshape(2, 2, 2, 128)
    out = dict(xT=np.asarray(i["x"])[0].T, gains=gains,
               lam=np.stack([np.asarray(i[n]) for n in ("diff_lq1", "diff_lk1", "diff_lq2", "diff_lk2")], 1),
               lb_logits=lb.transpose(3, 0, 1, 2),
               w_in=i["w_in"], w_uq=i["mla_w_uq"], w_ukv=i["mla_w_ukv"], w_branch=i["w_branch"], w_out=i["w_out"],
               w_gate_up=i["w_gate_up"], w_down=i["w_down"])
    return {k: np.ascontiguousarray(v) for k, v in out.items()}


def lay_out_second(np, i):
    fc = lambda v: feature_columns(np, v)
    g = {n: np.asarray(i[n + "_2"])[0] for n in (
        "w_ada", "b_ada", "w_in", "q_gain", "k_gain", "rpb", "sgu_ln", "sgu_w", "sgu_b", "out_gain", "w_out", "rg_w",
        "rg_b", "re_w", "re_b", "w1", "w3", "w2")}
    cond = np.stack([fc(np.asarray(i["c_2"])[0]), fc(np.asarray(i["c_ctx_2"]))], -1)
    col = np.arange(64)
    rpb = g["rpb"][:, :, np.clip(col[None, :] - col[:, None] + 15, 0, 30)].transpose(0, 2, 1, 3)
    out = dict(cond=cond, b_ada=fc(g["b_ada"]), w_ada=g["w_ada"], ctxT=np.asarray(i["ctx_2"])[0].T, w_in2=g["w_in"],
               vec2=np.concatenate([np.resize(g["q_gain"], 128)[:, None], np.resize(g["k_gain"], 128)[:, None],
                                    fc(g["out_gain"])], 1),
               rpb=rpb, sgu_ln=g["sgu_ln"][None], sgu_w=g["sgu_w"].transpose(2, 0, 1),
               sgu_b=np.repeat(g["sgu_b"].reshape(4, 2, 128), 64, axis=1).transpose(1, 0, 2), w_out2=g["w_out"],
               w_route=np.concatenate([g["rg_w"], g["re_w"].transpose(1, 0, 2).reshape(1024, 16)], 1),
               b_route=np.concatenate([g["rg_b"], g["re_b"].reshape(-1)])[None],
               w1=g["w1"], w3=g["w3"], w2=g["w2"])
    return {k: np.ascontiguousarray(v) for k, v in out.items()}


def program(nc, a, out):
    with ExitStack() as stack:
        m = Memory(nc, stack)
        load_constants(nc, m, a)
        first_block(nc, m, a)
        second_block(nc, m, a)
        store(nc, m, out)


def kernel(**inputs):
    import numpy as np
    import concourse.bacc as bacc
    from concourse.bass_utils import run_bass_kernel_spmd

    nc = bacc.Bacc("TRN2", target_bir_lowering=False, num_devices=1)
    arrays, a = {}, {}
    for name, x in {**lay_out_first(np, inputs), **lay_out_second(np, inputs), **constants(np)}.items():
        arrays[f"in_{name}"] = x
        a[name] = nc.dram_tensor(f"in_{name}", x.shape, mybir.dt.from_np(x.dtype), kind="ExternalInput").ap()
    out = nc.dram_tensor("out_xT", (D, T), F32, kind="ExternalOutput").ap()
    program(nc, a, out)
    r = run_bass_kernel_spmd(nc, [arrays], core_ids=[0])
    return np.ascontiguousarray(r.results[0]["out_xT"].T)[None]
```

```python
from contextlib import ExitStack

import concourse.bass as bass
from concourse import mybir

ALU = mybir.AluOpType
ACT = mybir.ActivationFunctionType
AX = mybir.AxisListType
F32 = mybir.dt.float32
F32R = mybir.dt.float32r
I32 = mybir.dt.int32

P = 128
T = 512
TT = T // P
D = 1024
KD = D // P
EPS = 1e-6
CW = 256
CHUNK = KD * CW
RING = 2
BW = 256
NB = 4
DFF = 2816
FF_STEPS = DFF // CW
NE, DE = 16, 512
OVER = (2 * T - 1) // P
SLOTS = NE + OVER
CTX = 256
CT = CTX // P
NEG = -1.0e30

C_FU, C_DQ, C_DK, C_DV, C_HQ, C_HV, C_HF, C_HB, C_HG, C_GATE = (
    544, 800, 1056, 1312, 1568, 1824, 2080, 2336, 2592, 2848)
C_KR = 448
KRW = 96
Z_CQ, Z_CKV, Z_FU, Z_DQ, Z_DK, Z_HQ, Z_HF, Z_HB, Z_HG = 0, 3, 4, 6, 8, 10, 12, 14, 16
Z_KR, Z_DV, Z_HV = 18, 19, 21
ZT = 23

G_MIX, G_QA, G_KVA, G_MQ, G_MK, G_DQ, G_DK, G_SUB, G_ON, G_FFN, G_N = 0, 8, 11, 12, 13, 14, 15, 16, 17, 18, 26

LEVELS = (64, 32, 16, 8, 4, 2, 1)


class Phase:

    def __init__(self, nc, name):
        self.nc, self.name, self.stack, self.sems = nc, name, ExitStack(), []

    def __enter__(self):
        return self

    def sem(self, name):
        s = self.stack.enter_context(self.nc.semaphore(f"{self.name}_{name}"))
        self.sems.append(s)
        return s

    def sb(self, name, shape, dt=F32):
        return self.stack.enter_context(self.nc.sbuf_tensor(f"{self.name}_{name}", shape, dt))

    def psum(self):
        return self.stack.enter_context(self.nc.psum_tensor(f"{self.name}_ps", [P, 8, 512], F32))

    def __exit__(self, *error):
        if error[0] is None:
            self.nc.all_engine_barrier()
            for s in self.sems:
                self.nc.sync.sem_clear(s)
            self.nc.all_engine_barrier()
        self.stack.close()


def linker(eng, sem):
    count = [0]

    def link(instruction):
        count[0] += 1
        instruction.then_inc(sem, 1)
        eng.wait_ge(sem, count[0])

    return link


def cols(tensor, n, k=KD):
    return tensor[:, 0:k * n].rearrange("p (k n) -> p k n", k=k)


class Ring:

    def __init__(self, ph, wide):
        self.raw = ph.sb("raw", [P, RING, CHUNK])
        self.hi = ph.sb("whi", [P, RING, CHUNK], F32R)
        self.lo = ph.sb("wlo", [P, RING, CHUNK], F32R)
        self.raw_ready = [ph.sem(f"raw_ready{i}") for i in range(RING)]
        self.hi_done, self.lo_done = ph.sem("hi_done"), ph.sem("lo_done")
        self.wide_lo = None
        if wide:
            self.wraw = ph.sb("wide_raw", [P, CHUNK])
            self.whi = ph.sb("wide_hi", [P, CHUNK], F32R)
            self.wlo = ph.sb("wide_lo", [P, CHUNK], F32R)
            self.wide_ready, self.wide_hi, self.wide_lo = (
                ph.sem("wide_ready"), ph.sem("wide_hi_done"), ph.sem("wide_lo_done"))

    def open(self, sp):
        sp.sem_inc(self.lo_done, RING)
        if self.wide_lo:
            sp.sem_inc(self.wide_lo, 1)

    def load(self, sp, c, slot, src, n=CW, k=KD):
        sp.wait_ge(self.lo_done, c + 1)
        sp.dma_start(cols(self.raw[:, slot], n, k), src).then_inc(self.raw_ready[slot], 16)

    def cut_hi(self, act, slot, arrived, n=CHUNK):
        act.wait_ge(self.raw_ready[slot], arrived)
        act.activation(self.hi[:, slot, 0:n], self.raw[:, slot, 0:n], ACT.Copy).then_inc(self.hi_done, 1)

    def cut_lo(self, eng, c, slot, n=CHUNK):
        eng.wait_ge(self.hi_done, c + 1)
        eng.tensor_tensor(self.lo[:, slot, 0:n], self.raw[:, slot, 0:n],
                          self.hi[:, slot, 0:n].bitcast(F32), ALU.subtract).then_inc(self.lo_done, 1)

    def wait_cut(self, pe, c):
        pe.wait_ge(self.lo_done, RING + c + 1)

    def load_wide(self, sp, w, src):
        sp.wait_ge(self.wide_lo, w + 1)
        sp.dma_start(cols(self.wraw, D, 2), src).then_inc(self.wide_ready, 16)

    def cut_wide_hi(self, act, w):
        act.wait_ge(self.wide_ready, 16 * w + 16)
        act.activation(self.whi[:], self.wraw[:], ACT.Copy).then_inc(self.wide_hi, 1)

    def cut_wide_lo(self, eng, w):
        eng.wait_ge(self.wide_hi, w + 1)
        eng.tensor_tensor(self.wlo[:], self.wraw[:], self.whi[:].bitcast(F32), ALU.subtract)\
           .then_inc(self.wide_lo, 1)


def product3(pe, out, whi, wlo, xhi, xlo, ks, start=True, stop=True):
    parts = ((whi, xhi), (whi, xlo), (wlo, xhi))
    mm = None
    for n, (w, x) in enumerate(parts):
        for i, k in enumerate(ks):
            mm = pe.matmul(out, w(k), x(k), start=start and n == 0 and i == 0,
                           stop=stop and n == 2 and i == len(ks) - 1)
    return mm


class Norm:

    def __init__(self, ph, name, src, sq, total, root, h, hi, lo, bank, ones, eps, width):
        self.src, self.sq, self.total, self.root, self.h, self.hi = src, sq, total, root, h, hi
        self.lo, self.bank, self.ones, self.eps, self.width = lo, bank, ones, eps, width
        (self.squares, self.totals, self.spread, self.roots, self.inverse, self.scaled,
         self.h_done, self.hi_cut, self.lo_cut) = (
            ph.sem(f"{name}_{s}") for s in ("squares", "totals", "spread", "roots", "inverse", "scaled", "h_done", "hi_cut", "lo_cut"))

    def act_squares(self, act):
        for k in range(KD):
            act.activation(self.sq[:, k], self.src[:, k], ACT.Square).then_inc(self.squares, 1)

    def dve_total(self, dve):
        dve.wait_ge(self.squares, KD)
        dve.tensor_reduce(self.total, self.sq.rearrange("p k t -> p t k"), AX.X, ALU.add)\
           .then_inc(self.totals, 1)

    def pe_spread(self, pe):
        pe.wait_ge(self.totals, 1)
        pe.matmul(self.bank, self.ones, self.total, start=True, stop=True).then_inc(self.spread, 1)

    def act_root(self, act):
        act.wait_ge(self.spread, 1)
        act.activation(self.root, self.bank, ACT.Sqrt, bias=self.eps, scale=1.0 / D).then_inc(self.roots, 1)

    def dve_apply(self, dve, gain, shift=None, cut=True):
        dve.wait_ge(self.roots, 1)
        dve.reciprocal(self.root, self.root).then_inc(self.inverse, 1)
        dve.wait_ge(self.inverse, 1)
        for k in range(KD):
            ins = dve.scalar_tensor_tensor(self.h[:, k], self.src[:, k], gain(k), self.root,
                                           ALU.mult, ALU.mult)
            if shift is None:
                ins.then_inc(self.h_done, 1)
            else:
                ins.then_inc(self.scaled, 1)
        if shift is not None:
            for k in range(KD):
                dve.wait_ge(self.scaled, k + 1)
                dve.tensor_scalar(self.h[:, k], self.h[:, k], shift(k), None, ALU.add).then_inc(self.h_done, 1)
        for k in range(KD if cut else 0):
            dve.wait_ge(self.hi_cut, k + 1)
            dve.tensor_tensor(self.lo[:, k], self.h[:, k], self.hi[:, k].bitcast(F32), ALU.subtract)\
               .then_inc(self.lo_cut, 1)

    def act_hi(self, act):
        for k in range(KD):
            act.wait_ge(self.h_done, k + 1)
            act.activation(self.hi[:, k], self.h[:, k], ACT.Copy).then_inc(self.hi_cut, 1)


def load_constants(nc, m, a):
    with Phase(nc, "consts") as ph:
        loaded, x_loaded, made, step, astep = (ph.sem(s) for s in ("loaded", "x_loaded", "made", "step", "astep"))
        logits = ph.sb("logits", [P, 2, 2, 2])
        e, r = ph.sb("e", [P, 2, 2, 2]), ph.sb("r", [P, 4, 2, 2])
        with nc.Block() as block:
            @block.sync
            def _(sp):
                sp.dma_start(logits[:], a["lb_logits"]).then_inc(loaded, 16)
                sp.dma_start(m.gains[:], a["gains"]).then_inc(loaded, 16)
                sp.dma_start(m.lam[:], a["lam"].rearrange("l f d -> (l f d)").rearrange("(o n) -> o n", o=1)
                             .broadcast_to([P, 2 * 4 * 32])).then_inc(loaded, 16)
                sp.dma_start(m.mats[:], a["mats"]).then_inc(loaded, 16)
                sp.dma_start(m.rope[:], a["rope"]).then_inc(loaded, 16)
                sp.dma_start(m.small[:], a["small"]).then_inc(loaded, 16)
                sp.dma_start(m.vec2[:], a["vec2"]).then_inc(loaded, 16)
                sp.dma_start(m.x[:], a["xT"].rearrange("(k p) t -> p k t", p=P)).then_inc(x_loaded, 16)
                sp.wait_ge(loaded, 112)
                sp.wait_ge(x_loaded, 16)

            @block.vector
            def _(dve):
                link = linker(dve, step)
                dve.wait_ge(loaded, 112)
                link(dve.tensor_tensor(r[:, 0], logits[:, :, 0], logits[:, :, 1], ALU.max))
                link(dve.tensor_tensor(e[:, :, 0], logits[:, :, 0], r[:, 0], ALU.subtract))
                link(dve.tensor_tensor(e[:, :, 1], logits[:, :, 1], r[:, 0], ALU.subtract))
                dve.tensor_copy(r[:, 3], r[:, 0]).then_inc(made, 1)
                dve.wait_ge(astep, 1)
                link(dve.tensor_tensor(r[:, 1], e[:, :, 0], e[:, :, 1], ALU.add))
                link(dve.reciprocal(r[:, 2], r[:, 1]))
                link(dve.tensor_tensor(e[:, :, 0], e[:, :, 0], r[:, 2], ALU.mult))
                link(dve.tensor_tensor(e[:, :, 1], e[:, :, 1], r[:, 2], ALU.mult))
                link(dve.tensor_tensor(m.lb[:, 0], e[:, :, 0], e[:, :, 0], ALU.subtract))
                link(dve.tensor_tensor(r[:, 3], e[:, :, 0], e[:, :, 1], ALU.add))
                link(dve.tensor_tensor(m.lb[:, 1], r[:, 3], e[:, :, 0], ALU.subtract))

            @block.scalar
            def _(act):
                act.wait_ge(made, 1)
                act.activation(e[:], e[:], ACT.Exp).then_inc(astep, 1)
                act.wait_ge(astep, 1)


def project(nc, m, a, l):
    plan = [(0, CW, "feature", (0, 1)), (CW, CW, "feature", (2, 3)), (C_KR, KRW, "rope", (Z_KR,))]
    for col, z in ((C_FU, Z_FU), (C_DQ, Z_DQ), (C_DK, Z_DK), (C_HQ, Z_HQ), (C_HF, Z_HF), (C_HB, Z_HB), (C_HG, Z_HG)):
        plan.append((col, CW, "feature", (z, z + 1)))
    plan += [(C_DV, CW, "token", (Z_DV,)), (C_HV, CW, "token", (Z_HV,))]
    tiles = []
    for c, (_, _, kind, _) in enumerate(plan):
        tiles += [(c, i) for i in range({"feature": 2, "rope": 1, "token": TT}[kind])]
    with Phase(nc, "proj") as ph:
        ring = Ring(ph, False)
        ps = ph.psum()
        tile_done, evicted, layer = (ph.sem(s) for s in ("tile_done", "evicted", "layer_gains"))
        z = m.z
        norm = Norm(ph, "n", m.x, z[:, 8:16], z[:, 16], z[:, 17], z[:, 0:8], m.hi, m.lo, ps[:, 7],
                    m.ones, m.eps, T)
        w = a["w_in"][l].rearrange("(k p) n -> p k n", p=P)
        with nc.Block() as block:
            @block.sync
            def _(sp):
                ring.open(sp)
                for c, (col, n, _, _) in enumerate(plan):
                    ring.load(sp, c, c % RING, w[:, :, col:col + n], n)

            @block.gpsimd
            def _(pool):
                for c, (_, n, _, _) in enumerate(plan):
                    ring.cut_lo(pool, c, c % RING, KD * n)

            @block.vector
            def _(dve):
                dve.tensor_copy(m.g[:], m.gains[:, bass.ds(l, 1), :].rearrange("p o g -> p (o g)")).then_inc(layer, 1)
                dve.tensor_copy(m.lbl[:], m.lb[:, bass.ds(l, 1)].rearrange("p o d t -> p (o d t)")).then_inc(layer, 1)
                dve.tensor_copy(m.lamv[:], m.lam[:, bass.ds(l * 128, 128)]).then_inc(layer, 1)
                dve.tensor_copy(m.laminit[:], m.small[:, bass.ds(l * 2, 2)]).then_inc(layer, 1)
                norm.dve_total(dve)
                dve.wait_ge(layer, 4)
                norm.dve_apply(dve, lambda k: m.g[:, G_MIX + k:G_MIX + k + 1])

            @block.scalar
            def _(act):
                def cut(c):
                    if c < len(plan):
                        if c >= RING:
                            act.wait_ge(tile_done, max(i for i, t in enumerate(tiles) if t[0] == c - RING) + 1)
                        ring.cut_hi(act, c % RING, 16 * (c // RING + 1), KD * plan[c][1])

                norm.act_squares(act)
                cut(0)
                cut(1)
                norm.act_root(act)
                norm.act_hi(act)
                for i, (c, part) in enumerate(tiles):
                    if part == 0 and c:
                        cut(c + 1)
                    kind, dst = plan[c][2:]
                    bank = ps[:, i % 6]
                    act.wait_ge(tile_done, i + 1)
                    if kind == "feature":
                        ins = act.activation(z[:, dst[part]], bank, ACT.Copy)
                    elif kind == "rope":
                        ins = act.activation(z[0:KRW, dst[0]], bank[0:KRW], ACT.Copy)
                    else:
                        half = z[:, dst[0] + part // 2, (part % 2) * BW:(part % 2 + 1) * BW]
                        ins = act.activation(half, bank[:, 0:BW], ACT.Copy)
                    ins.then_inc(evicted, 1)
                act.wait_ge(evicted, len(tiles))

            @block.tensor
            def _(pe):
                norm.pe_spread(pe)
                pe.wait_ge(norm.lo_cut, KD)
                for i, (c, part) in enumerate(tiles):
                    _, n, kind, _ = plan[c]
                    hi, lo = cols(ring.hi[:, c % RING], n), cols(ring.lo[:, c % RING], n)
                    if part == 0:
                        ring.wait_cut(pe, c)
                    if i >= 6:
                        pe.wait_ge(evicted, i - 5)
                    bank = ps[:, i % 6]
                    if kind == "feature":
                        at = slice(part * P, (part + 1) * P)
                        mm = product3(pe, bank, lambda k: hi[:, k, at], lambda k: lo[:, k, at],
                                      lambda k: m.hi[:, k], lambda k: m.lo[:, k], range(KD))
                    elif kind == "rope":
                        mm = product3(pe, bank[0:KRW], lambda k: hi[:, k], lambda k: lo[:, k],
                                      lambda k: m.hi[:, k], lambda k: m.lo[:, k], range(KD))
                    else:
                        at = slice(part * P, (part + 1) * P)
                        mm = product3(pe, bank[:, 0:BW], lambda k: m.hi[:, k, at], lambda k: m.lo[:, k, at],
                                      lambda k: hi[:, k], lambda k: lo[:, k], range(KD))
                    mm.then_inc(tile_done, 1)


class GroupNorm:

    def __init__(self, ph, name, units, parts, size, ones, eps, ps, sq, rt, rope=None, width=T):
        self.units, self.parts, self.size, self.ones, self.eps, self.ps = units, parts, size, ones, eps, ps
        self.sq, self.rt, self.rope, self.width = sq, rt, rope, width
        self.step = ph.sb(f"{name}_newton", [P, T])
        (self.squares, self.spread, self.roots, self.inverse, self.refined, self.normed,
         self.rotated, self.with_cos, self.with_sin, self.done) = (
            ph.sem(f"{name}_{s}") for s in ("squares", "spread", "roots", "inverse", "refined", "normed", "rotated", "with_cos", "with_sin", "done"))

    def act(self, act):
        n, w = self.parts, self.width
        for i, (src, _, _) in enumerate(self.units):
            act.activation(self.sq[0:n, i, 0:w], src, ACT.Square).then_inc(self.squares, 1)
        for i in range(len(self.units)):
            act.wait_ge(self.spread, i + 1)
            act.activation(self.rt[0:n, i, 0:w], self.ps[0:n, i % 4, 0:w], ACT.Sqrt, bias=self.eps[0:n],
                           scale=1.0 / self.size).then_inc(self.roots, 1)

    def pe(self, pe):
        n, w = self.parts, self.width
        for i in range(len(self.units)):
            pe.wait_ge(self.squares, i + 1)
            if i >= 4:
                pe.wait_ge(self.normed, i - 3)
            pe.matmul(self.ps[0:n, i % 4, 0:w], self.ones, self.sq[0:n, i, 0:w], start=True, stop=True)\
              .then_inc(self.spread, 1)
        if self.rope:
            for i in range(len(self.units)):
                pe.wait_ge(self.normed, i + 1)
                if i >= 4:
                    pe.wait_ge(self.with_sin, i - 3)
                pe.matmul(self.ps[0:n, 4 + i % 4, 0:w], self.rope[2], self.sq[0:n, i, 0:w],
                          start=True, stop=True).then_inc(self.rotated, 1)

    def dve(self, dve):
        n, w = self.parts, self.width
        link = linker(dve, self.refined)
        for i, (src, gain, dst) in enumerate(self.units):
            dve.wait_ge(self.roots, i + 1)
            dve.reciprocal(self.rt[0:n, i, 0:w], self.rt[0:n, i, 0:w]).then_inc(self.inverse, 1)
            dve.wait_ge(self.inverse, i + 1)
            r, total, step = self.rt[0:n, i, 0:w], self.ps[0:n, i % 4, 0:w], self.step[0:n, 0:w]
            link(dve.tensor_tensor(step, r, r, ALU.mult))
            link(dve.scalar_tensor_tensor(step, total, 1.0 / self.size, step, ALU.mult, ALU.mult))
            link(dve.tensor_scalar(step, step, -0.5, 1.5, ALU.mult, ALU.add))
            link(dve.tensor_tensor(r, r, step, ALU.mult))
            to = self.sq[0:n, i, 0:w] if self.rope else dst
            dve.scalar_tensor_tensor(to, src, gain, self.rt[0:n, i, 0:w], ALU.mult, ALU.mult)\
               .then_inc(self.normed, 1)
        if not self.rope:
            return
        for i, (_, _, dst) in enumerate(self.units):
            dve.wait_ge(self.normed, i + 1)
            dve.tensor_tensor(dst, self.sq[0:n, i, 0:w], self.rope[0], ALU.mult).then_inc(self.with_cos, 1)
            dve.wait_ge(self.rotated, i + 1)
            dve.tensor_tensor(self.rt[0:n, i, 0:w], self.ps[0:n, 4 + i % 4, 0:w], self.rope[1], ALU.mult)\
               .then_inc(self.with_sin, 1)
            dve.wait_ge(self.with_cos, i + 1)
            dve.wait_ge(self.with_sin, i + 1)
            dve.tensor_tensor(dst, dst, self.rt[0:n, i, 0:w], ALU.add).then_inc(self.done, 1)


class Attention:

    def __init__(self, ph, kind, heads, ps, ident, scores, values, out, neglam=None, bias=None):
        self.kind, self.heads, self.ps, self.ident = kind, heads, ps, ident
        self.scores, self.values, self.out, self.neglam, self.bias = scores, values, out, neglam, bias
        self.nk = 6 if kind == "bias" else 4
        self.maps = 2 if kind == "diff" else 1
        self.t_slots = 1 if kind == "bias" else 2
        self.prob = ph.sb("prob", [P, 2, self.maps, self.nk * P])
        self.probT = ph.sb("probT", [P, 2, self.nk, T])
        self.stat = ph.sb("stat", [P, 2, 8])
        (self.scored, self.biased, self.ctx_copied, self.negmax, self.exps, self.inverse,
         self.scaled, self.prob_done, self.turned, self.turned_out, self.head_done, self.head_out) = (
            ph.sem(f"att_{s}") for s in ("scored", "biased", "ctx_copied", "negmax", "exps", "inverse", "scaled", "prob_done", "turned", "turned_out",
                  "head_done", "head_out"))
        self.units = heads * TT

    def pe(self, pe):
        units = self.units
        for step in range(units + 3):
            u = step
            if u < units:
                if u >= 2:
                    pe.wait_ge(self.exps, self.maps * (u - 1))
                self.scores(pe, u // TT, u % TT, self.ps[:, 2 * (u % 2):2 * (u % 2) + 2]).then_inc(self.scored, 1)
            u = step - 2
            if 0 <= u < units:
                pe.wait_ge(self.prob_done, u + 1)
                if u >= self.t_slots:
                    pe.wait_ge(self.turned_out, u - self.t_slots + 1)
                for kt in range(self.nk):
                    mm = pe.transpose(self.turned_at(u, kt), self.prob[:, u % 2, 0, kt * P:(kt + 1) * P], self.ident)
                mm.then_inc(self.turned, 1)
            u = step - 3
            if u >= 0 and u % TT == TT - 1:
                h = u // TT
                pe.wait_ge(self.turned_out, u + 1)
                if h >= 2:
                    pe.wait_ge(self.head_out, h - 1)
                for kt in range(self.nk):
                    mm = pe.matmul(self.head_at(h), self.values(h, kt), self.probT[:, h % 2, kt],
                                   start=(kt == 0), stop=(kt == self.nk - 1))
                mm.then_inc(self.head_done, 1)

    def turned_at(self, u, kt):
        slot = (u % 2) if self.t_slots == 2 else 0
        return self.ps[:, 4 + slot + kt // 4, (kt % 4) * P:(kt % 4 + 1) * P]

    def head_at(self, h):
        return self.ps[64 * (h % 2):64 * (h % 2) + 64, 6 + h % 2]

    def dve(self, dve):
        units, maps = self.units, self.maps
        for step in range(units + 1):
            u = step
            if u < units:
                st = self.stat[:, u % 2]
                dve.wait_ge(self.scored, u + 1)
                if u >= 2:
                    dve.wait_ge(self.prob_done, u - 1)
                if self.kind == "bias":
                    self.bias(dve, u)
                    if u >= 2:
                        dve.wait_ge(self.turned, u - 1)
                    dve.tensor_tensor(self.prob[:, u % 2, 0, 0:T], self.ps[:, 2 * (u % 2)],
                                      self.bias_at(u), ALU.add).then_inc(self.biased, 1)
                    dve.wait_ge(self.biased, u + 1)
                    dve.wait_ge(self.ctx_copied, u + 1)
                    dve.tensor_reduce(st[:, 0:1], self.prob[:, u % 2, 0, :], AX.X, ALU.max, negate=True)\
                       .then_inc(self.negmax, 1)
                else:
                    for i in range(maps):
                        dve.tensor_reduce(st[:, i:i + 1], self.ps[:, 2 * (u % 2) + i], AX.X, ALU.max,
                                          negate=True).then_inc(self.negmax, 1)
            u = step - 1
            if u >= 0:
                st = self.stat[:, u % 2]
                dve.wait_ge(self.exps, maps * (u + 1))
                dve.reciprocal(st[:, 4:4 + maps], st[:, 2:2 + maps]).then_inc(self.inverse, 1)
                dve.wait_ge(self.inverse, u + 1)
                p0 = self.prob[:, u % 2, 0]
                if maps == 1:
                    dve.tensor_scalar(p0, p0, st[:, 4:5], None, ALU.mult).then_inc(self.prob_done, 1)
                else:
                    dve.tensor_scalar(p0, p0, st[:, 4:5], None, ALU.mult).then_inc(self.scaled, 1)
                    dve.tensor_scalar(st[:, 6:7], st[:, 5:6], self.neglam, None, ALU.mult).then_inc(self.scaled, 1)
                    dve.wait_ge(self.scaled, 2 * (u + 1))
                    dve.scalar_tensor_tensor(p0, self.prob[:, u % 2, 1], st[:, 6:7], p0, ALU.mult, ALU.add)\
                       .then_inc(self.prob_done, 1)

    def act(self, act):
        units, maps = self.units, self.maps
        for step in range(units + 4):
            u = step
            if u < units:
                st = self.stat[:, u % 2]
                if self.kind == "bias":
                    act.wait_ge(self.scored, u + 1)
                if u >= 2:
                    act.wait_ge(self.turned, u - 1)
                if self.kind == "bias":
                    act.activation(self.prob[:, u % 2, 0, T:T + CTX], self.ps[:, 2 * (u % 2) + 1, 0:CTX], ACT.Copy)\
                       .then_inc(self.ctx_copied, 1)
                for i in range(maps):
                    act.wait_ge(self.negmax, maps * u + i + 1)
                    src = self.prob[:, u % 2, 0] if self.kind == "bias" else self.ps[:, 2 * (u % 2) + i]
                    act.activation(self.prob[:, u % 2, i], src, ACT.Exp, bias=st[:, i:i + 1],
                                   accum_out=st[:, 2 + i:3 + i]).then_inc(self.exps, 1)
            u = step - 2
            if 0 <= u < units:
                h, qt = u // TT, u % TT
                act.wait_ge(self.turned, u + 1)
                if h >= 2:
                    act.wait_ge(self.head_done, h - 1)
                n = min(4, self.nk)
                slot = 4 + ((u % 2) if self.t_slots == 2 else 0)
                ins = act.activation(self.probT[:, h % 2, 0:n, qt * P:(qt + 1) * P],
                                     self.ps[:, slot].rearrange("p (k t) -> p k t", k=4), ACT.Copy)
                if self.nk > 4:
                    ins = act.activation(self.probT[:, h % 2, 4:self.nk, qt * P:(qt + 1) * P],
                                         self.ps[:, 5, 0:(self.nk - 4) * P].rearrange("p (k t) -> p k t", k=self.nk - 4),
                                         ACT.Copy)
                ins.then_inc(self.turned_out, 1)
            u = step - 3
            if u >= 0 and u % TT == TT - 1:
                h = u // TT
                act.wait_ge(self.head_done, h + 1)
                act.activation(self.out(h), self.head_at(h), ACT.Copy).then_inc(self.head_out, 1)
        act.wait_ge(self.head_out, self.heads)


def mla_prepare(nc, m, a, l, mem):
    with Phase(nc, "mlap") as ph:
        ps = ph.psum()
        wuq, wukv = ph.sb("wuq", [P, 3, 384]), ph.sb("wukv", [P, 512])
        sq, rt = ph.sb("sq", [P, 8, T]), ph.sb("rt", [P, 8, T])
        raw = mem.raw
        loaded, step, astep, squares, spread, roots, latent, up, out, prep = (
            ph.sem(s) for s in ("loaded", "step", "astep", "squares", "spread", "roots", "latent", "up", "out", "prep"))
        z = m.z
        units = [(raw[0:96, i], mem.gq if i < 4 else m.g[0:96, G_MK:G_MK + 1], mem.qk[0:96, i]) for i in range(8)]
        gn = GroupNorm(ph, "gn", units, 96, 96, m.ones[0:96, 0:96], m.eps, ps, sq, rt,
                       (m.rope[0:96, 0], m.rope[0:96, 1], m.rot96))
        with nc.Block() as block:
            @block.sync
            def _(sp):
                sp.dma_start(wuq[:], a["w_uq"][l].rearrange("(k p) n -> p k n", p=P)).then_inc(loaded, 16)
                sp.dma_start(wukv[:], a["w_ukv"][l]).then_inc(loaded, 16)
                sp.wait_ge(loaded, 32)

            @block.scalar
            def _(act):
                for k in range(4):
                    act.activation(sq[:, k], z[:, k], ACT.Square).then_inc(squares, 1)
                for i, n in ((0, 384), (1, 128)):
                    act.wait_ge(spread, i + 1)
                    act.activation(rt[:, i], ps[:, i], ACT.Sqrt, bias=m.eps, scale=1.0 / n).then_inc(roots, 1)
                for i in range(8):
                    act.wait_ge(up, i + 1)
                    n = 96 if i < 4 else 64
                    act.activation(raw[0:n, i], ps[0:n, i % 4], ACT.Copy).then_inc(out, 1)
                    if i >= 4:
                        act.activation(raw[64:96, i], z[64:96, Z_KR], ACT.Copy).then_inc(astep, 1)
                for t in range(TT):
                    act.wait_ge(up, 9 + t)
                    act.activation(mem.v[:, t], ps[:, 4 + t, 0:BW], ACT.Copy).then_inc(out, 1)
                act.wait_ge(astep, 4)
                act.wait_ge(out, 12)
                gn.act(act)

            @block.vector
            def _(dve):
                link = linker(dve, step)
                dve.tensor_scalar(mem.gq, m.g[0:96, G_MQ:G_MQ + 1], float(96 ** -0.5), None, ALU.mult).then_inc(prep, 1)
                for i in range(2):
                    dve.wait_ge(roots, i + 1)
                    link(dve.reciprocal(rt[:, i], rt[:, i]))
                for k in range(4):
                    dve.scalar_tensor_tensor(z[:, k], z[:, k], m.g[:, G_QA + k:G_QA + k + 1], rt[:, k // 3],
                                             ALU.mult, ALU.mult).then_inc(latent, 1)
                dve.wait_ge(prep, 1)
                dve.wait_ge(latent, 4)
                dve.wait_ge(out, 12)
                gn.dve(dve)
                dve.wait_ge(gn.done, 8)

            @block.tensor
            def _(pe):
                pe.wait_ge(squares, 4)
                for k in range(3):
                    mm = pe.matmul(ps[:, 0], m.ones, sq[:, k], start=(k == 0), stop=(k == 2))
                mm.then_inc(spread, 1)
                pe.matmul(ps[:, 1], m.ones, sq[:, 3], start=True, stop=True).then_inc(spread, 1)
                pe.wait_ge(latent, 4)
                pe.wait_ge(loaded, 32)
                for h in range(4):
                    for k in range(3):
                        mm = pe.matmul(ps[0:96, h], wuq[:, k, 96 * h:96 * h + 96], z[:, k], start=(k == 0), stop=(k == 2))
                    mm.then_inc(up, 1)
                for h in range(4):
                    pe.wait_ge(out, h + 1)
                    pe.matmul(ps[0:64, h], wukv[:, 128 * h:128 * h + 64], z[:, Z_CKV], start=True, stop=True)\
                      .then_inc(up, 1)
                v_cols = wukv[:].rearrange("p (h n) -> p h n", h=4)[:, :, 64:128]
                for t in range(TT):
                    pe.matmul(ps[:, 4 + t, 0:BW], z[:, Z_CKV, t * P:(t + 1) * P], v_cols, start=True, stop=True)\
                      .then_inc(up, 1)
                pe.wait_ge(out, 12)
                gn.pe(pe)


def mla_attend(nc, m, mem):
    with Phase(nc, "mlaa") as ph:
        ps = ph.psum()

        def scores(pe, h, qt, banks):
            return pe.matmul(banks[:, 0], mem.qk[0:96, h, qt * P:(qt + 1) * P], mem.qk[0:96, 4 + h],
                             start=True, stop=True)

        att = Attention(ph, "plain", 4, ps, m.ident, scores,
                        lambda h, kt: mem.v[:, kt, 64 * h:64 * h + 64],
                        lambda h: m.o[64 * (h % 2):64 * (h % 2) + 64, h // 2])
        with nc.Block() as block:
            @block.scalar
            def _(act):
                att.act(act)

            @block.vector
            def _(dve):
                att.dve(dve)

            @block.tensor
            def _(pe):
                att.pe(pe)


def diff_prepare(nc, m, mem):
    with Phase(nc, "difp") as ph:
        ps = ph.psum()
        sq, rt = ph.sb("sq", [P, 4, T]), ph.sb("rt", [P, 4, T])
        lamp = ph.sb("lamp", [P, 64])
        step, astep, prep = ph.sem("step"), ph.sem("astep"), ph.sem("prep")
        z = m.z
        units = [(z[:, Z_DQ + i], mem.gq if i < 2 else m.g[:, G_DK:G_DK + 1], mem.qk[:, i]) for i in range(4)]
        gn = GroupNorm(ph, "gn", units, P, 32, m.ones32, m.eps, ps, sq, rt, (m.rope[:, 2], m.rope[:, 3], m.rot32))
        lam = m.lamv[:].rearrange("p (a b d) -> p a b d", a=2, b=2)
        with nc.Block() as block:
            @block.scalar
            def _(act):
                act.wait_ge(prep, 1)
                act.activation(mem.lam2[:], mem.lam2[:], ACT.Exp).then_inc(astep, 1)
                gn.act(act)

            @block.vector
            def _(dve):
                link = linker(dve, step)
                link(dve.tensor_tensor(lamp[:].rearrange("p (a d) -> p a d", a=2), lam[:, :, 0], lam[:, :, 1], ALU.mult))
                dve.tensor_reduce(mem.lam2[:], lamp[:].rearrange("p (a d) -> p a d", a=2), AX.X, ALU.add).then_inc(prep, 1)
                dve.wait_ge(astep, 1)
                link(dve.tensor_tensor(mem.lamt[:, 0:1], mem.lam2[:, 1:2], mem.lam2[:, 0:1], ALU.subtract))
                link(dve.tensor_tensor(mem.lamt[:, 1:2], mem.lamt[:, 0:1], m.laminit[:, 0:1], ALU.subtract))
                link(dve.tensor_scalar(mem.gq, m.g[:, G_DQ:G_DQ + 1], float(32 ** -0.5), None, ALU.mult))
                link(dve.tensor_tensor(mem.gsub, m.g[:, G_SUB:G_SUB + 1], m.laminit[:, 1:2], ALU.mult))
                gn.dve(dve)
                dve.wait_ge(gn.done, 4)

            @block.tensor
            def _(pe):
                gn.pe(pe)


def diff_attend(nc, m, mem):
    with Phase(nc, "difa") as ph:
        ps = ph.psum()
        values = m.z[:, Z_DV:Z_DV + 2].rearrange("p a (b n) -> p (a b) n", b=2)

        def scores(pe, h, qt, banks):
            for i in range(2):
                s = 2 * h + i
                at = slice(32 * (s % 4), 32 * (s % 4) + 32)
                mm = pe.matmul(banks[:, i], mem.qk[at, s // 4, qt * P:(qt + 1) * P], mem.qk[at, 2 + s // 4],
                               start=True, stop=True, tile_position=(32 * (s % 4), 0))
            return mm

        att = Attention(ph, "diff", 4, ps, m.ident, scores,
                        lambda h, kt: values[:, kt, 64 * h:64 * h + 64],
                        lambda h: mem.od[64 * (h % 2):64 * (h % 2) + 64, h // 2], neglam=mem.lamt[:, 1:2])
        with nc.Block() as block:
            @block.scalar
            def _(act):
                att.act(act)

            @block.vector
            def _(dve):
                att.dve(dve)

            @block.tensor
            def _(pe):
                att.pe(pe)


def head_norm(nc, m, name, src, gain, dst, gate=None):
    with Phase(nc, name) as ph:
        ps = ph.psum()
        sq, rt = ph.sb("sq", [P, 2, T]), ph.sb("rt", [P, 2, T])
        gated = ph.sem("gated")
        gn = GroupNorm(ph, "gn", [(src[:, j], gain, dst[:, j]) for j in range(2)], P, 64, m.ones64, m.eps, ps, sq, rt)
        with nc.Block() as block:
            @block.scalar
            def _(act):
                gn.act(act)

            @block.vector
            def _(dve):
                gn.dve(dve)
                dve.wait_ge(gn.normed, 2)
                if gate is not None:
                    dve.tensor_tensor(dst, dst, gate, ALU.mult).then_inc(gated, 1)
                    dve.wait_ge(gated, 1)

            @block.tensor
            def _(pe):
                gn.pe(pe)


def fnet(nc, m, a):
    with Phase(nc, "fnet") as ph:
        ps = ph.psum()
        dft = ph.sb("dft", [P, 2, TT, T])
        dft64 = ph.sb("dft64", [P, 2 * P])
        mixed = ph.sb("mixed", [P, 2, TT, 2 * P])
        loaded, inner, inner_out, outer, outer_out = (
            ph.sem(s) for s in ("loaded", "inner", "inner_out", "outer", "outer_out"))
        with nc.Block() as block:
            @block.sync
            def _(sp):
                sp.dma_start(dft64[:], a["dft64"]).then_inc(loaded, 16)
                sp.dma_start(dft[:], a["dft"]).then_inc(loaded, 16)
                sp.wait_ge(loaded, 32)

            @block.tensor
            def _(pe):
                pe.wait_ge(loaded, 32)
                for i in range(2 * TT):
                    j, t = divmod(i, TT)
                    if i >= 4:
                        pe.wait_ge(inner_out, i - 3)
                    pe.matmul(ps[:, i % 4, 0:2 * P], m.z[:, Z_FU + j, t * P:(t + 1) * P], dft64[:],
                              start=True, stop=True).then_inc(inner, 1)
                pe.wait_ge(inner_out, 2 * TT)
                for j in range(2):
                    for t in range(TT):
                        for part in range(2):
                            mm = pe.matmul(ps[:, 4 + j], mixed[:, j, t, part * P:(part + 1) * P], dft[:, part, t],
                                           start=(t == 0 and part == 0), stop=(t == TT - 1 and part == 1))
                    mm.then_inc(outer, 1)

            @block.scalar
            def _(act):
                for i in range(2 * TT):
                    j, t = divmod(i, TT)
                    act.wait_ge(inner, i + 1)
                    act.activation(mixed[:, j, t], ps[:, i % 4, 0:2 * P], ACT.Copy).then_inc(inner_out, 1)
                for j in range(2):
                    act.wait_ge(outer, j + 1)
                    act.activation(m.o[:, 2 + j], ps[:, 4 + j], ACT.Copy).then_inc(outer_out, 1)
                act.wait_ge(outer_out, 2)


def hgrn(nc, m, a, od):
    with Phase(nc, "hgrn") as ph:
        ps = ph.psum()
        big = lambda name, n=1: ph.sb(name, [P, n, 2 * T] if n > 1 else [P, 2 * T])
        cum, key, work = big("cum", 2), big("key", 2), big("work", 2)
        qs, ks = big("qs", 2), big("ks", 2)
        masks = ph.sb("masks", [P, len(LEVELS) + 1, P])
        reset = ph.sb("reset", [P, T])
        masked = ph.sb("masked", [P, 2, T])
        kturned = ph.sb("kturned", [P, 2, TT, 2 * P])
        state = ph.sb("state", [P, 2, 3, 2, P])
        decay = ph.sb("decay", [P, 2, 2, TT])
        omlb = ph.sb("omlb", [P, 4])
        names = ("loaded", "prep", "sig", "forget", "logs", "scans", "link_v", "link_a", "diffs", "exps", "operands", "scored",
                 "masked_s", "valued", "carry_in", "carry_turned", "carry_out", "grown", "states", "out_copied")
        s = {n: ph.sem(n) for n in names}
        z = m.z
        hq = z[:, Z_HQ:Z_HQ + 2].rearrange("p a t -> p (a t)")
        gates = z[:, Z_HF:Z_HF + 4]
        values = z[:, Z_HV:Z_HV + 2].rearrange("p a (b n) -> p (a b) n", b=2)
        nl = len(LEVELS) + 1

        def halves(x, b):
            v = x.rearrange("p (n c) -> p n c", c=2 * b)
            return v[:, :, 0:b], v[:, :, b:2 * b]

        def blocks(x):
            return x.rearrange("p (n c) -> p n c", c=P)

        with nc.Block() as block:
            @block.sync
            def _(sp):
                sp.dma_start(masks[:], a["masks"]).then_inc(s["loaded"], 16)
                sp.dma_start(reset[:], a["reset"]).then_inc(s["loaded"], 16)
                sp.wait_ge(s["loaded"], 32)

            @block.gpsimd
            def _(pool):
                pool.memset(state[:], 0.0).then_inc(s["states"], 1)

            @block.scalar
            def _(act):
                act.activation(gates, gates, ACT.Sigmoid).then_inc(s["sig"], 1)
                act.activation(z[:, Z_HG:Z_HG + 2], z[:, Z_HG:Z_HG + 2], ACT.Sigmoid).then_inc(s["sig"], 1)
                act.wait_ge(s["forget"], 4)
                act.activation(work[:].rearrange("p d t -> p (d t)"), gates.rearrange("p a t -> p (a t)"), ACT.Ln)\
                   .then_inc(s["logs"], 1)
                act.wait_ge(s["diffs"], 1)
                act.activation(work[:], work[:], ACT.Exp).then_inc(s["exps"], 1)
                act.activation(decay[:, 0], cum[:, 0].rearrange("p (j n c) -> p j n c", j=2, c=P)[:, :, :, P - 1],
                               ACT.Exp).then_inc(s["exps"], 1)
                act.activation(decay[:, 1], cum[:, 1].rearrange("p (j n c) -> p j n c", j=2, c=P)[:, :, :, 0],
                               ACT.Exp).then_inc(s["exps"], 1)
                act.activation(qs[:], cum[:], ACT.Exp).then_inc(s["exps"], 1)
                for i in range(4):
                    d, j = divmod(i, 2)
                    act.wait_ge(s["carry_turned"], i + 1)
                    act.activation(kturned[:, d].rearrange("p t (j n) -> p t j n", j=2)[:, :, j],
                                   ps[:, i].rearrange("p (t n) -> p t n", t=TT), ACT.Copy).then_inc(s["carry_out"], 1)
                for n, b in enumerate(LEVELS):
                    fl, fu = halves(work[:, 0], b)
                    bl, bu = halves(work[:, 1], b)
                    ql, qu = halves(qs[:, n % 2], b)
                    kl, ku = halves(ks[:, n % 2], b)
                    act.wait_ge(s["diffs"], 2 + 2 * n + 1)
                    if n >= 1:
                        act.wait_ge(s["scored"], TT * (n - 1))
                    act.activation(qu, fu, ACT.Exp).then_inc(s["exps"], 1)
                    act.activation(kl, fl, ACT.Exp, scale=-1.0).then_inc(s["exps"], 1)
                    act.activation(ql, bl, ACT.Exp).then_inc(s["exps"], 1)
                    act.activation(ku, bu, ACT.Exp, scale=-1.0).then_inc(s["exps"], 1)
                for j in range(2):
                    act.wait_ge(s["valued"], nl * TT + 1)
                    act.activation(od[:, j], ps[:, 6 + j], ACT.Copy).then_inc(s["out_copied"], 1)
                act.wait_ge(s["out_copied"], 2)

            @block.vector
            def _(dve):
                link = linker(dve, s["link_v"])
                link(dve.tensor_scalar(omlb[:], m.lbl[:], -1.0, 1.0, ALU.mult, ALU.add))
                dve.wait_ge(s["sig"], 1)
                for i in range(4):
                    dve.tensor_scalar(gates[:, i], gates[:, i], omlb[:, i:i + 1], m.lbl[:, i:i + 1], ALU.mult, ALU.add)\
                       .then_inc(s["forget"], 1)
                dve.wait_ge(s["forget"], 4)
                link(dve.tensor_scalar(key[:].rearrange("p d t -> p (d t)"), gates.rearrange("p a t -> p (a t)"),
                                       -1.0, 1.0, ALU.mult, ALU.add))
                dve.wait_ge(s["logs"], 1)
                dve.wait_ge(s["loaded"], 32)
                for j in range(2):
                    at = slice(j * T, (j + 1) * T)
                    dve.tensor_tensor_scan(cum[:, 0, at], reset[:], work[:, 0, at], 0.0, ALU.mult, ALU.add)\
                       .then_inc(s["scans"], 1)
                    dve.tensor_tensor_scan(cum[:, 1, at][:, ::-1], reset[:], work[:, 1, at][:, ::-1], 0.0,
                                           ALU.mult, ALU.add).then_inc(s["scans"], 1)
                dve.wait_ge(s["scans"], 4)
                last_f = blocks(cum[:, 0])[:, :, P - 1:P].broadcast_to([P, 2 * TT, P])
                last_b = blocks(cum[:, 1])[:, :, 0:1].broadcast_to([P, 2 * TT, P])
                link(dve.tensor_tensor(blocks(work[:, 0]), last_f, blocks(cum[:, 0]), ALU.subtract))
                dve.tensor_tensor(blocks(work[:, 1]), last_b, blocks(cum[:, 1]), ALU.subtract).then_inc(s["diffs"], 1)
                dve.wait_ge(s["exps"], 4)
                dve.tensor_tensor(work[:], work[:], key[:], ALU.mult).then_inc(s["carry_in"], 1)
                hq2 = hq.rearrange("p (o t) -> p o t", o=1).broadcast_to([P, 2, 2 * T])
                dve.tensor_tensor(qs[:], qs[:], hq2, ALU.mult).then_inc(s["carry_in"], 1)
                dve.wait_ge(s["states"], 1)
                done = 1
                for d in range(2):
                    for i in range(3):
                        c = i if d == 0 else TT - 1 - i
                        for j in range(2):
                            g = (d * 3 + i) * 2 + j
                            dve.wait_ge(s["grown"], 4 * (g // 4) + 4)
                            for half in range(2):
                                r = slice(64 * half, 64 * half + 64)
                                new = state[r, d, i, j, r]
                                src = ps[r, 4 + g // 4 if g < 8 else 0, (g % 4) * P + 64 * half:(g % 4) * P + 64 * half + 64]
                                if i == 0:
                                    ins = dve.tensor_copy(new, src)
                                else:
                                    dve.wait_ge(s["states"], done - 3)
                                    ins = dve.scalar_tensor_tensor(new, state[r, d, i - 1, j, r], decay[r, d, j, c:c + 1],
                                                                   src, ALU.mult, ALU.add)
                                ins.then_inc(s["states"], 1)
                                done += 1
                def mask_out(n):
                    for t in range(TT):
                        i = n * TT + t
                        dve.wait_ge(s["scored"], i + 1)
                        if i >= 2:
                            dve.wait_ge(s["valued"], i)
                        b = 2 * (i % 3)
                        for odd in range(2):
                            ins = dve.tensor_tensor(
                                masked[:, i % 2, odd * 2 * P:(odd + 1) * 2 * P].rearrange("p (h t) -> p h t", h=2),
                                ps[:, b + odd, 0:2 * P].rearrange("p (h t) -> p h t", h=2),
                                masks[:, n:n + 1].broadcast_to([P, 2, P]), ALU.mult)
                        ins.then_inc(s["masked_s"], 1)

                dve.wait_ge(s["carry_out"], 4)
                dve.wait_ge(s["valued"], 1)
                for n, b in enumerate(LEVELS):
                    if n >= 1:
                        dve.wait_ge(s["exps"], 4 + 4 * n)
                    for d in range(2):
                        v = cum[:, d].rearrange("p (n c) -> p n c", c=2 * b)
                        ref = v[:, :, b - 1:b] if d == 0 else v[:, :, b:b + 1]
                        dve.tensor_tensor(work[:, d].rearrange("p (n c) -> p n c", c=2 * b), v,
                                          ref.broadcast_to([P, T // b, 2 * b]), ALU.subtract).then_inc(s["diffs"], 1)
                    if n >= 1:
                        mask_out(n - 1)
                    dve.wait_ge(s["exps"], 4 + 4 * (n + 1))
                    dve.tensor_tensor(qs[:, n % 2], qs[:, n % 2], hq, ALU.mult).then_inc(s["operands"], 1)
                    kl, ku = halves(ks[:, n % 2], b)
                    dve.tensor_tensor(kl, kl, halves(key[:, 0], b)[0], ALU.mult).then_inc(s["operands"], 1)
                    dve.tensor_tensor(ku, ku, halves(key[:, 1], b)[1], ALU.mult).then_inc(s["operands"], 1)
                n = nl - 1
                mask_out(n - 1)
                dve.tensor_copy(qs[:, n % 2], hq).then_inc(s["operands"], 1)
                dve.tensor_tensor(ks[:, n % 2], key[:, 0], key[:, 1], ALU.add).then_inc(s["operands"], 1)
                mask_out(n)

            @block.tensor
            def _(pe):
                pe.wait_ge(s["carry_in"], 2)
                for i in range(4):
                    d, j = divmod(i, 2)
                    for t in range(TT):
                        mm = pe.transpose(ps[:, i, t * P:(t + 1) * P], work[:, d, j * T + t * P:j * T + (t + 1) * P], m.ident)
                    mm.then_inc(s["carry_turned"], 1)
                for g in range(12):
                    di, j = divmod(g, 2)
                    d, i = divmod(di, 3)
                    c = i if d == 0 else TT - 1 - i
                    pe.wait_ge(s["carry_out"], 4)
                    pe.matmul(ps[:, 4 + g // 4 if g < 8 else 0, (g % 4) * P:(g % 4 + 1) * P],
                              kturned[:, d, c, j * P:(j + 1) * P], values[:, c, j * P:(j + 1) * P],
                              start=True, stop=True).then_inc(s["grown"], 1)
                pe.wait_ge(s["states"], 25)
                for j in range(2):
                    for d in range(2):
                        for i in range(3):
                            c = i + 1 if d == 0 else TT - 2 - i
                            mm = pe.matmul(ps[:, 6 + j, c * P:(c + 1) * P], state[:, d, i, j],
                                           qs[:, d, j * T + c * P:j * T + (c + 1) * P],
                                           start=(d == 0 and i == 0), stop=False, skip_group_check=True)
                mm.then_inc(s["valued"], 1)
                total = nl * TT
                for i in range(total + 1):
                    if i < total:
                        n, t = divmod(i, TT)
                        if t == 0:
                            pe.wait_ge(s["operands"], 3 * (n + 1) if n < nl - 1 else 3 * n + 2)
                        if i >= 3:
                            pe.wait_ge(s["masked_s"], i - 2)
                        for h in range(4):
                            r = slice(64 * (h % 2), 64 * (h % 2) + 64)
                            at = slice((h // 2) * T + t * P, (h // 2) * T + (t + 1) * P)
                            mm = pe.matmul(ps[:, 2 * (i % 3) + h % 2, (h // 2) * P:(h // 2 + 1) * P], ks[r, n % 2, at], qs[r, n % 2, at],
                                           start=True, stop=True)
                        mm.then_inc(s["scored"], 1)
                    i -= 1
                    if i >= 0:
                        n, t = divmod(i, TT)
                        pe.wait_ge(s["masked_s"], i + 1)
                        for h in range(4):
                            mm = pe.matmul(ps[64 * (h % 2):64 * (h % 2) + 64, 6 + h // 2, t * P:(t + 1) * P],
                                           values[:, t, 64 * h:64 * h + 64], masked[:, i % 2, (2 * (h % 2) + h // 2) * P:(2 * (h % 2) + h // 2 + 1) * P],
                                           start=False, stop=(i == total - 1), skip_group_check=True)
                        mm.then_inc(s["valued"], 1)


class SwiGLU:

    def __init__(self, ph, m, ring, ps, steps, c0, w0, hidden):
        self.m, self.ring, self.ps, self.steps, self.c0, self.w0 = m, ring, ps, steps, c0, w0
        self.hid_hi, self.hid_lo = hidden
        self.silu, self.hid = m.z[:, 18:20], m.z[:, 20:22]
        (self.up_done, self.silu_done, self.product_done, self.hid_hi_done,
         self.hid_lo_done, self.down_done, self.down_added) = (
            ph.sem(f"x_{s}") for s in ("up_done", "silu_done", "product_done", "hid_hi_done", "hid_lo_done", "down_done", "down_added"))

    def open(self, sp):
        sp.sem_inc(self.product_done, 2)
        sp.sem_inc(self.up_done, 2)
        sp.sem_inc(self.down_done, KD)
        sp.sem_inc(self.down_added, 4)

    def sp(self, sp, gate_src, up_src, down_src):
        with sp.Fori(0, self.steps) as j:
            self.ring.load(sp, 2 * j + self.c0, self.c0 % 2, gate_src(j))
            self.ring.load(sp, 2 * j + (self.c0 + 1), (self.c0 + 1) % 2, up_src(j))
            self.ring.load_wide(sp, j + self.w0, down_src(j))

    def pool(self, pool):
        with pool.Fori(0, self.steps) as j:
            self.ring.cut_lo(pool, 2 * j + self.c0, self.c0 % 2)
            self.ring.cut_lo(pool, 2 * j + (self.c0 + 1), (self.c0 + 1) % 2)
            self.ring.cut_wide_lo(pool, j + self.w0)

    def act(self, act):
        ring, c0 = self.ring, self.c0
        with act.Fori(0, self.steps) as j:
            act.wait_ge(self.up_done, 2 * j + 2)
            ring.cut_hi(act, c0 % 2, 16 * j + 16 * (c0 // 2 + 1))
            ring.cut_hi(act, (c0 + 1) % 2, 16 * j + 16 * ((c0 + 1) // 2 + 1))
            act.wait_ge(self.down_done, 8 * j + 8)
            ring.cut_wide_hi(act, j + self.w0)
            for i in range(2):
                act.wait_ge(self.up_done, 2 * j + (i + 3))
                act.activation(self.silu[:, i], self.ps[:, 2 * i], ACT.Silu).then_inc(self.silu_done, 1)
            for i in range(2):
                act.wait_ge(self.product_done, 2 * j + (i + 3))
                act.activation(self.hid_hi[:, i], self.hid[:, i], ACT.Copy).then_inc(self.hid_hi_done, 1)

    def dve(self, dve):
        m = self.m
        with dve.Fori(0, self.steps) as j:
            for i in range(2):
                dve.wait_ge(self.silu_done, 2 * j + (i + 1))
                dve.tensor_tensor(self.hid[:, i], self.silu[:, i], self.ps[:, 2 * i + 1], ALU.mult)\
                   .then_inc(self.product_done, 1)
            for i in range(2):
                dve.wait_ge(self.hid_hi_done, 2 * j + (i + 1))
                dve.tensor_tensor(self.hid_lo[:, i], self.hid[:, i], self.hid_hi[:, i].bitcast(F32), ALU.subtract)\
                   .then_inc(self.hid_lo_done, 1)
            for c in range(KD):
                dve.wait_ge(self.down_done, 8 * j + (c + 9))
                bank = self.ps[:, 4 + c % 4]
                dve.tensor_tensor(m.x[:, c], m.x[:, c], bank, ALU.add).then_inc(self.down_added, 1)
        dve.wait_ge(self.down_added, 4 + 8 * self.steps)

    def pe(self, pe):
        m, ring, ps = self.m, self.ring, self.ps
        slots = [(cols(ring.hi[:, (self.c0 + i) % 2], CW), cols(ring.lo[:, (self.c0 + i) % 2], CW)) for i in range(2)]
        whi, wlo = cols(ring.whi, D, 2), cols(ring.wlo, D, 2)
        with pe.Fori(0, self.steps) as j:
            ring.wait_cut(pe, 2 * j + (self.c0 + 1))
            for i in range(2):
                pe.wait_ge(self.product_done, 2 * j + (i + 1))
                at = slice(i * P, (i + 1) * P)
                for g, (hi, lo) in enumerate(slots):
                    mm = product3(pe, ps[:, 2 * i + g], lambda k: hi[:, k, at], lambda k: lo[:, k, at],
                                  lambda k: m.hi[:, k], lambda k: m.lo[:, k], range(KD))
                mm.then_inc(self.up_done, 1)
            pe.wait_ge(ring.wide_lo, j + (self.w0 + 2))
            pe.wait_ge(self.hid_lo_done, 2 * j + 1)

            def down(c, ks, start, stop):
                at = slice(c * P, (c + 1) * P)
                return product3(pe, ps[:, 4 + c % 4], lambda k: whi[:, k, at], lambda k: wlo[:, k, at],
                                lambda k: self.hid_hi[:, k], lambda k: self.hid_lo[:, k], ks, start, stop)

            for c in range(4):
                pe.wait_ge(self.down_added, 8 * j + (c + 1))
                down(c, (0,), True, False)
            pe.wait_ge(self.hid_lo_done, 2 * j + 2)
            for c in range(4):
                down(c, (1,), False, True).then_inc(self.down_done, 1)
            for c in range(4, 8):
                pe.wait_ge(self.down_added, 8 * j + (c + 1))
                down(c, (0, 1), True, True).then_inc(self.down_done, 1)


def merge_and_ffn(nc, m, a, l):
    with Phase(nc, "ffn") as ph:
        ring = Ring(ph, True)
        ps = ph.psum()
        z = m.z
        ohi, olo = ph.sb("ohi", [P, 2, T], F32R), ph.sb("olo", [P, 2, T], F32R)
        merged, sig, tmp = z[:, 0:8], z[:, 18:22], z[:, 22]
        names = ("o_hi", "o_lo", "gate_done", "sig_done", "gated", "merged_s", "m_hi", "m_lo", "out_done", "out_added", "zeroed")
        s = {n: ph.sem(n) for n in names}
        norm = Norm(ph, "n", m.x, z[:, 8:16], z[:, 16], z[:, 17], z[:, 0:8], m.hi, m.lo, ps[:, 7], m.ones, m.eps, T)
        c_out, c_ffn = 4 * NB, 4 * NB + 4
        ex = SwiGLU(ph, m, ring, ps, FF_STEPS, c_ffn, NB, (ohi, olo))
        w_in = a["w_in"][l].rearrange("(k p) n -> p k n", p=P)
        w_br = a["w_branch"][l].rearrange("n (k p) d -> n p k d", p=P)
        w_out = a["w_out"][l].rearrange("(k p) n -> p k n", p=P)
        w_gu = a["w_gate_up"][l].rearrange("(k p) n -> p k n", p=P)
        w_dn = a["w_down"][l].rearrange("(j k p) n -> j p k n", p=P, k=2)
        with nc.Block() as block:
            @block.sync
            def _(sp):
                ring.open(sp)
                ex.open(sp)
                sp.sem_inc(s["merged_s"], 4)
                sp.sem_inc(s["gate_done"], 8)
                with sp.Fori(0, NB) as n:
                    ring.load_wide(sp, n, w_br[n])
                    for i in range(4):
                        ring.load(sp, 4 * n + i, i % 2, w_in[:, :, bass.ds(n * D + (C_GATE + i * CW), CW)])
                for i in range(4):
                    ring.load(sp, c_out + i, i % 2, w_out[:, :, i * CW:(i + 1) * CW])
                ex.sp(sp, lambda j: w_gu[:, :, bass.ds(j * CW, CW)],
                      lambda j: w_gu[:, :, bass.ds(j * CW + DFF, CW)], lambda j: w_dn[j])

            @block.gpsimd
            def _(pool):
                with pool.Fori(0, NB) as n:
                    ring.cut_wide_lo(pool, n)
                    for i in range(4):
                        ring.cut_lo(pool, 4 * n + i, i % 2)
                for i in range(4):
                    ring.cut_lo(pool, c_out + i, i % 2)
                ex.pool(pool)

            @block.scalar
            def _(act):
                ring.cut_hi(act, 0, 16)
                with act.Fori(0, NB) as n:
                    act.wait_ge(s["gate_done"], 8 * n + 8)
                    for j in range(2):
                        act.activation(ohi[:, j], m.o[:, bass.ds(2 * n + j, 1)].rearrange("p o t -> p (o t)"), ACT.Copy)\
                           .then_inc(s["o_hi"], 1)
                    ring.cut_wide_hi(act, n)
                    for i in range(4):
                        act.wait_ge(s["gate_done"], 8 * n + (2 * i + 8))
                        ring.cut_hi(act, (i + 1) % 2, 32 * n + 16 * ((i + 1) // 2 + 1))
                        for p in range(2):
                            t = 2 * i + p
                            act.wait_ge(s["gate_done"], 8 * n + (t + 9))
                            act.wait_ge(s["merged_s"], 8 * n + (t + 1))
                            act.activation(sig[:, t % 4], ps[:, t % 4], ACT.Sigmoid).then_inc(s["sig_done"], 1)
                act.wait_ge(s["gate_done"], 8 * NB + 8)
                for k in range(KD):
                    act.wait_ge(s["merged_s"], 4 + 8 * (NB - 1) + k + 1)
                    act.activation(m.hi[:, k], merged[:, k], ACT.Copy).then_inc(s["m_hi"], 1)
                for i in range(3):
                    if i:
                        act.wait_ge(s["out_done"], 2 * i)
                    ring.cut_hi(act, (i + 1) % 2, 16 * ((c_out + i + 1) // 2 + 1))
                act.wait_ge(s["out_added"], KD)
                norm.act_squares(act)
                norm.act_root(act)
                act.wait_ge(s["out_done"], KD)
                norm.act_hi(act)
                ex.act(act)

            @block.vector
            def _(dve):
                dve.memset(merged, 0.0).then_inc(s["zeroed"], 1)
                dve.wait_ge(s["zeroed"], 1)
                with dve.Fori(0, NB) as n:
                    for j in range(2):
                        dve.wait_ge(s["o_hi"], 2 * n + (j + 1))
                        dve.tensor_tensor(olo[:, j], m.o[:, bass.ds(2 * n + j, 1)].rearrange("p o t -> p (o t)"),
                                          ohi[:, j].bitcast(F32), ALU.subtract).then_inc(s["o_lo"], 1)
                    for t in range(KD):
                        dve.wait_ge(s["sig_done"], 8 * n + (t + 1))
                        dve.wait_ge(s["merged_s"], 8 * n + (t + 4))
                        dve.tensor_tensor(tmp, sig[:, t % 4], ps[:, 4 + t % 4], ALU.mult).then_inc(s["gated"], 1)
                        dve.wait_ge(s["gated"], 8 * n + (t + 1))
                        dve.tensor_tensor(merged[:, t], merged[:, t], tmp, ALU.add).then_inc(s["merged_s"], 1)
                for k in range(KD):
                    dve.wait_ge(s["m_hi"], k + 1)
                    dve.tensor_tensor(m.lo[:, k], merged[:, k], m.hi[:, k].bitcast(F32), ALU.subtract).then_inc(s["m_lo"], 1)
                for t in range(KD):
                    dve.wait_ge(s["out_done"], t + 1)
                    dve.tensor_tensor(m.x[:, t], m.x[:, t], ps[:, t % 4], ALU.add).then_inc(s["out_added"], 1)
                norm.dve_total(dve)
                norm.dve_apply(dve, lambda k: m.g[:, G_FFN + k:G_FFN + k + 1])
                ex.dve(dve)

            @block.tensor
            def _(pe):
                whi, wlo = cols(ring.whi, D, 2), cols(ring.wlo, D, 2)
                with pe.Fori(0, NB) as n:
                    pe.wait_ge(s["o_lo"], 2 * n + 2)
                    pe.wait_ge(ring.wide_lo, n + 2)
                    for i in range(4):
                        ring.wait_cut(pe, 4 * n + i)
                        hi, lo = cols(ring.hi[:, i % 2], CW), cols(ring.lo[:, i % 2], CW)
                        for p in range(2):
                            t = 2 * i + p
                            pe.wait_ge(s["merged_s"], 8 * n + (t + 1))
                            ct, cp = slice(t * P, (t + 1) * P), slice(p * P, (p + 1) * P)
                            product3(pe, ps[:, 4 + t % 4], lambda k: whi[:, k, ct], lambda k: wlo[:, k, ct],
                                     lambda k: ohi[:, k], lambda k: olo[:, k], range(2))
                            product3(pe, ps[:, t % 4], lambda k: hi[:, k, cp], lambda k: lo[:, k, cp],
                                     lambda k: m.hi[:, k], lambda k: m.lo[:, k], range(KD)).then_inc(s["gate_done"], 1)
                pe.wait_ge(s["m_lo"], KD)
                for t in range(KD):
                    i = t // 2
                    if t % 2 == 0:
                        ring.wait_cut(pe, c_out + i)
                    hi, lo = cols(ring.hi[:, i % 2], CW), cols(ring.lo[:, i % 2], CW)
                    cp = slice((t % 2) * P, (t % 2 + 1) * P)
                    if t >= 4:
                        pe.wait_ge(s["out_added"], t - 3)
                    product3(pe, ps[:, t % 4], lambda k: hi[:, k, cp], lambda k: lo[:, k, cp],
                             lambda k: m.hi[:, k], lambda k: m.lo[:, k], range(KD)).then_inc(s["out_done"], 1)
                norm.pe_spread(pe)
                pe.wait_ge(norm.lo_cut, KD)
                ex.pe(pe)


M_SHA, M_SCA, M_GA, M_SHF, M_SCF, M_GF = 0, 8, 16, 24, 32, 40
MODS = 48


def modulation(nc, m, a):
    slots, turns = 4, 6
    with Phase(nc, "ada") as ph:
        ps = ph.psum()
        raw = ph.sb("raw", [P, slots, CHUNK])
        cond = ph.sb("cond", [P, KD, 2])
        bias = ph.sb("bias", [P, MODS])
        small, silu, chunk_used, done, scaled = (ph.sem(s) for s in ("small", "silu", "chunk_used", "done", "scaled"))
        ready = [ph.sem(f"ready{i}") for i in range(slots)]
        w = a["w_ada"].rearrange("(k p) n -> p k n", p=P)
        with nc.Block() as block:
            @block.sync
            def _(sp):
                sp.dma_start(cond[:], a["cond"]).then_inc(small, 16)
                sp.dma_start(bias[:], a["b_ada"]).then_inc(small, 16)
                sp.sem_inc(chunk_used, slots)
                with sp.Fori(0, turns) as j:
                    for i in range(slots):
                        sp.wait_ge(chunk_used, slots * j + (i + 1))
                        sp.dma_start(cols(raw[:, i], CW), w[:, :, bass.ds(j * (slots * CW) + i * CW, CW)])\
                          .then_inc(ready[i], 16)

            @block.scalar
            def _(act):
                act.wait_ge(small, 32)
                act.activation(cond[:], cond[:], ACT.Silu).then_inc(silu, 1)

            @block.tensor
            def _(pe):
                pe.wait_ge(silu, 1)
                with pe.Fori(0, turns) as j:
                    for i in range(slots):
                        pe.wait_ge(ready[i], 16 * j + 16)
                        chunk = cols(raw[:, i], CW)
                        for p in range(2):
                            for k in range(KD):
                                mm = pe.matmul(ps[:, 0, bass.ds(j * (4 * slots) + (4 * i + 2 * p), 2)],
                                               chunk[:, k, p * P:(p + 1) * P], cond[:, k],
                                               start=(k == 0), stop=(k == KD - 1))
                        mm.then_inc(chunk_used, 1)

            @block.vector
            def _(dve):
                dve.wait_ge(chunk_used, slots * (turns + 1))
                dve.tensor_tensor(m.mod[:], ps[:, 0, 0:2 * MODS].rearrange("p (n o) -> p n o", o=2),
                                  bias[:].rearrange("p (n o) -> p n o", o=1).broadcast_to([P, MODS, 2]), ALU.add)\
                   .then_inc(done, 1)
                dve.wait_ge(done, 1)
                for t in (M_SCA, M_SCF):
                    dve.tensor_scalar(m.mod[:, t:t + KD], m.mod[:, t:t + KD], 1.0, None, ALU.add).then_inc(scaled, 1)
                dve.wait_ge(scaled, 2)


NA_W = 512
N_Q, N_K, N_U, N_VS, N_V, N_KC = 0, 4, 8, 12, 16, 20


def project2(nc, m, a):
    plan = []
    for base, kind in ((0, "q"), (NA_W, "k"), (3 * NA_W, "u"), (2 * NA_W, "v"), (4 * NA_W, "vs")):
        plan += [(base + half * CW, kind, half) for half in range(2)]
    tiles = []
    for c, (_, kind, _) in enumerate(plan):
        n = {"q": 2, "u": 2, "k": 4, "vs": TT, "v": TT + CT}[kind]
        tiles += [(c, i) for i in range(n)]
    with Phase(nc, "proj2") as ph:
        ring = Ring(ph, False)
        ps = ph.psum()
        ctx = ph.sb("ctx", [P, KD, CTX])
        chi, clo = ph.sb("ctx_hi", [P, KD, CTX], F32R), ph.sb("ctx_lo", [P, KD, CTX], F32R)
        ctx_loaded, tile_done, evicted = (ph.sem(s) for s in ("ctx_loaded", "tile_done", "evicted"))
        z = m.z
        norm = Norm(ph, "n", m.x, z[:, 8:16], z[:, 16], z[:, 17], z[:, 0:8], m.hi, m.lo, ps[:, 7],
                    m.ones, m.eps, T)
        half_tiles = lambda x: x.rearrange("p a (b t) -> p (a b) t", b=2)
        cnorm = Norm(ph, "c", ctx, half_tiles(m.o[:, 4:8]), z[:, 18, 0:CTX], z[:, 19, 0:CTX],
                     half_tiles(m.o[:, 0:4]), chi, clo, ps[:, 6, 0:CTX], m.ones, m.eps, CTX)
        w = a["w_in2"].rearrange("(k p) n -> p k n", p=P)
        with nc.Block() as block:
            @block.sync
            def _(sp):
                ring.open(sp)
                sp.dma_start(ctx[:], a["ctxT"].rearrange("(k p) t -> p k t", p=P)).then_inc(ctx_loaded, 16)
                for c, (col, _, _) in enumerate(plan):
                    ring.load(sp, c, c % RING, w[:, :, col:col + CW])

            @block.gpsimd
            def _(pool):
                for c in range(len(plan)):
                    ring.cut_lo(pool, c, c % RING)

            @block.vector
            def _(dve):
                norm.dve_total(dve)
                norm.dve_apply(dve, lambda k: m.mod[:, M_SCA + k, 0:1], lambda k: m.mod[:, M_SHA + k, 0:1])
                cnorm.dve_total(dve)
                cnorm.dve_apply(dve, lambda k: m.mod[:, M_SCA + k, 1:2], lambda k: m.mod[:, M_SHA + k, 1:2])

            @block.scalar
            def _(act):
                def cut(c):
                    if c < len(plan):
                        if c >= RING:
                            act.wait_ge(tile_done, max(i for i, t in enumerate(tiles) if t[0] == c - RING) + 1)
                        ring.cut_hi(act, c % RING, 16 * (c // RING + 1))

                norm.act_squares(act)
                act.wait_ge(ctx_loaded, 16)
                cnorm.act_squares(act)
                cut(0)
                cut(1)
                norm.act_root(act)
                norm.act_hi(act)
                cnorm.act_root(act)
                cnorm.act_hi(act)
                for i, (c, part) in enumerate(tiles):
                    if part == 0 and c:
                        cut(c + 1)
                    _, kind, half = plan[c]
                    bank = ps[:, i % 6]
                    act.wait_ge(tile_done, i + 1)
                    if kind == "k" and part >= 2:
                        t = 2 * half + part - 2
                        ins = act.activation(z[:, N_KC + t // 2, (t % 2) * CTX:(t % 2 + 1) * CTX], bank[:, 0:CTX], ACT.Copy)
                    elif kind in "qku":
                        first = {"q": N_Q, "k": N_K, "u": N_U}[kind]
                        ins = act.activation(z[:, first + 2 * half + part], bank,
                                             ACT.Gelu_apprx_tanh if kind == "u" else ACT.Copy)
                    else:
                        at = slice(half * CW, (half + 1) * CW)
                        if kind == "vs":
                            ins = act.activation(z[:, N_VS + part, at], bank[:, 0:CW], ACT.Gelu_apprx_tanh)
                        elif part < TT:
                            ins = act.activation(z[:, N_V + part, at], bank[:, 0:CW], ACT.Copy)
                        else:
                            ins = act.activation(m.o[:, part - TT, at], bank[:, 0:CW], ACT.Copy)
                    ins.then_inc(evicted, 1)
                act.wait_ge(evicted, len(tiles))

            @block.tensor
            def _(pe):
                norm.pe_spread(pe)
                cnorm.pe_spread(pe)
                pe.wait_ge(norm.lo_cut, KD)
                for i, (c, part) in enumerate(tiles):
                    _, kind, _ = plan[c]
                    hi, lo = cols(ring.hi[:, c % RING], CW), cols(ring.lo[:, c % RING], CW)
                    if part == 0:
                        ring.wait_cut(pe, c)
                    if i >= 6:
                        pe.wait_ge(evicted, i - 5)
                    bank = ps[:, i % 6]
                    if kind in "qku":
                        of_ctx = part >= 2
                        if of_ctx:
                            pe.wait_ge(cnorm.lo_cut, KD)
                        at = slice((part % 2) * P, (part % 2 + 1) * P)
                        xh, xl = (chi, clo) if of_ctx else (m.hi, m.lo)
                        mm = product3(pe, bank[:, 0:CTX] if of_ctx else bank, lambda k: hi[:, k, at], lambda k: lo[:, k, at],
                                      lambda k: xh[:, k], lambda k: xl[:, k], range(KD))
                    else:
                        xh, xl, t = (m.hi, m.lo, part) if part < TT else (chi, clo, part - TT)
                        at = slice(t * P, (t + 1) * P)
                        mm = product3(pe, bank[:, 0:CW], lambda k: xh[:, k, at], lambda k: xl[:, k, at],
                                      lambda k: hi[:, k], lambda k: lo[:, k], range(KD))
                    mm.then_inc(tile_done, 1)


def na_prepare(nc, m, a):
    with Phase(nc, "nap") as ph:
        ps = ph.psum()
        sq, rt = ph.sb("sq", [P, 12, T]), ph.sb("rt", [P, 12, T])
        prep = ph.sem("prep")
        z, kc = m.z, m.z[:, N_KC:N_KC + 2].rearrange("p a (b t) -> p (a b) t", b=2)
        qg, kg = m.vec2[:, 0:1], m.vec2[:, 1:2]
        gn = GroupNorm(ph, "gn", [(z[:, i], qg if i < 4 else kg, z[:, i]) for i in range(8)], P, 64, m.ones64,
                       m.eps, ps, sq, rt)
        cn = GroupNorm(ph, "cn", [(kc[:, i], kg, kc[:, i]) for i in range(4)], P, 64, m.ones64, m.eps,
                       ps[:, 4:8], sq[:, 8:12], rt[:, 8:12], width=CTX)
        with nc.Block() as block:
            @block.scalar
            def _(act):
                gn.act(act)
                cn.act(act)

            @block.vector
            def _(dve):
                dve.tensor_scalar(qg, qg, 0.125, None, ALU.mult).then_inc(prep, 1)
                dve.wait_ge(prep, 1)
                gn.dve(dve)
                cn.dve(dve)
                dve.wait_ge(cn.normed, 4)

            @block.tensor
            def _(pe):
                gn.pe(pe)
                cn.pe(pe)


def na_attend(nc, m, a):
    OFFSETS = 14
    heads = 8
    with Phase(nc, "naa") as ph:
        ps = ph.psum()
        bias = ph.sb("rpb", [P, 2, OFFSETS * 64])
        mask = ph.sb("mask", [P, 64])
        mask_loaded, masked = ph.sem("mask_loaded"), ph.sem("masked")
        bias_loaded = [ph.sem(f"bias_loaded{i}") for i in range(2)]
        z, kc = m.z, m.z[:, N_KC:N_KC + 2].rearrange("p a (b t) -> p (a b) t", b=2)

        def scores(pe, h, qt, banks):
            r, j = slice(64 * (h % 2), 64 * (h % 2) + 64), h // 2
            q = z[r, N_Q + j, qt * P:(qt + 1) * P]
            pe.matmul(banks[:, 0], q, z[r, N_K + j], start=True, stop=True)
            return pe.matmul(banks[:, 1, 0:CTX], q, kc[r, j], start=True, stop=True)

        def values(h, kt):
            v = z[:, N_V + kt] if kt < 4 else m.o[:, kt - 4]
            return v[:, 64 * h:64 * h + 64]

        def add_mask(dve, u):
            h = u // TT
            if u % TT == 0:
                dve.wait_ge(mask_loaded, 16)
                dve.wait_ge(bias_loaded[h % 2], 32 * (h // 2 + 1))
                b = bias[:, h % 2].rearrange("p (r c) -> p r c", c=64)
                dve.tensor_tensor(b, b, mask[:].rearrange("p (o c) -> p o c", o=1).broadcast_to([P, OFFSETS, 64]),
                                  ALU.add).then_inc(masked, 1)
                dve.wait_ge(masked, h + 1)

        att = Attention(ph, "bias", heads, ps, m.ident, scores, values,
                        lambda h: m.o[64 * (h % 2):64 * (h % 2) + 64, 4 + h // 2], bias=add_mask)
        att.bias_at = lambda u: bias[:, (u // TT) % 2, (6 - 2 * (u % TT)) * 64:(14 - 2 * (u % TT)) * 64]
        with nc.Block() as block:
            @block.sync
            def _(sp):
                sp.dma_start(mask[:], a["window"]).then_inc(mask_loaded, 16)
                for h in range(heads):
                    if h >= 2:
                        sp.wait_ge(att.biased, TT * (h - 1))
                    for parity in range(2):
                        sp.dma_start(bias[64 * parity:64 * parity + 64, h % 2].rearrange("p (r c) -> p r c", c=64),
                                     a["rpb"][h, :, 1 - parity:15 - parity]).then_inc(bias_loaded[h % 2], 16)

            @block.scalar
            def _(act):
                att.act(act)

            @block.vector
            def _(dve):
                att.dve(dve)

            @block.tensor
            def _(pe):
                att.pe(pe)


def spatial_gate(nc, m, a):
    with Phase(nc, "sgu") as ph:
        ps = ph.psum()
        ws, bs, lng = ph.sb("ws", [P, 8, P]), ph.sb("bs", [P, 4, P]), ph.sb("lng", [P, T])
        stats, mv, std = ph.sb("stats", [P, TT, 6]), ph.sb("mv", [P, TT, 2]), ph.sb("std", [P, TT])
        mixed = ph.sb("mixed", [P, 4, T])
        loaded, st, ag, root, inv, centered, normed, mix, biased, gated = (ph.sem(s) for s in (
            "loaded", "stats_done", "aggr", "root", "inverse", "centered", "normed", "mixed_s", "biased", "gated"))
        v = m.z[:, N_VS:N_VS + TT]
        with nc.Block() as block:
            @block.sync
            def _(sp):
                sp.dma_start(ws[:], a["sgu_w"]).then_inc(loaded, 16)
                sp.dma_start(bs[:], a["sgu_b"]).then_inc(loaded, 16)
                sp.dma_start(lng[:], a["sgu_ln"].broadcast_to([P, T])).then_inc(loaded, 16)
                sp.wait_ge(loaded, 48)

            @block.vector
            def _(dve):
                for t in range(TT):
                    dve.bn_stats(stats[:, t], v[:, t]).then_inc(st, 1)
                for t in range(TT):
                    dve.wait_ge(st, t + 1)
                    dve.bn_aggr(mv[:, t], stats[:, t]).then_inc(ag, 1)
                dve.wait_ge(root, 1)
                dve.reciprocal(std[:], std[:]).then_inc(inv, 1)
                dve.wait_ge(inv, 1)
                dve.wait_ge(loaded, 48)
                for t in range(TT):
                    dve.tensor_scalar(v[:, t], v[:, t], mv[:, t, 0:1], std[:, t:t + 1], ALU.subtract, ALU.mult)\
                       .then_inc(centered, 1)
                for t in range(TT):
                    dve.wait_ge(centered, t + 1)
                    dve.tensor_tensor(v[:, t], v[:, t], lng[:], ALU.mult).then_inc(normed, 1)
                for j in range(4):
                    dve.wait_ge(mix, j + 1)
                    dve.tensor_tensor(mixed[:, j].rearrange("p (n q) -> p n q", n=TT), ps[:, j].rearrange("p (n q) -> p n q", n=TT),
                                      bs[:, j:j + 1].broadcast_to([P, TT, P]), ALU.add).then_inc(biased, 1)
                for j in range(4):
                    dve.wait_ge(biased, j + 1)
                    dve.tensor_tensor(m.o[:, j], mixed[:, j], m.z[:, N_U + j], ALU.mult).then_inc(gated, 1)
                dve.wait_ge(gated, 4)

            @block.scalar
            def _(act):
                act.wait_ge(ag, TT)
                act.activation(std[:], mv[:, :, 1], ACT.Sqrt, bias=m.eps).then_inc(root, 1)

            @block.tensor
            def _(pe):
                pe.wait_ge(normed, TT)
                for j in range(4):
                    for h in (2 * j, 2 * j + 1):
                        r = slice(64 * (h % 2), 64 * (h % 2) + 64)
                        for t in range(TT):
                            mm = pe.matmul(ps[r, j, t * P:(t + 1) * P], v[:, t, 64 * h:64 * h + 64], ws[:, h],
                                           start=True, stop=True)
                    mm.then_inc(mix, 1)


def merge2(nc, m, a):
    with Phase(nc, "out2") as ph:
        ring = Ring(ph, False)
        ps = ph.psum()
        names = ("squares", "totals", "spread", "roots", "inverse", "y_done", "y_hi", "y_lo", "out_done", "out_added")
        s = {n: ph.sem(n) for n in names}
        z = m.z
        norm = Norm(ph, "n", m.x, z[:, 8:16], z[:, 16], z[:, 17], z[:, 0:8], m.hi, m.lo, ps[:, 7], m.ones, m.eps, T)
        w = a["w_out2"].rearrange("(k p) n -> p k n", p=P)
        of = lambda k: m.o[:, (k + 4) % 8]
        with nc.Block() as block:
            @block.sync
            def _(sp):
                ring.open(sp)
                for i in range(4):
                    ring.load(sp, i, i % 2, w[:, :, i * CW:(i + 1) * CW])

            @block.gpsimd
            def _(pool):
                for i in range(4):
                    ring.cut_lo(pool, i, i % 2)

            @block.scalar
            def _(act):
                for k in range(KD):
                    act.activation(z[:, 8 + k], of(k), ACT.Square).then_inc(s["squares"], 1)
                ring.cut_hi(act, 0, 16)
                ring.cut_hi(act, 1, 16)
                for g in range(2):
                    act.wait_ge(s["spread"], g + 1)
                    act.activation(z[:, 18 + g], ps[:, 5 + g], ACT.Sqrt, bias=m.eps, scale=1.0 / NA_W).then_inc(s["roots"], 1)
                for k in range(KD):
                    act.wait_ge(s["y_done"], k + 1)
                    act.activation(m.hi[:, k], z[:, k], ACT.Copy).then_inc(s["y_hi"], 1)
                for i in range(2, 4):
                    act.wait_ge(s["out_done"], 2 * (i - 1))
                    ring.cut_hi(act, i % 2, 32)
                act.wait_ge(s["out_added"], KD)
                norm.act_squares(act)
                norm.act_root(act)

            @block.vector
            def _(dve):
                for g in range(2):
                    dve.wait_ge(s["squares"], 4 * g + 4)
                    dve.tensor_reduce(z[:, 20 + g], z[:, 8 + 4 * g:12 + 4 * g].rearrange("p k t -> p t k"), AX.X, ALU.add)\
                       .then_inc(s["totals"], 1)
                for g in range(2):
                    dve.wait_ge(s["roots"], g + 1)
                    dve.reciprocal(z[:, 18 + g], z[:, 18 + g]).then_inc(s["inverse"], 1)
                    dve.wait_ge(s["inverse"], g + 1)
                    for k in range(4 * g, 4 * g + 4):
                        dve.scalar_tensor_tensor(z[:, k], of(k), m.vec2[:, 2 + k:3 + k], z[:, 18 + g], ALU.mult, ALU.mult)\
                           .then_inc(s["y_done"], 1)
                for k in range(KD):
                    dve.wait_ge(s["y_hi"], k + 1)
                    dve.tensor_tensor(m.lo[:, k], z[:, k], m.hi[:, k].bitcast(F32), ALU.subtract).then_inc(s["y_lo"], 1)
                for t in range(KD):
                    dve.wait_ge(s["out_done"], t + 1)
                    dve.scalar_tensor_tensor(m.x[:, t], ps[:, t % 4], m.mod[:, M_GA + t, 0:1], m.x[:, t], ALU.mult, ALU.add)\
                       .then_inc(s["out_added"], 1)
                norm.dve_total(dve)
                norm.dve_apply(dve, lambda k: m.mod[:, M_SCF + k, 0:1], lambda k: m.mod[:, M_SHF + k, 0:1], cut=False)
                dve.wait_ge(norm.h_done, KD)

            @block.tensor
            def _(pe):
                for g in range(2):
                    pe.wait_ge(s["totals"], g + 1)
                    pe.matmul(ps[:, 5 + g], m.ones, z[:, 20 + g], start=True, stop=True).then_inc(s["spread"], 1)
                pe.wait_ge(s["y_lo"], KD)
                for t in range(KD):
                    i = t // 2
                    if t % 2 == 0:
                        ring.wait_cut(pe, i)
                    hi, lo = cols(ring.hi[:, i % 2], CW), cols(ring.lo[:, i % 2], CW)
                    cp = slice((t % 2) * P, (t % 2 + 1) * P)
                    if t >= 4:
                        pe.wait_ge(s["out_added"], t - 3)
                    product3(pe, ps[:, t % 4], lambda k: hi[:, k, cp], lambda k: lo[:, k, cp],
                             lambda k: m.hi[:, k], lambda k: m.lo[:, k], range(KD)).then_inc(s["out_done"], 1)
                norm.pe_spread(pe)


class RouteMemory:

    def __init__(self, nc, stack):
        def sb(name, shape, dt=F32):
            return stack.enter_context(nc.sbuf_tensor(f"moe_{name}", shape, dt))

        self.weight = sb("weight1", [P, TT, 1]), sb("weight2", [P, TT, 1])
        self.row = sb("row1", [P, TT], I32), sb("row2", [P, TT], I32)
        self.over = sb("over", [P, OVER], I32)
        self.token = sb("token", [P, SLOTS], I32)
        self.h = nc.dram_tensor("moe_h", (T, D), F32, kind="Internal").ap()
        self.places = nc.dram_tensor("moe_places", (SLOTS * P, 1), F32, kind="Internal").ap()
        self.y = nc.dram_tensor("moe_y", (SLOTS * P, D), F32, kind="Internal").ap()


def route(nc, m, a, r):
    NG, NX = 4, 4
    with Phase(nc, "route") as ph:
        ps = ph.psum()
        wr, rb = ph.sb("wr", [P, KD, 20]), ph.sb("rb", [P, 20])
        table, ids = ph.sb("table", [P, P + NE + OVER * NE]), ph.sb("ids", [P, TT])
        later, first_row = table[:, 0:P], table[:, P:P + NE]
        over_index = table[:, P + NE:].rearrange("p (o e) -> p o e", o=OVER)
        lg = ph.sb("logits", [P, TT, 20])
        four = {n: ph.sb(n, [P, TT, 4]) for n in ("ge", "geq", "ghot", "le", "le2", "eq1", "eq2", "hot1", "hot2")}
        one = {n: ph.sb(n, [P, TT, 1]) for n in ("gm", "gs", "ptop", "m1", "m2", "d", "den", "rem")}
        by = ph.sb("by", [P, TT, NG, NX])
        hot = ph.sb("expert1", [P, TT, NE]), ph.sb("expert2", [P, TT, NE])
        both, place, low = ph.sb("both", [P, TT, NE]), ph.sb("place", [P, TT, NE]), ph.sb("low", [P, TT, NE])
        count, more, upto, tmp = ph.sb("count", [P, NE]), ph.sb("more", [P, NE]), ph.sb("upto", [P, 2, NE]), ph.sb("tmp", [P, NE])
        cmp, over = ph.sb("cmp", [P, OVER, NE]), ph.sb("over_f", [P, OVER])
        rows = ph.sb("rows1_f", [P, TT]), ph.sb("rows2_f", [P, TT])
        zero, listed_at = ph.sb("zero", [P, SLOTS]), ph.sb("listed_at", [SLOTS, P])
        h_tok = m.o[:].rearrange("p k t -> p (k t)").rearrange("p (t f) -> p t f", t=TT)
        (loaded, logit, step, to_exp, exp_done, masks, ranks, rows_done, zeroed, cleared, turned, turned_out,
         h_stored, placed, listed, list_turned) = (ph.sem(s) for s in (
            "loaded", "logit", "step", "to_exp", "exp_done", "masks", "ranks", "rows_done", "zeroed", "cleared", "turned",
            "turned_out", "h_stored", "placed", "listed", "list_turned"))
        with nc.Block() as block:
            @block.sync
            def _(sp):
                sp.dma_start(wr[:], a["w_route"].rearrange("(k p) n -> p k n", p=P)).then_inc(loaded, 16)
                sp.dma_start(rb[:], a["b_route"].broadcast_to([P, 20])).then_inc(loaded, 16)
                sp.dma_start(table[:], a["moe_table"]).then_inc(loaded, 16)
                sp.dma_start(ids[:], a["token_ids"]).then_inc(loaded, 16)
                sp.wait_ge(zeroed, 1)
                sp.dma_start(r.places.rearrange("(p s) o -> p (s o)", p=P), zero[:]).then_inc(cleared, 16)
                sp.wait_ge(turned_out, 2 * TT)
                sp.dma_start(r.h.rearrange("(t p) f -> p t f", p=P), h_tok).then_inc(h_stored, 16)
                sp.wait_ge(placed, 32 * TT)
                sp.dma_start(listed_at[:], r.places.rearrange("(s p) o -> s (p o)", p=P)).then_inc(listed, 16)
                sp.wait_ge(h_stored, 16)
                sp.wait_ge(listed, 16)
                sp.wait_ge(loaded, 64)

            @block.gpsimd
            def _(pool):
                pool.memset(zero[:], 0.0).then_inc(zeroed, 1)
                pool.wait_ge(loaded, 64)
                pool.wait_ge(cleared, 16)
                pool.wait_ge(rows_done, 2)
                for row in r.row:
                    for t in range(TT):
                        pool.indirect_dma_start(r.places, bass.IndirectOffsetOnAxis(row[:, t:t + 1], 0),
                                                ids[:, t:t + 1], None).then_inc(placed, 16)
                pool.wait_ge(placed, 32 * TT)

            @block.tensor
            def _(pe):
                pe.wait_ge(loaded, 64)
                for t in range(TT):
                    for k in range(KD):
                        mm = pe.matmul(ps[:, 0, t * 32:t * 32 + 20], m.z[:, k, t * P:(t + 1) * P], wr[:, k],
                                       start=(k == 0), stop=(k == KD - 1))
                mm.then_inc(logit, 1)
                for i in range(2 * TT):
                    t, half = i // 2, i % 2
                    if i >= 4:
                        pe.wait_ge(turned_out, i - 3)
                    for k in range(4):
                        mm = pe.transpose(ps[:, 2 + i % 4, k * P:(k + 1) * P], m.z[:, 4 * half + k, t * P:(t + 1) * P], m.ident)
                    mm.then_inc(turned, 1)
                pe.wait_ge(masks, 1)
                for t in range(TT):
                    for u in range(t):
                        pe.matmul(ps[:, 1, t * NE:(t + 1) * NE], m.ones, both[:, u], start=(u == 0), stop=False)
                    pe.matmul(ps[:, 1, t * NE:(t + 1) * NE], later, both[:, t], start=(t == 0), stop=True)
                for u in range(TT):
                    mm = pe.matmul(ps[:, 1, TT * NE:(TT + 1) * NE], m.ones, both[:, u], start=(u == 0), stop=(u == TT - 1))
                mm.then_inc(ranks, 1)
                pe.wait_ge(listed, 16)
                pe.transpose(ps[:, 6, 0:SLOTS], listed_at[:], m.ident[0:SLOTS, 0:SLOTS]).then_inc(list_turned, 1)

            @block.scalar
            def _(act):
                act.wait_ge(to_exp, 1)
                act.activation(four["ge"][:], four["ge"][:], ACT.Exp).then_inc(exp_done, 1)
                act.wait_ge(to_exp, 2)
                act.activation(one["d"][:], one["d"][:], ACT.Exp).then_inc(exp_done, 1)
                for i in range(2 * TT):
                    act.wait_ge(turned, i + 1)
                    act.activation(h_tok[:, i // 2, (i % 2) * 512:(i % 2 + 1) * 512], ps[:, 2 + i % 4], ACT.Copy)\
                       .then_inc(turned_out, 1)

            @block.vector
            def _(dve):
                link = linker(dve, step)

                def wide(x):
                    return x[:].broadcast_to([P, TT, 4])

                def first_hot(dst, eq):
                    rem = one["rem"]
                    link(dve.tensor_copy(dst[:, :, 0:1], eq[:, :, 0:1]))
                    link(dve.tensor_scalar(rem[:], eq[:, :, 0:1], -1.0, 1.0, ALU.mult, ALU.add))
                    for i in range(1, 4):
                        link(dve.tensor_tensor(dst[:, :, i:i + 1], eq[:, :, i:i + 1], rem[:], ALU.mult))
                        if i < 3:
                            link(dve.tensor_tensor(rem[:], rem[:], dst[:, :, i:i + 1], ALU.subtract))

                dve.wait_ge(logit, 1)
                dve.wait_ge(loaded, 64)
                link(dve.tensor_tensor(lg[:], ps[:, 0, 0:TT * 32].rearrange("p (t n) -> p t n", n=32)[:, :, 0:20],
                                       rb[:].rearrange("p (o n) -> p o n", o=1).broadcast_to([P, TT, 20]), ALU.add))
                link(dve.tensor_reduce(one["gm"][:], lg[:, :, 0:4], AX.X, ALU.max))
                dve.tensor_tensor(four["ge"][:], lg[:, :, 0:4], wide(one["gm"]), ALU.subtract).then_inc(to_exp, 1)
                link(dve.tensor_tensor(four["geq"][:], lg[:, :, 0:4], wide(one["gm"]), ALU.is_equal))
                first_hot(four["ghot"], four["geq"])
                hot_g = four["ghot"][:].rearrange("p t (g o) -> p t g o", o=1).broadcast_to([P, TT, NG, NX])
                for t in range(TT):
                    ins = dve.tensor_tensor(by[:, t], lg[:, t, 4:20].rearrange("p (g x) -> p g x", g=NG), hot_g[:, t], ALU.mult)
                link(ins)
                for t in range(TT):
                    ins = dve.tensor_reduce(four["le"][:, t], by[:, t].rearrange("p g x -> p x g"), AX.X, ALU.add)
                link(ins)
                link(dve.tensor_reduce(one["m1"][:], four["le"][:], AX.X, ALU.max))
                link(dve.tensor_tensor(four["eq1"][:], four["le"][:], wide(one["m1"]), ALU.is_equal))
                first_hot(four["hot1"], four["eq1"])
                link(dve.scalar_tensor_tensor(four["le2"][:], four["hot1"][:], NEG, four["le"][:], ALU.mult, ALU.add))
                link(dve.tensor_reduce(one["m2"][:], four["le2"][:], AX.X, ALU.max))
                link(dve.tensor_tensor(four["eq2"][:], four["le2"][:], wide(one["m2"]), ALU.is_equal))
                dve.tensor_tensor(one["d"][:], one["m2"][:], one["m1"][:], ALU.subtract).then_inc(to_exp, 1)
                first_hot(four["hot2"], four["eq2"])
                for n, name in ((0, "hot1"), (1, "hot2")):
                    within = four[name][:].rearrange("p t (o x) -> p t o x", o=1).broadcast_to([P, TT, NG, NX])
                    for t in range(TT):
                        ins = dve.tensor_tensor(hot[n][:, t].rearrange("p (g x) -> p g x", g=NG), within[:, t], hot_g[:, t], ALU.mult)
                    link(ins)
                dve.tensor_tensor(both[:], hot[0][:], hot[1][:], ALU.add).then_inc(masks, 1)
                dve.wait_ge(exp_done, 2)
                link(dve.tensor_reduce(one["gs"][:], four["ge"][:], AX.X, ALU.add))
                link(dve.reciprocal(one["ptop"][:], one["gs"][:]))
                link(dve.tensor_scalar(one["den"][:], one["d"][:], 1.0, None, ALU.add))
                link(dve.reciprocal(one["den"][:], one["den"][:]))
                link(dve.tensor_tensor(r.weight[0][:], one["den"][:], one["ptop"][:], ALU.mult))
                link(dve.tensor_tensor(r.weight[1][:], r.weight[0][:], one["d"][:], ALU.mult))
                dve.wait_ge(ranks, 1)
                link(dve.tensor_copy(count[:], ps[:, 1, TT * NE:(TT + 1) * NE]))
                link(dve.tensor_scalar(more[:], count[:], float(P), None, ALU.is_gt))
                for n in range(2, TT):
                    link(dve.tensor_scalar(tmp[:], count[:], float(n * P), None, ALU.is_gt))
                    link(dve.tensor_tensor(more[:], more[:], tmp[:], ALU.add))
                link(dve.tensor_copy(upto[:, 0], more[:]))
                for n, shift in enumerate((1, 2, 4, 8)):
                    src, dst = upto[:, n % 2], upto[:, (n + 1) % 2]
                    link(dve.tensor_copy(dst[:, 0:shift], src[:, 0:shift]))
                    link(dve.tensor_tensor(dst[:, shift:NE], src[:, shift:NE], src[:, 0:NE - shift], ALU.add))
                sums = upto[:, 0].rearrange("p (o e) -> p o e", o=1).broadcast_to([P, OVER, NE])
                link(dve.tensor_tensor(cmp[:], sums, over_index, ALU.is_le))
                link(dve.tensor_reduce(over[:], cmp[:], AX.X, ALU.add))
                link(dve.tensor_scalar(over[:], over[:], float(NE - 1), None, ALU.min))
                link(dve.tensor_copy(r.over[:], over[:]))
                link(dve.tensor_tensor(tmp[:], upto[:, 0], more[:], ALU.subtract))
                link(dve.tensor_scalar(tmp[:], tmp[:], float(NE - 1), float(P), ALU.add, ALU.mult))
                link(dve.tensor_tensor(more[:], first_row, tmp[:], ALU.subtract))
                link(dve.tensor_copy(place[:], ps[:, 1, 0:TT * NE].rearrange("p (t e) -> p t e", t=TT)))
                link(dve.tensor_scalar(low[:], place[:], float(P), None, ALU.is_lt))
                for t in range(TT):
                    link(dve.tensor_tensor(low[:, t], low[:, t], more[:], ALU.mult))
                    link(dve.tensor_tensor(low[:, t], low[:, t], tmp[:], ALU.add))
                link(dve.tensor_tensor(place[:], place[:], low[:], ALU.add))
                for n in range(2):
                    link(dve.tensor_tensor(low[:], hot[n][:], place[:], ALU.mult))
                    link(dve.tensor_reduce(rows[n][:], low[:], AX.X, ALU.add))
                    dve.tensor_copy(r.row[n][:], rows[n][:]).then_inc(rows_done, 1)
                dve.wait_ge(list_turned, 1)
                link(dve.tensor_copy(r.token[:], ps[:, 6, 0:SLOTS]))


def experts(nc, m, a, r):
    HALF = KD // 2
    with Phase(nc, "moe") as ph:
        ps = ph.psum()
        weights = [ph.sb(f"weights{b}", [P, 6, CHUNK]) for b in range(2)]
        weights = [[w[:, i].rearrange("p (k t) -> p k t", k=HALF) for i in range(6)] for w in weights]
        flat = m.z[:].rearrange("p k t -> p (k t)")

        def part(tile, n, k):
            return flat[:, tile * T:tile * T + n * k].rearrange("p (k n) -> p k n", k=k)

        rows = [part(8, D, 1), part(10, D, 1)]
        x_t = [part(12, P, KD), part(14, P, KD)]
        y = [part(16, D, 1), part(18, D, 1)]
        silu, hid, hid_t = m.z[:, 0:2], m.z[:, 2:4], [part(4, P, DE // P), part(5, P, DE // P)]
        ready = [[ph.sem(f"weights{b}{i}") for i in range(6)] for b in range(2)]
        (x_turned, x_out, gate_done, up_done, silu_done, hid_done, hid_turned, hid_out,
         y_done, y_out) = (ph.sem(s) for s in ("x_turned", "x_out", "gate_done", "up_done", "silu_done",
                                               "hid_done", "hid_turned", "hid_out", "y_done", "y_out"))
        gathered = [ph.sem(f"gathered{b}") for b in range(2)]
        y_stored = [ph.sem(f"y_stored{b}") for b in range(2)]
        y_rows = r.y.rearrange("(s p) f -> s p f", p=P)
        w1 = a["w1"].rearrange("e (h k p) n -> e h p k n", p=P, k=HALF)
        w3 = a["w3"].rearrange("e (h k p) n -> e h p k n", p=P, k=HALF)
        w2 = a["w2"].rearrange("e (h k p) n -> e h p k n", p=P, h=2)
        TURNS = SLOTS // 2
        open_two = (gate_done, up_done, y_done, x_out, hid_turned, hid_done, y_out)
        with nc.Block() as block:
            @block.sync
            def _(sp):
                for s in open_two:
                    sp.sem_inc(s, 2)
                sp.sem_inc(hid_out, 1)
                for s in y_stored:
                    sp.sem_inc(s, 16)

                def load(slot, b, e):
                    for n, (w, done) in enumerate(((w1, gate_done), (w3, up_done), (w2, y_done))):
                        sp.wait_ge(done, slot + 1)
                        for half in range(2):
                            dst = weights[b][2 * n + half]
                            if n == 2:
                                dst = dst.rearrange("p k t -> p (k t)").rearrange("p (k n) -> p k n", k=2)
                            sp.dma_start(dst, w[e, half]).then_inc(ready[b][2 * n + half], 16)

                with sp.Fori(0, NE // 2) as turn:
                    for b in range(2):
                        load(2 * turn + b, b, 2 * turn + b)
                for i in range(OVER):
                    load(NE + i, i % 2, sp.value_load(r.over[0:1, i:i + 1], min_val=0, max_val=NE - 1))

            @block.gpsimd
            def _(pool):
                for s in range(SLOTS):
                    if s >= 2:
                        pool.wait_ge(x_turned, s - 1)
                    pool.indirect_dma_start(rows[s % 2][:, 0], None, r.h,
                                            bass.IndirectOffsetOnAxis(r.token[:, s:s + 1], 0)).then_inc(gathered[s % 2], 16)

            @block.tensor
            def _(pe):
                def turn_x(s, turn, b):
                    pe.wait_ge(gathered[b], 16 * turn + 16)
                    pe.wait_ge(x_out, 2 * s + 2)
                    for k in range(KD):
                        mm = pe.transpose(ps[:, k // 4, (k % 4) * P:(k % 4 + 1) * P], rows[b][:, 0, k * P:(k + 1) * P], m.ident)
                    mm.then_inc(x_turned, 1)

                def turn_hidden(s, b):
                    pe.wait_ge(hid_done, s + 3)
                    pe.wait_ge(hid_out, s + 1)
                    for k in range(DE // P):
                        mm = pe.transpose(ps[:, 4, k * P:(k + 1) * P], hid[:, b, k * P:(k + 1) * P], m.ident)
                    mm.then_inc(hid_turned, 1)

                def gate_up(s, turn, b):
                    pe.wait_ge(x_out, 2 * s + 4)
                    for n, done in ((0, gate_done), (1, up_done)):
                        for k in range(KD):
                            if k % HALF == 0:
                                pe.wait_ge(ready[b][2 * n + k // HALF], 16 * turn + 16)
                            mm = pe.matmul(ps[:, 2 + n], x_t[b][:, k], weights[b][2 * n + k // HALF][:, k % HALF],
                                           start=(k == 0), stop=(k == KD - 1))
                        mm.then_inc(done, 1)

                def down(s, turn, b):
                    pe.wait_ge(hid_out, s + 2)
                    pe.wait_ge(y_out, 2 * s + 2)
                    for k in range(DE // P):
                        if k % 2 == 0:
                            pe.wait_ge(ready[b][4 + k // 2], 16 * turn + 16)
                        w = weights[b][4 + k // 2].rearrange("p k t -> p (k t)")
                        for half in range(2):
                            at = (k % 2) * D + half * T
                            mm = pe.matmul(ps[:, 5 + half], hid_t[b][:, k], w[:, at:at + T],
                                           start=(k == 0), stop=(k == DE // P - 1))
                    mm.then_inc(y_done, 1)

                def two(turn, last=False):
                    gate_up(2 * turn + 1, turn, 1)
                    turn_x(2 * turn + 2, turn + 1, 0)
                    down(2 * turn, turn, 0)
                    turn_hidden(2 * turn + 1, 1)
                    gate_up(2 * turn + 2, turn + 1, 0)
                    if not last:
                        turn_x(2 * turn + 3, turn + 1, 1)
                    down(2 * turn + 1, turn, 1)
                    turn_hidden(2 * turn + 2, 0)

                turn_x(0, 0, 0)
                gate_up(0, 0, 0)
                turn_x(1, 0, 1)
                turn_hidden(0, 0)
                with pe.Fori(0, TURNS - 1) as turn:
                    two(turn)
                two(TURNS - 1, last=True)
                down(SLOTS - 1, TURNS, 0)

            @block.scalar
            def _(act):
                def copy_x(s, b):
                    act.wait_ge(x_turned, s + 1)
                    act.wait_ge(up_done, s + 1)
                    for h in range(2):
                        act.activation(x_t[b][:, 4 * h:4 * h + 4], ps[:, h].rearrange("p (k n) -> p k n", k=4), ACT.Copy)\
                           .then_inc(x_out, 1)

                def store_y(s, turn, b):
                    act.wait_ge(y_out, 2 * s + 4)
                    act.dma_start(y_rows[s], y[b][:, 0]).then_inc(y_stored[b], 16)

                def slot(s, b, more=True):
                    act.wait_ge(gate_done, s + 3)
                    act.wait_ge(hid_done, s + 1)
                    act.activation(silu[:, b], ps[:, 2], ACT.Silu).then_inc(silu_done, 1)
                    if more:
                        copy_x(s + 1, 1 - b)
                    act.wait_ge(hid_turned, s + 3)
                    act.wait_ge(y_done, s + 1)
                    act.activation(hid_t[b], ps[:, 4].rearrange("p (k n) -> p k n", k=4), ACT.Copy).then_inc(hid_out, 1)

                copy_x(0, 0)
                slot(0, 0)
                with act.Fori(0, TURNS - 1) as turn:
                    slot(2 * turn + 1, 1)
                    store_y(2 * turn, turn, 0)
                    slot(2 * turn + 2, 0)
                    store_y(2 * turn + 1, turn, 1)
                slot(SLOTS - 2, 1)
                store_y(SLOTS - 3, TURNS - 1, 0)
                slot(SLOTS - 1, 0, more=False)
                store_y(SLOTS - 2, TURNS - 1, 1)
                store_y(SLOTS - 1, TURNS, 0)
                for b in range(2):
                    act.wait_ge(y_stored[b], 16 + 16 * (TURNS + 1 - b))

            @block.vector
            def _(dve):
                def hidden(s, b):
                    dve.wait_ge(silu_done, s + 1)
                    dve.wait_ge(up_done, s + 3)
                    dve.wait_ge(hid_turned, s + 1)
                    dve.tensor_tensor(hid[:, b], silu[:, b], ps[:, 3], ALU.mult).then_inc(hid_done, 1)

                def copy_y(s, turn, b):
                    dve.wait_ge(y_done, s + 3)
                    dve.wait_ge(y_stored[b], 16 * turn + 16)
                    for half in range(2):
                        dve.tensor_copy(y[b][:, 0, half * T:(half + 1) * T], ps[:, 5 + half]).then_inc(y_out, 1)

                hidden(0, 0)
                with dve.Fori(0, TURNS) as turn:
                    hidden(2 * turn + 1, 1)
                    copy_y(2 * turn, turn, 0)
                    hidden(2 * turn + 2, 0)
                    copy_y(2 * turn + 1, turn, 1)
                copy_y(SLOTS - 1, TURNS, 0)


def combine(nc, m, r):
    with Phase(nc, "combine") as ph:
        ps = ph.psum()
        flat = m.z[:].rearrange("p k t -> p (k t)")
        got = [[flat[:, (2 * t + n) * D:(2 * t + n + 1) * D] for n in range(2)] for t in range(TT)]
        ready = [ph.sem(f"ready{t}") for t in range(TT)]
        scaled, summed, turned, added = (ph.sem(s) for s in ("scaled", "summed", "turned", "added"))
        with nc.Block() as block:
            @block.gpsimd
            def _(pool):
                for t in range(TT):
                    for n in range(2):
                        pool.indirect_dma_start(got[t][n], None, r.y, bass.IndirectOffsetOnAxis(r.row[n][:, t:t + 1], 0))\
                            .then_inc(ready[t], 16)

            @block.vector
            def _(dve):
                for t in range(TT):
                    dve.wait_ge(ready[t], 32)
                    dve.tensor_scalar(got[t][0], got[t][0], r.weight[0][:, t], None, ALU.mult).then_inc(scaled, 1)
                    dve.wait_ge(scaled, t + 1)
                    dve.scalar_tensor_tensor(got[t][1], got[t][1], r.weight[1][:, t], got[t][0], ALU.mult, ALU.add)\
                       .then_inc(summed, 1)
                dve.wait_ge(turned, 1)
                for c in range(KD):
                    dve.scalar_tensor_tensor(m.x[:, c], ps[:, c], m.mod[:, M_GF + c, 0:1], m.x[:, c], ALU.mult, ALU.add)\
                       .then_inc(added, 1)
                dve.wait_ge(added, KD)

            @block.tensor
            def _(pe):
                for t in range(TT):
                    pe.wait_ge(summed, t + 1)
                    for c in range(KD):
                        mm = pe.transpose(ps[:, c, t * P:(t + 1) * P], got[t][1][:, c * P:(c + 1) * P], m.ident)
                mm.then_inc(turned, 1)


def store(nc, m, out):
    with Phase(nc, "store") as ph:
        stored = ph.sem("stored")
        with nc.Block() as block:
            @block.sync
            def _(sp):
                sp.dma_start(out.rearrange("(k p) t -> p k t", p=P), m.x[:]).then_inc(stored, 16)
                sp.wait_ge(stored, 16)


def second_block(nc, m, a):
    modulation(nc, m, a)
    project2(nc, m, a)
    na_prepare(nc, m, a)
    na_attend(nc, m, a)
    spatial_gate(nc, m, a)
    merge2(nc, m, a)
    m.parts.close()
    with ExitStack() as stack:
        r = RouteMemory(nc, stack)
        route(nc, m, a, r)
        experts(nc, m, a, r)
        combine(nc, m, r)


class Memory:

    def __init__(self, nc, stack):
        def sb(name, shape, dt=F32):
            return stack.enter_context(nc.sbuf_tensor(name, shape, dt))

        self.x = sb("x", [P, KD, T])
        self.o = sb("o", [P, 2 * NB, T])
        self.z = sb("z", [P, ZT, T])
        self.mats = sb("mats", [P, 5 * P + KRW])
        self.rope = sb("rope", [P, 4, T])
        self.small = sb("small", [P, 6])
        self.gains, self.g = sb("gains", [P, 2, G_N]), sb("g", [P, G_N])
        self.lam, self.lamv = sb("lam", [P, 256]), sb("lamv", [P, 128])
        self.lb, self.lbl, self.laminit = sb("lb", [P, 2, 2, 2]), sb("lbl", [P, 4]), sb("laminit", [P, 2])
        self.ones, self.ident, self.ones32, self.ones64, self.rot32 = (
            self.mats[:, i * P:(i + 1) * P] for i in range(5))
        self.rot96 = self.mats[0:KRW, 5 * P:5 * P + KRW]
        self.eps = self.small[:, 4:5]
        self.mod = sb("mod", [P, MODS, 2])
        self.vec2 = sb("vec2", [P, 10])
        self.parts = stack.enter_context(ExitStack())
        self.hi, self.lo = (self.parts.enter_context(nc.sbuf_tensor(name, [P, KD, T], F32R)) for name in ("h_hi", "h_lo"))


class MixerMemory:
    def __init__(self, nc, stack, name, mla):
        def sb(n, shape):
            return stack.enter_context(nc.sbuf_tensor(f"{name}_{n}", shape, F32))

        self.gqt = sb("gq", [P, 2])
        self.gq = self.gqt[0:96, 0:1] if mla else self.gqt[:, 0:1]
        self.gsub = self.gqt[:, 1:2]
        if mla:
            self.raw, self.qk, self.v = sb("raw", [96, 8, T]), sb("qk", [96, 8, T]), sb("v", [P, TT, BW])
        else:
            self.qk = sb("qk", [P, 4, T])
            self.lam2, self.lamt = sb("lam2", [P, 2]), sb("lamt", [P, 2])
        self.od = sb("od", [P, 2, T])


def first_block(nc, m, a, layers=2):
    with nc.Fori(0, layers) as l:
        project(nc, m, a, l)
        with ExitStack() as stack:
            mem = MixerMemory(nc, stack, "mla", True)
            mla_prepare(nc, m, a, l, mem)
            mla_attend(nc, m, mem)
        with ExitStack() as stack:
            mem = MixerMemory(nc, stack, "diff", False)
            diff_prepare(nc, m, mem)
            diff_attend(nc, m, mem)
            head_norm(nc, m, "difn", mem.od, mem.gsub, m.o[:, 4:6])
            fnet(nc, m, a)
        with ExitStack() as stack:
            od = stack.enter_context(nc.sbuf_tensor("hgrn_od", [P, 2, T], F32))
            hgrn(nc, m, a, od)
            head_norm(nc, m, "hgrnn", od, m.g[:, G_ON:G_ON + 1], m.o[:, 6:8], m.z[:, Z_HG:Z_HG + 2])
        merge_and_ffn(nc, m, a, l)

def feature_columns(np, v):
    v = np.asarray(v)
    return np.moveaxis(v.reshape(v.shape[:-1] + (v.shape[-1] // 128, 128)), -1, 0)


def repeated(np, v):
    v = np.asarray(v)
    return np.moveaxis(np.stack([np.resize(r, 128) for r in v]), -1, 0)[:, :, None]


def constants(np):
    eye = np.eye(128)
    blocks = lambda n: np.kron(np.eye(128 // n), np.ones((n, n)))

    def rotation(size, starts, half):
        r = np.zeros((size, size))
        for s in starts:
            for i in range(half):
                r[s + half + i, s + i] = -1.0
                r[s + i, s + half + i] = 1.0
        return r

    rot96 = np.zeros((128, 96))
    rot96[:96] = rotation(96, [64], 16)
    mats = np.concatenate([np.ones((128, 128)), eye, blocks(32), blocks(64), rotation(128, [0, 32, 64, 96], 16), rot96], 1)
    inv = (1.0 / (np.float32(10000.0) ** (np.arange(0, 32, 2, dtype=np.float32) / np.float32(32)))).astype(np.float32)
    ang = (np.arange(512, dtype=np.float32)[None, :] * inv[:, None]).astype(np.float32)
    cos, sin = np.cos(ang.astype(np.float64)), np.sin(ang.astype(np.float64))
    rope = np.zeros((128, 4, 512))
    rope[:64, 0] = 1.0
    rope[64:96, 0], rope[64:96, 1] = np.tile(cos, (2, 1)), np.tile(sin, (2, 1))
    rope[:, 2], rope[:, 3] = np.tile(cos, (8, 1)), np.tile(sin, (8, 1))
    small = np.zeros((128, 6))
    for l in range(2):
        init = 0.8 - 0.6 * np.exp(-0.3 * l)
        small[:, 2 * l], small[:, 2 * l + 1] = init, 1.0 - init
    small[:, 4] = 1e-6
    t = np.arange(512)
    phase = 2 * np.pi * (np.outer(t, t) % 512) / 512
    dft = np.stack([np.cos(phase), np.sin(phase)]) / np.sqrt(512)
    dft = dft.reshape(2, 4, 128, 512).transpose(2, 0, 1, 3)
    c = np.arange(64)
    p64 = 2 * np.pi * (np.outer(c, c) % 64) / 64
    dft64 = np.concatenate([np.kron(np.eye(2), np.cos(p64)), np.kron(np.eye(2), -np.sin(p64))], 1) / 8
    s, q = np.arange(128)[:, None], np.arange(128)[None, :]
    masks = [((s // (2 * b) == q // (2 * b)) & (s // b != q // b)) for b in (64, 32, 16, 8, 4, 2, 1)] + [s == q]
    masks = np.stack(masks, 1)
    reset = np.tile((np.arange(512) % 128 != 0)[None], (128, 1))
    c, kc = np.arange(128)[:, None] % 64, np.arange(64)[None, :]
    start = np.clip(c - 8, 0, 48)
    window = np.where((kc >= start) & (kc < start + 16), 0.0, -1.0e30)
    later = np.triu(np.ones((P, P)), 1)
    over = np.repeat(np.arange(OVER), NE)
    moe_table = np.concatenate([later, np.tile(np.concatenate([P * np.arange(NE), over]), (P, 1))], 1)
    token_ids = np.arange(T, dtype=np.float32).reshape(TT, P).T
    out = {k: np.ascontiguousarray(v, dtype=np.float32) for k, v in dict(
        window=window, mats=mats, rope=rope, small=small, dft=dft, dft64=dft64, masks=masks, reset=reset,
        moe_table=moe_table).items()}
    return {**out, "token_ids": np.ascontiguousarray(token_ids)}


def lay_out_first(np, i):
    fc = lambda n: feature_columns(np, i[n])
    rep = lambda n: repeated(np, i[n])
    gains = np.concatenate([fc("ln_mix"), fc("mla_g_qa"), fc("mla_g_kva"), rep("mla_g_qn"), rep("mla_g_kn"),
                            rep("diff_g_qn"), rep("diff_g_kn"), rep("diff_g_sub"), rep("hgrn_g_on"), fc("ln_ffn")], -1)
    lb = np.asarray(i["hgrn_lb_logits"]).reshape(2, 2, 2, 128)
    out = dict(xT=np.asarray(i["x"])[0].T, gains=gains,
               lam=np.stack([np.asarray(i[n]) for n in ("diff_lq1", "diff_lk1", "diff_lq2", "diff_lk2")], 1),
               lb_logits=lb.transpose(3, 0, 1, 2),
               w_in=i["w_in"], w_uq=i["mla_w_uq"], w_ukv=i["mla_w_ukv"], w_branch=i["w_branch"], w_out=i["w_out"],
               w_gate_up=i["w_gate_up"], w_down=i["w_down"])
    return {k: np.ascontiguousarray(v) for k, v in out.items()}


def lay_out_second(np, i):
    fc = lambda v: feature_columns(np, v)
    g = {n: np.asarray(i[n + "_2"])[0] for n in (
        "w_ada", "b_ada", "w_in", "q_gain", "k_gain", "rpb", "sgu_ln", "sgu_w", "sgu_b", "out_gain", "w_out", "rg_w",
        "rg_b", "re_w", "re_b", "w1", "w3", "w2")}
    cond = np.stack([fc(np.asarray(i["c_2"])[0]), fc(np.asarray(i["c_ctx_2"]))], -1)
    col = np.arange(64)
    rpb = g["rpb"][:, :, np.clip(col[None, :] - col[:, None] + 15, 0, 30)].transpose(0, 2, 1, 3)
    out = dict(cond=cond, b_ada=fc(g["b_ada"]), w_ada=g["w_ada"], ctxT=np.asarray(i["ctx_2"])[0].T, w_in2=g["w_in"],
               vec2=np.concatenate([np.resize(g["q_gain"], 128)[:, None], np.resize(g["k_gain"], 128)[:, None],
                                    fc(g["out_gain"])], 1),
               rpb=rpb, sgu_ln=g["sgu_ln"][None], sgu_w=g["sgu_w"].transpose(2, 0, 1),
               sgu_b=np.repeat(g["sgu_b"].reshape(4, 2, 128), 64, axis=1).transpose(1, 0, 2), w_out2=g["w_out"],
               w_route=np.concatenate([g["rg_w"], g["re_w"].transpose(1, 0, 2).reshape(1024, 16)], 1),
               b_route=np.concatenate([g["rg_b"], g["re_b"].reshape(-1)])[None],
               w1=g["w1"], w3=g["w3"], w2=g["w2"])
    return {k: np.ascontiguousarray(v) for k, v in out.items()}


def program(nc, a, out):
    with ExitStack() as stack:
        m = Memory(nc, stack)
        load_constants(nc, m, a)
        first_block(nc, m, a)
        second_block(nc, m, a)
        store(nc, m, out)


def kernel(**inputs):
    import numpy as np
    import concourse.bacc as bacc
    from concourse.bass_utils import run_bass_kernel_spmd

    nc = bacc.Bacc("TRN2", target_bir_lowering=False, num_devices=1)
    arrays, a = {}, {}
    for name, x in {**lay_out_first(np, inputs), **lay_out_second(np, inputs), **constants(np)}.items():
        arrays[f"in_{name}"] = x
        a[name] = nc.dram_tensor(f"in_{name}", x.shape, mybir.dt.from_np(x.dtype), kind="ExternalInput").ap()
    out = nc.dram_tensor("out_xT", (D, T), F32, kind="ExternalOutput").ap()
    program(nc, a, out)
    r = run_bass_kernel_spmd(nc, [arrays], core_ids=[0])
    return np.ascontiguousarray(r.results[0]["out_xT"].T)[None]
```
